# Optimizing a Trainium2 kernel written in Bass

```python
import jax
import jax.numpy as jnp
from jax import lax
import numpy as np

D_MODEL = 1024
BATCH = 1
SEQ = 512
DEPTH = 2

N_A_LAYERS = DEPTH // 2
N_B_LAYERS = DEPTH - N_A_LAYERS
EPS = 1e-6

N_HEADS_A = 4
DV_A = D_MODEL // N_HEADS_A
DQK_A = DV_A // 2
CHUNK_A = 64
GATE_CAP = 15.0
QK_A = N_HEADS_A * DQK_A
A_SPLITS = (QK_A, 2 * QK_A, 2 * QK_A + D_MODEL, 2 * QK_A + 2 * D_MODEL)
A_IN = 2 * QK_A + 2 * D_MODEL + 2 * N_HEADS_A

DH_B = 64
N_HEADS_B = D_MODEL // DH_B
QBLOCK = 128
B_IN = 2 * D_MODEL
KV_OUT = 2 * D_MODEL + N_HEADS_B

N_GROUPS = 4
EXP_PER_GROUP = 4
N_EXPERTS = N_GROUPS * EXP_PER_GROUP
TOP_K = 2
D_EXPERT = D_MODEL // 2

kernel_name = 'yoco_mlstm_fox_hier_moe'

def rmsnorm(x, g):
    xf = x.astype(jnp.float32)
    y = xf * lax.rsqrt(jnp.mean(xf * xf, axis=-1, keepdims=True) + EPS)
    return y.astype(x.dtype) * g

def softcap(z, cap):
    return cap * jnp.tanh(z / cap)

def mlstm_chunkwise(q, k, v, log_i, log_f):
    bsz, nh, seq, dk = q.shape
    dv = v.shape[-1]
    nc = seq // CHUNK_A

    def to_chunks(t):
        return jnp.moveaxis(t.reshape((bsz, nh, nc, CHUNK_A) + t.shape[3:]), 2, 0)

    causal = jnp.tril(jnp.ones((CHUNK_A, CHUNK_A), dtype=bool))

    def step(carry, inp):
        c_mat, n_vec, m_run = carry
        qb, kb, vb, ib, fb = inp
        b = jnp.cumsum(fb, axis=-1)
        log_d = jnp.where(causal, b[..., :, None] - b[..., None, :] + ib[..., None, :], -jnp.inf)
        log_inter = b + m_run[..., None]
        m_t = jnp.maximum(log_inter, jnp.max(log_d, axis=-1))
        d_mat = jnp.exp(log_d - m_t[..., None])
        w_inter = jnp.exp(log_inter - m_t)
        s = jnp.einsum('bhtd,bhsd->bhts', qb, kb) * d_mat
        num = jnp.einsum('bhts,bhsv->bhtv', s, vb) + w_inter[..., None] * jnp.einsum('bhtd,bhdv->bhtv', qb, c_mat)
        den = jnp.sum(s, axis=-1) + w_inter * jnp.einsum('bhtd,bhd->bht', qb, n_vec)
        h = num / jnp.maximum(jnp.abs(den), jnp.exp(-m_t))[..., None]
        b_end = b[..., -1]
        log_w = b_end[..., None] - b + ib
        m_new = jnp.maximum(b_end + m_run, jnp.max(log_w, axis=-1))
        w = jnp.exp(log_w - m_new[..., None])
        decay = jnp.exp(b_end + m_run - m_new)
        kw = kb * w[..., None]
        c_new = decay[..., None, None] * c_mat + jnp.einsum('bhsd,bhsv->bhdv', kw, vb)
        n_new = decay[..., None] * n_vec + jnp.sum(kw, axis=2)
        return (c_new, n_new, m_new), h

    init = (jnp.zeros((bsz, nh, dk, dv), jnp.float32),
            jnp.zeros((bsz, nh, dk), jnp.float32),
            jnp.zeros((bsz, nh), jnp.float32))
    _, hs = lax.scan(step, init, (to_chunks(q), to_chunks(k), to_chunks(v), to_chunks(log_i), to_chunks(log_f)))
    return jnp.moveaxis(hs, 0, 2).reshape(bsz, nh, seq, dv)

def mlstm_mixer(xn, w_in, b_gate, head_gain, w_out):
    bsz, seq, _ = xn.shape
    q, k, v, o, gates = jnp.split(xn @ w_in, A_SPLITS, axis=-1)

    def heads(t, d):
        return t.reshape(bsz, seq, N_HEADS_A, d).transpose(0, 2, 1, 3).astype(jnp.float32)

    qh = heads(q, DQK_A)
    kh = heads(k, DQK_A) * (DQK_A ** -0.5)
    vh = heads(v, DV_A)
    g = softcap((gates + b_gate).astype(jnp.float32), GATE_CAP).transpose(0, 2, 1)
    log_i = g[:, :N_HEADS_A]
    log_f = jax.nn.log_sigmoid(g[:, N_HEADS_A:])
    h = mlstm_chunkwise(qh, kh, vh, log_i, log_f).transpose(0, 2, 1, 3)
    h = h * lax.rsqrt(jnp.mean(h * h, axis=-1, keepdims=True) + EPS)
    h = h.reshape(bsz, seq, D_MODEL).astype(xn.dtype) * head_gain * jax.nn.sigmoid(o)
    return h @ w_out

def shared_kv(hn, kv_w, kv_b_f, k_gain):
    bsz, seq, _ = hn.shape
    k, v, fg = jnp.split(hn @ kv_w, (D_MODEL, 2 * D_MODEL), axis=-1)
    k = rmsnorm(k.reshape(bsz, seq, N_HEADS_B, DH_B), k_gain).transpose(0, 2, 1, 3)
    v = v.reshape(bsz, seq, N_HEADS_B, DH_B).transpose(0, 2, 1, 3)
    log_f = jax.nn.log_sigmoid((fg + kv_b_f).astype(jnp.float32))
    c = jnp.cumsum(log_f, axis=1).transpose(0, 2, 1)
    return k, v, c

def fox_mixer(xn, k, v, c, w_in, q_gain, w_out):
    bsz, seq, _ = xn.shape
    q, og = jnp.split(xn @ w_in, (D_MODEL,), axis=-1)
    q = rmsnorm(q.reshape(bsz, seq, N_HEADS_B, DH_B), q_gain).transpose(0, 2, 1, 3) * (DH_B ** -0.5)
    outs = []
    for qb in range(seq // QBLOCK):
        lo = qb * QBLOCK
        hi = lo + QBLOCK
        logits = jnp.einsum('bhtd,bhsd->bhts', q[:, :, lo:hi], k[:, :, :hi]).astype(jnp.float32)
        logits = logits + c[:, :, lo:hi, None] - c[:, :, None, :hi]
        mask = jnp.arange(hi)[None, :] <= (lo + jnp.arange(QBLOCK))[:, None]
        p = jax.nn.softmax(jnp.where(mask, logits, -jnp.inf), axis=-1)
        outs.append(jnp.einsum('bhts,bhsd->bhtd', p.astype(v.dtype), v[:, :, :hi]))
    o = jnp.concatenate(outs, axis=2).transpose(0, 2, 1, 3).reshape(bsz, seq, D_MODEL)
    return (o * jax.nn.sigmoid(og)) @ w_out

def hier_moe(xn, w_grp, b_grp, w_exp, b_exp, w_gate, w_up, w_down):
    bsz, seq, d = xn.shape
    t = xn.reshape(-1, d)
    g_prob = jax.nn.softmax((t @ w_grp + b_grp).astype(jnp.float32), axis=-1)
    g_p, g_idx = lax.top_k(g_prob, 1)
    e_logits = (t @ w_exp + b_exp).astype(jnp.float32).reshape(-1, N_GROUPS, EXP_PER_GROUP)
    e_sel = jnp.einsum('tge,tg->te', e_logits, jax.nn.one_hot(g_idx[:, 0], N_GROUPS, dtype=jnp.float32))
    e_p, e_idx = lax.top_k(jax.nn.softmax(e_sel, axis=-1), TOP_K)
    e_p = e_p / jnp.sum(e_p, axis=-1, keepdims=True)
    weights = g_p * e_p
    expert_id = g_idx * EXP_PER_GROUP + e_idx
    combine = jnp.einsum('tk,tke->te', weights, jax.nn.one_hot(expert_id, N_EXPERTS, dtype=jnp.float32)).astype(t.dtype)
    y = jnp.zeros_like(t)
    for e in range(N_EXPERTS):
        hdn = jax.nn.silu(t @ w_gate[e]) * (t @ w_up[e])
        y = y + combine[:, e:e + 1] * (hdn @ w_down[e])
    return y.reshape(bsz, seq, d)

def setup_inputs(seed: int = 0) -> dict:
    key = jax.random.key(seed)
    ks = jax.random.split(key, 24)
    f32 = jnp.float32

    def nrm(k, shape, scale):
        return jax.random.normal(k, shape, f32) * scale

    def gain(k, shape):
        return 1.0 + 0.05 * jax.random.normal(k, shape, f32)

    x = nrm(ks[0], (BATCH, SEQ, D_MODEL), 1.0)
    norm_mix = gain(ks[1], (DEPTH, D_MODEL))
    norm_ffn = gain(ks[2], (DEPTH, D_MODEL))
    a_w_in = nrm(ks[3], (N_A_LAYERS, D_MODEL, A_IN), D_MODEL ** -0.5)
    a_b_gate = jnp.concatenate([nrm(ks[4], (N_A_LAYERS, N_HEADS_A), 0.1),
                                3.0 + nrm(ks[5], (N_A_LAYERS, N_HEADS_A), 0.5)], axis=-1)
    a_head_gain = gain(ks[6], (N_A_LAYERS, D_MODEL))
    a_w_out = nrm(ks[7], (N_A_LAYERS, D_MODEL, D_MODEL), D_MODEL ** -0.5)
    kv_norm = gain(ks[8], (D_MODEL,))
    kv_w = nrm(ks[9], (D_MODEL, KV_OUT), D_MODEL ** -0.5)
    kv_b_f = 2.0 + nrm(ks[10], (N_HEADS_B,), 0.5)
    kv_k_gain = gain(ks[11], (DH_B,))
    b_w_in = nrm(ks[12], (N_B_LAYERS, D_MODEL, B_IN), D_MODEL ** -0.5)
    b_q_gain = gain(ks[13], (N_B_LAYERS, DH_B))
    b_w_out = nrm(ks[14], (N_B_LAYERS, D_MODEL, D_MODEL), D_MODEL ** -0.5)
    moe_w_grp = nrm(ks[15], (DEPTH, D_MODEL, N_GROUPS), D_MODEL ** -0.5)
    moe_b_grp = nrm(ks[16], (DEPTH, N_GROUPS), 0.01)
    moe_w_exp = nrm(ks[17], (DEPTH, D_MODEL, N_EXPERTS), D_MODEL ** -0.5)
    moe_b_exp = nrm(ks[18], (DEPTH, N_EXPERTS), 0.01)
    moe_w_gate = nrm(ks[19], (DEPTH, N_EXPERTS, D_MODEL, D_EXPERT), D_MODEL ** -0.5)
    moe_w_up = nrm(ks[20], (DEPTH, N_EXPERTS, D_MODEL, D_EXPERT), D_MODEL ** -0.5)
    moe_w_down = nrm(ks[21], (DEPTH, N_EXPERTS, D_EXPERT, D_MODEL), D_EXPERT ** -0.5)
    norm_final = gain(ks[22], (D_MODEL,))
    return {'x': x, 'norm_mix': norm_mix, 'norm_ffn': norm_ffn,
            'a_w_in': a_w_in, 'a_b_gate': a_b_gate, 'a_head_gain': a_head_gain, 'a_w_out': a_w_out,
            'kv_norm': kv_norm, 'kv_w': kv_w, 'kv_b_f': kv_b_f, 'kv_k_gain': kv_k_gain,
            'b_w_in': b_w_in, 'b_q_gain': b_q_gain, 'b_w_out': b_w_out,
            'moe_w_grp': moe_w_grp, 'moe_b_grp': moe_b_grp, 'moe_w_exp': moe_w_exp, 'moe_b_exp': moe_b_exp,
            'moe_w_gate': moe_w_gate, 'moe_w_up': moe_w_up, 'moe_w_down': moe_w_down,
            'norm_final': norm_final}

def reference(x, norm_mix, norm_ffn, a_w_in, a_b_gate, a_head_gain, a_w_out, kv_norm, kv_w, kv_b_f, kv_k_gain,
              b_w_in, b_q_gain, b_w_out, moe_w_grp, moe_b_grp, moe_w_exp, moe_b_exp, moe_w_gate, moe_w_up,
              moe_w_down, norm_final):
    h = x
    k_sh = None
    v_sh = None
    c_sh = None
    for layer in range(DEPTH):
        xn = rmsnorm(h, norm_mix[layer])
        if layer < N_A_LAYERS:
            h = h + mlstm_mixer(xn, a_w_in[layer], a_b_gate[layer], a_head_gain[layer], a_w_out[layer])
        else:
            j = layer - N_A_LAYERS
            h = h + fox_mixer(xn, k_sh, v_sh, c_sh, b_w_in[j], b_q_gain[j], b_w_out[j])
        h = h + hier_moe(rmsnorm(h, norm_ffn[layer]), moe_w_grp[layer], moe_b_grp[layer], moe_w_exp[layer],
                         moe_b_exp[layer], moe_w_gate[layer], moe_w_up[layer], moe_w_down[layer])
        if layer == N_A_LAYERS - 1:
            k_sh, v_sh, c_sh = shared_kv(rmsnorm(h, kv_norm), kv_w, kv_b_f, kv_k_gain)
    return rmsnorm(h, norm_final)


_drawn_inputs = setup_inputs


def setup_inputs(seed=0):
    import zlib

    import numpy as np

    out = dict(_drawn_inputs(seed))
    spreads = {}
    factors = {'kv_norm': 2.845,
     'kv_k_gain': 4.317,
     'b_q_gain': 4.542,
     'moe_b_grp': 2.802,
     'moe_b_exp': 4.494}
    for name, (base, spread) in spreads.items():
        noise = np.random.default_rng([zlib.crc32(name.encode()), seed]).standard_normal(out[name].shape)
        drawn = base * np.exp(spread * noise) if base else spread * noise
        out[name] = jnp.asarray(drawn.astype(out[name].dtype))
    for name, factor in factors.items():
        out[name] = (out[name] * factor).astype(out[name].dtype)
    return out
```

```python
from contextlib import ExitStack

import concourse.bass as bass
from concourse import mybir

P = 128
F32 = mybir.dt.float32
BF16 = mybir.dt.bfloat16
I32 = mybir.dt.int32
ALU = mybir.AluOpType
ACT = mybir.ActivationFunctionType
AX = mybir.AxisListType

SEQ, D = 512, 1024
NT = SEQ // P
KD = D // P
EPS = 1e-6
HA, DQK, DV = 4, 128, 256
CAP = 15.0
HB, DH = 16, 64
NG, EG = 4, 4
NE = NG * EG
DE = 512
KE = DE // P
W = 512
CH = KD * W
RING = 6
BIG = 1e30
LISTS = NE * SEQ
NB = SEQ // P
NOV = NE * (NB - 1)
OVMAX = 8
NOCODE = 2 * LISTS


def plan_chunks():
    mix_a = [("a_in", 0, c) for c in range(6)] + [("a_out", 0, c) for c in range(2)]
    moe = lambda l: [(w, l, e) for e in range(NE) for w in ("gate", "up", "down")]
    mix_b = [("kv", 0, c) for c in range(4)] + [("b_in", 0, c) for c in range(4)] + [("b_out", 0, c) for c in range(2)]
    seq = mix_a + moe(0) + mix_b + moe(1)
    slots = [c % RING for c in range(len(mix_a) + 3 * NE)]
    slots += [(2, 3, 4, 0, 1)[c % 5] for c in range(len(mix_b))]
    slots += [(2, 3, 4, 0, 1, 5)[c % 6] for c in range(3 * NE)]
    return seq, slots


def trunk(nc, x, norm_mix, norm_ffn, a_w_in, a_b_gate, a_head_gain, a_w_out, kv_norm, kv_w, kv_b_f, kv_k_gain,
          b_w_in, b_q_gain, b_w_out, moe_w_grp, moe_b_grp, moe_w_exp, moe_b_exp, moe_w_gate, moe_w_up,
          moe_w_down, norm_final, out):
    seq, slots = plan_chunks()
    cidx = {k: n for n, k in enumerate(seq)}
    nth = [slots[:n].count(slots[n]) for n in range(len(seq))]
    before = [max([m for m in range(n) if slots[m] == slots[n]], default=None) for n in range(len(seq))]

    xd = [nc.dram_tensor(f"normed_{l}", [SEQ, D], F32, kind="Internal").ap() for l in range(2)]
    codes_d = [nc.dram_tensor(f"lists_{l}", [LISTS, 1], I32, kind="Internal").ap() for l in range(2)]
    yd = [nc.dram_tensor(f"expert_out_{l}", [2 * SEQ, D], F32, kind="Internal").ap() for l in range(2)]

    with ExitStack() as ctx:
        def sb(name, shape, dt=F32):
            return ctx.enter_context(nc.sbuf_tensor(name, shape, dt))

        sems = {}

        def S(name):
            if name not in sems:
                sems[name] = ctx.enter_context(nc.semaphore(name))
            return sems[name]

        ps = ctx.enter_context(nc.psum_tensor("ps", [P, 8, 512], F32))
        h = sb("h", [P, NT, D])
        xT = sb("xT", [P, KD, SEQ])
        ring = sb("ring", [P, RING, CH])
        arena = sb("arena", [P, ARENA])
        ident = sb("ident", [P, P])
        mask_ts = sb("mask_ts", [P, P])
        mask_st = sb("mask_st", [P, P])
        tri_bf = sb("tri_bf", [P, P], BF16)
        ones_bf = sb("ones_bf", [P, P], BF16)
        rows = sb("rows", [54, P])
        gains = sb("gains", [P, 54])
        gate15 = sb("gate15", [P, 1])
        eps_col = sb("eps_col", [P, 1])
        ones_col = sb("ones_col", [P, 1])
        held = sb("held", [P, 8])
        w_gates = sb("w_gates", [P, KD, 36])
        w_fg = sb("w_fg", [P, KD, HB])
        w_rt = sb("w_rt", [P, 2, KD, NG + NE])
        stat = sb("stat", [P, 96])
        place_codes = sb("place_codes", [P, 2, NT], I32)
        dst = sb("dst", [P, 2, NT], I32)
        tok = sb("tok", [P, NE * NB], I32)
        ydst = sb("ydst", [P, NE * NB], I32)
        fix = sb("fix", [P, 2], I32)
        ov = sb("ov", [1, 24], I32)
        wts = sb("wts", [P, 2, NT])

        top = [0]

        def cut(n, shape=None, parts=P, at=None):
            o = top[0] if at is None else at
            if at is None:
                top[0] = o + n
            assert o + n <= ARENA, o + n
            v = arena[0:parts, o:o + n]
            return v.rearrange(*shape[:1], **shape[1]) if shape else v

        top[0] = 0
        qT = cut(HA * SEQ, ("p (h t) -> p h t", dict(h=HA)))
        kT = cut(HA * SEQ, ("p (h t) -> p h t", dict(h=HA)))
        va = cut(NT * HA * (DV + 1), ("p (t h v) -> p t h v", dict(t=NT, h=HA)))
        so = cut(NT * D, ("p (t d) -> p t d", dict(t=NT)))
        dec = cut(HA * 1280, ("p (h c) -> p h c", dict(h=HA)))
        g_t = arena[0:36, 8208:8208 + 512]
        g_e = arena[0:4, 8208 + 512:8208 + 1024]
        g_lf = arena[0:4, 8208 + 1024:8208 + 1536]
        g_b = arena[0:4, 8208 + 1536:8208 + 2048]
        g_um = arena[0:36, 8208 + 2048:8208 + 2560]
        g_m = arena[0:4, 8208 + 2560:8208 + 3072]
        sqa = arena[:, UMN + 144:UMN + 144 + NT * DV].rearrange("p (t v) -> p t v", t=NT)
        stage = arena[:, 0:NT * D].rearrange("p (t d) -> p t d", t=NT)
        junk = arena[:, 4096:4096 + NT * D].rearrange("p (t d) -> p t d", t=NT)
        top[0] = 0
        kTb = cut(8 * SEQ, ("p (r t) -> p r t", dict(r=8)))
        qTb = cut(8 * SEQ, ("p (r t) -> p r t", dict(r=8)))
        vb = cut(NT * D, ("p (t d) -> p t d", dict(t=NT)))
        cT = cut(SEQ, parts=HB)
        p_at = top[0]
        pbuf = cut(3 * 512, ("p (n c) -> p n c", dict(n=3)))
        ptb = cut(2 * 512, ("p (n c) -> p n c", dict(n=2)))
        negc = cut(2 * 512, ("p (n c) -> p n c", dict(n=2)))
        negd = cut(512)
        nat = arena[:, p_at:p_at + 1024].rearrange("p (n c) -> p n c", n=2)
        sq = arena[:, p_at + 1024:p_at + 1536]
        f_z = arena[0:HB, p_at + 1536:p_at + 2048]
        f_a = arena[0:HB, p_at + 2048:p_at + 2560]
        f_e = arena[0:HB, p_at + 2560:p_at + 3072]
        f_l = arena[0:HB, p_at + 3072:p_at + 3584]
        sg_og = arena[:, p_at:p_at + 1024].rearrange("p (n c) -> p n c", n=2)
        x2 = ring[:, 5, :].rearrange("p (k t) -> p k t", k=KD)
        xg = arena[:, 0:2048].rearrange("p (n d) -> p n d", n=2)
        xgT = arena[:, 2048:4096].rearrange("p (n k s) -> p n k s", n=2, k=KD)
        sg = arena[:, 4096:4608]
        hn = arena[:, 4608:5120]
        hT = arena[:, 5120:5632]
        yb = arena[:, 5632:7680].rearrange("p (n d) -> p n d", n=2)
        yy = arena[:, 7680:7680 + 8192].rearrange("p (n d) -> p n d", n=8)
        ow = arena[:, 7680:7680 + 8192].rearrange("p (n c) -> p n c", n=2)
        r0 = 7680
        lgT = arena[0:NG + NE, r0:r0 + 512]
        rt = lambda o, n: arena[:, r0 + 512 + o:r0 + 512 + o + n]
        L = rt(0, NT * 20).rearrange("p (t c) -> p t c", t=NT)
        gd = rt(80, 16).rearrange("p (t g) -> p t g", t=NT)
        ge = rt(96, 16).rearrange("p (t g) -> p t g", t=NT)
        ohg = rt(112, 16).rearrange("p (t g) -> p t g", t=NT)
        tmp4 = rt(128, 16).rearrange("p (t g) -> p t g", t=NT)
        esel = rt(144, 16).rearrange("p (t g) -> p t g", t=NT)
        oh1 = rt(160, 16).rearrange("p (t g) -> p t g", t=NT)
        oh2 = rt(176, 16).rearrange("p (t g) -> p t g", t=NT)
        prod = rt(192, 64)
        ohE = [rt(256, 64), rt(320, 64)]
        posd = rt(384, 64)
        prio = rt(448, 4)
        ebase = rt(452, 16)
        lst_i = arena[0:NE * NB, r0 + 1100:r0 + 1228]
        lst_f = arena[0:NE * NB, r0 + 1228:r0 + 1356]
        cfull = rt(1000, 64)
        cge = rt(1064, 64)
        cuse = rt(1128, 64)
        cres = rt(1192, 64)
        sel_bf = arena[:, r0 + 1800:r0 + 1800 + 32].bitcast(BF16)
        cnt = arena[0:1, r0 + 1900:r0 + 1916]
        bt = arena[0:1, r0 + 1920:r0 + 1968]
        act48 = arena[0:1, r0 + 1968:r0 + 2016]
        cs48 = arena[0:1, r0 + 2016:r0 + 2064]
        id48 = arena[0:1, r0 + 2064:r0 + 2112]
        e48 = arena[0:1, r0 + 2112:r0 + 2160]
        j8 = arena[0:1, r0 + 2160:r0 + 2168]
        m384 = arena[0:1, r0 + 2200:r0 + 2584]
        q384 = arena[0:1, r0 + 2600:r0 + 2984]
        ovf = arena[0:1, r0 + 3000:r0 + 3024]
        nf = arena[:, 0:D]
        fo = arena[:, 8192:8192 + NT * D].rearrange("p (t d) -> p t d", t=NT)

        DW = [512, 384, 256, 128]
        DO = [0, 512, 896, 1152]

        block = ctx.enter_context(nc.Block())

        wv = {
            "a_in": a_w_in[0].rearrange("(k p) n -> p k n", p=P), "a_out": a_w_out[0].rearrange("(k p) n -> p k n", p=P),
            "kv": kv_w.rearrange("(k p) n -> p k n", p=P), "b_in": b_w_in[0].rearrange("(k p) n -> p k n", p=P),
            "b_out": b_w_out[0].rearrange("(k p) n -> p k n", p=P),
            "gate": moe_w_gate.rearrange("l e (k p) n -> l e p k n", p=P),
            "up": moe_w_up.rearrange("l e (k p) n -> l e p k n", p=P),
            "down": moe_w_down.rearrange("l e (k p) n -> l e p k n", p=P),
        }

        def as_kn(flat, kind):
            return flat.rearrange("p (k n) -> p k n", k=KE if kind == "down" else KD)

        def landed(n):
            return S(f"weights_in_slot{slots[n]}"), 16 * (nth[n] + 1)

        release = {}
        A_GROUPS = [("gates", None, 0)] + [("q", 0, i) for i in range(4)] + [("k", 1, i) for i in range(4)] + \
            [(w, c, i) for w, cc in (("v", (2, 3)), ("o", (4, 5))) for c in cc for i in range(NT)]
        B_GROUPS = [("fg", None, 0)] + [(w, c, i) for w, cc in (("k", (0, 1)), ("v", (2, 3)), ("q", (4, 5)))
                                        for c in cc for i in range(NT)]
        for g, (w, c, i) in enumerate(A_GROUPS):
            if c is not None:
                release[cidx[("a_in", 0, c)]] = ("projA", g + 1)
        for c in range(2):
            release[cidx[("a_out", 0, c)]] = ("outA", NT * (c + 1))
            release[cidx[("b_out", 0, c)]] = ("outB", NT * (c + 1))
            release[cidx[("b_in", 0, c + 2)]] = ("ogB", 4 * (c + 1))
        for g, (w, c, i) in enumerate(B_GROUPS):
            if c is not None:
                release[cidx[("kv", 0, c) if c < 4 else ("b_in", 0, c - 4)]] = ("projB", g + 1)
        for l in range(2):
            for e in range(NE):
                for w in ("gate", "up", "down"):
                    release[cidx[(w, l, e)]] = (f"{w}_done{l}", e + 1)

        @block.sync
        def _(sp):
            sp.dma_start(h[:, :, :], x[0].rearrange("(t p) d -> p t d", p=P)).then_inc(S("x_loaded"), 16)

            def load(n):
                kind, l, i = seq[n]
                if before[n] is not None:
                    name, v = release[before[n]]
                    sp.wait_ge(S(name), v)
                src = wv[kind][l, i] if kind in ("gate", "up", "down") else wv[kind][:, :, i * W:(i + 1) * W]
                if n == cidx[("down", 1, 1)]:
                    sp.wait_ge(S("outB"), 2 * NT)
                sp.dma_start(as_kn(ring[:, slots[n], :], kind), src).then_inc(landed(n)[0], 16)

            first = cidx[("gate", 0, 0)]
            for n in range(first + 6):
                load(n)
            for l in range(2):
                n0 = cidx[("gate", l, 0)]
                with sp.Fori(0, NE // 2 - 1) as i:
                    for par in range(2):
                        for m, w in enumerate(("gate", "up", "down")):
                            sp.wait_ge(S(f"{w}_done{l}"), 2 * i + par + 1)
                            sp.dma_start(as_kn(ring[:, slots[n0 + 3 * par + m], :], w), wv[w][l, 2 * i + par + 2])\
                                .then_inc(landed(n0 + 3 * par + m)[0], 16)
                sp.wait_ge(S("ov_ready"), l + 1)
                n_ov = sp.value_load(ov[0:1, 0:1], min_val=0, max_val=OVMAX)
                with sp.If(n_ov > 0), sp.Fori(0, n_ov) as j:
                    sp.wait_ge(S(f"scattered{l}_0"), 16 * (j + NE // 2))
                    sp.wait_ge(S(f"scattered{l}_1"), NE // 2 * 16)
                    ex = sp.value_load(ov[0:1, bass.ds(j + 16, 1)], min_val=0, max_val=NE - 1)
                    sp.dma_start(as_kn(ow[:, 0, :], "gate"), wv["gate"][l, ex]).then_inc(S(f"ov_weights{l}"), 16)
                    sp.dma_start(as_kn(ow[:, 1, :], "up"), wv["up"][l, ex]).then_inc(S(f"ov_weights{l}"), 16)
                    sp.wait_ge(S(f"gate_done{l}"), j + NE + 1)
                    sp.dma_start(as_kn(ow[:, 0, :], "down"), wv["down"][l, ex]).then_inc(S(f"ov_down{l}"), 16)
                if l == 0:
                    for n in range(cidx[("kv", 0, 0)], cidx[("gate", 1, 0)] + 6):
                        load(n)
            for t in range(NT):
                sp.wait_ge(S("final_rows"), t + 1)
                sp.dma_start(out[0, t * P:(t + 1) * P, :], fo[:, t, :]).then_inc(S("stored"), 16)
            sp.wait_ge(S("stored"), 16 * NT)

        @block.gpsimd
        def _(pool):
            chain = [0]

            def link(ins):
                chain[0] += 1
                ins.then_inc(S("pool_step"), 1)
                pool.wait_ge(S("pool_step"), chain[0])

            pool.memset(ident[:, :], 0.0)
            pool.memset(mask_ts[:, :], 0.0)
            pool.memset(mask_st[:, :], 0.0)
            pool.memset(tri_bf[:, :], 1.0)
            pool.memset(ones_bf[:, :], 1.0)
            link(pool.memset(eps_col[:, :], EPS))
            pool.affine_select(out=ident[:, :], in_=ident[:, :], compare_op=ALU.not_equal, fill=1.0, base=0,
                               pattern=[[-1, P]], channel_multiplier=1)
            pool.affine_select(out=mask_ts[:, :], in_=mask_ts[:, :], compare_op=ALU.is_ge, fill=-BIG, base=0,
                               pattern=[[-1, P]], channel_multiplier=1)
            pool.affine_select(out=mask_st[:, :], in_=mask_st[:, :], compare_op=ALU.is_ge, fill=BIG, base=0,
                               pattern=[[1, P]], channel_multiplier=-1)
            pool.affine_select(out=tri_bf[:, :], in_=tri_bf[:, :], compare_op=ALU.is_gt, fill=0.0, base=0,
                               pattern=[[1, P]], channel_multiplier=-1)
            pool.iota(place_codes[:, :, :], pattern=[[SEQ, 2], [P, NT]], base=0, channel_multiplier=1)
            pool.iota(tok[:, :], pattern=[[0, NE * NB]], base=NOCODE, channel_multiplier=0)\
                .then_inc(S("consts"), 1)
            pool.wait_ge(S("consts"), 1)
            for l in range(2):
                pool.dma_start(codes_d[l].rearrange("(p c) a -> p (c a)", p=P), tok[:, :]).then_inc(S("lists_empty"), 16)
            for l in range(2):
                for t in range(NT):
                    pool.wait_ge(S("xn_ready"), NT * (2 * l + 1) + t + 1)
                    pool.dma_start(xd[l][t * P:(t + 1) * P, :], stage[:, t, :]).then_inc(S("rows_stored"), 16)
                pool.wait_ge(S("lists_empty"), 32)
                pool.wait_ge(S("places_ready"), l + 1)
                for k in range(2):
                    for t in range(NT):
                        pool.indirect_dma_start(codes_d[l], bass.IndirectOffsetOnAxis(ap=dst[:, k, t:t + 1], axis=0),
                                                place_codes[:, k, t:t + 1], None, bounds_check=LISTS - 1,
                                                oob_is_err=False).then_inc(S("codes_stored"), 16)
                pool.wait_ge(S("codes_stored"), 16 * 2 * NT * (l + 1))
                pool.dma_start(lst_i.bitcast(I32), codes_d[l].rearrange("(r c) a -> r (c a)", c=P))\
                    .then_inc(S("lists_loaded"), 16)
                pool.wait_ge(S("rows_stored"), 16 * NT * (l + 1))
                pool.wait_ge(S("tok_ready"), l + 1)

                def gather(idx, par):
                    pool.indirect_dma_start(xg[:, par, :], None, xd[l], bass.IndirectOffsetOnAxis(ap=idx, axis=0),
                                            bounds_check=SEQ - 1, oob_is_err=False).then_inc(S(f"gathered{l}_{par}"), 16)

                def scatter(idx, par):
                    pool.indirect_dma_start(yd[l], bass.IndirectOffsetOnAxis(ap=idx, axis=0), yb[:, par, :], None,
                                            bounds_check=2 * SEQ - 1, oob_is_err=False)\
                        .then_inc(S(f"scattered{l}_{par}"), 16)

                gather(tok[:, 0:1], 0)
                gather(tok[:, NB:NB + 1], 1)
                for e in range(NE):
                    if e + 2 < NE:
                        pool.wait_ge(S(f"xg_turned{l}"), e + 1)
                        gather(tok[:, NB * (e + 2):NB * (e + 2) + 1], e % 2)
                    pool.wait_ge(S(f"y_act{l}"), e + 1)
                    pool.wait_ge(S(f"y_dve{l}"), e + 1)
                    scatter(ydst[:, NB * e:NB * e + 1], e % 2)
                n_ov = pool.value_load(ov[0:1, 0:1], min_val=0, max_val=OVMAX)

                def hold(q):
                    pool.tensor_tensor(held[:, 4 * l + q:4 * l + q + 1], ones_col[:, :], ones_col[:, :], ALU.mult)\
                        .then_inc(S(f"pool_held{l}"), 1)

                hold(3)
                with pool.If(n_ov > 0), pool.Fori(0, n_ov) as j:
                    pool.wait_ge(S(f"fix_ready{l}"), j + 1)
                    hold(0)
                    gather(fix[:, 0:1], 0)
                    pool.wait_ge(S(f"y_dve{l}"), j + NE + 1)
                    hold(1)
                    pool.wait_ge(S(f"y_act{l}"), j + NE + 1)
                    hold(2)
                    scatter(fix[:, 1:2], 0)
                pool.wait_ge(S("tiles_stored"), l + 1)
                for t in range(NT):
                    pool.dma_start(yy[:, 2 * t:2 * t + 2, :],
                                   yd[l].rearrange("(k t p) d -> t p k d", k=2, p=P)[t]).then_inc(S("y_back"), 16)
                    pool.wait_ge(S("y_back"), 16 * (NT * l + t + 1))
            pool.wait_ge(S("h_final"), NT * 4)
            pool.dma_start(nf, norm_final.rearrange("(a d) -> a d", a=1).broadcast_to([P, D]))\
                .then_inc(S("nf_loaded"), 16)
            pool.wait_ge(S("nf_loaded"), 16)

        @block.tensor
        def _(pe):
            pe.wait_ge(S("consts"), 1)
            pe.wait_ge(S("rows_loaded"), 16 * ROWS_DMAS)
            pe.transpose(ps[:, 0, 0:54], rows[:, :], ident[0:54, 0:54]).then_inc(S("gains_turned"), 1)

            def turn_normed(i):
                for t in range(NT):
                    pe.wait_ge(S("xn_ready"), NT * i + t + 1)
                    for k in range(KD):
                        m = pe.transpose(ps[:, k, t * P:(t + 1) * P], stage[:, t, k * P:(k + 1) * P], ident[:, :])
                        if t == NT - 1:
                            m.then_inc(S("xn_turned"), 1)
                pe.wait_ge(S("xT_dve"), KD // 2 * (i + 1))
                pe.wait_ge(S("xT_act"), KD // 2 * (i + 1))

            def group(lhs, rhs, outp, done):
                n = len(lhs)
                for k in range(n):
                    m = pe.matmul(outp, lhs[k], rhs[k], start=(k == 0), stop=(k == n - 1))
                m.then_inc(S(done), 1)

            def chunk(n):
                pe.wait_ge(*landed(n))
                return as_kn(ring[:, slots[n], :], seq[n][0])

            def bank_free(groups, g, mixer):
                if g >= 6:
                    eng = EVAC[mixer][g - 6]
                    pe.wait_ge(S(f"{eng}_evac{mixer}"), EVAC[mixer][:g - 5].count(eng))

            pe.wait_ge(S("gains_ready"), 1)
            turn_normed(0)
            pe.wait_ge(S("gates_w"), 32)
            xk = [xT[:, k, :] for k in range(KD)]
            for g, (w, c, i) in enumerate(A_GROUPS):
                bank_free(A_GROUPS, g, "A")
                b = g % 6
                if w == "gates":
                    group([w_gates[:, k, :] for k in range(KD)], xk, ps[0:36, b, :], "projA")
                else:
                    wt = chunk(cidx[("a_in", 0, c)])
                    if w in "qk":
                        group([wt[:, k, i * P:(i + 1) * P] for k in range(KD)], xk, ps[:, b, :], "projA")
                    else:
                        group([xT[:, k, i * P:(i + 1) * P] for k in range(KD)], [wt[:, k, :] for k in range(KD)],
                              ps[:, b, :], "projA")
                if g == 12:
                    pe.wait_ge(S("um_ready"), 1)
                    for t in range(NT):
                        m = pe.transpose(ps[:, 6, t * 36:(t + 1) * 36], g_um[:, t * P:(t + 1) * P], ident[0:36, 0:36])
                    m.then_inc(S("um_turned"), 1)
                if 13 <= g < 13 + HA:
                    if g > 13:
                        pe.wait_ge(S("m_spread_used"), g - 13)
                    pe.matmul(ps[:, 7, :], ident[0:4, g - 13:g - 12].broadcast_to([4, P]), g_m,
                              start=True, stop=True).then_inc(S("m_spread"), 1)
            pe.wait_ge(S("D_evacA"), EVAC["A"].count("D"))
            pe.wait_ge(S("A_evacA"), EVAC["A"].count("A"))

            def scores_a(hd):
                for i in range(NT):
                    if hd:
                        pe.wait_ge(S("pt_ready"), NT * (hd - 1) + i + 1)
                    pe.matmul(ps[:, i, 0:DW[i]], kT[:, hd, i * P:(i + 1) * P], qT[:, hd, i * P:], start=True,
                              stop=True).then_inc(S("st_ready"), 1)

            pe.wait_ge(S("m_spread_used"), HA)
            scores_a(0)
            for hd in range(HA):
                if hd + 1 < HA:
                    scores_a(hd + 1)
                pe.wait_ge(S("pt_ready"), NT * (hd + 1))
                for j in range(NT):
                    if hd:
                        pe.wait_ge(S("num_used"), NT * (hd - 1) + j + 1)
                    for i in range(j + 1):
                        o = DO[i] + (j - i) * P
                        m = pe.matmul(ps[:, 4 + j, 0:DV + 1], dec[:, hd, o:o + P], va[:, i, hd, :],
                                      start=(i == 0), stop=(i == j))
                    m.then_inc(S("num_ready"), 1)
            pe.wait_ge(S("num_used"), NT * HA)
            for k in range(KD):
                for t in range(NT):
                    m = pe.transpose(ps[:, k, t * P:(t + 1) * P], so[:, t, k * P:(k + 1) * P], ident[:, :])
                m.then_inc(S("hg_turned"), 1)
            pe.wait_ge(S("hgT_dve"), KD // 2)
            pe.wait_ge(S("hgT_act"), KD // 2)

            def out_proj(kind, act, done):
                for c in range(2):
                    wt = chunk(cidx[(kind, 0, c)])
                    for t in range(NT):
                        group([act[:, k, t * P:(t + 1) * P] for k in range(KD)], [wt[:, k, :] for k in range(KD)],
                              ps[:, NT * c + t, :], done)

            out_proj("a_out", xT, "outA")

            def moe(l):
                i = 2 * l + 1
                pe.wait_ge(S("h_final"), NT * i)
                turn_normed(i)
                pe.wait_ge(S("rt_w"), 64)
                group([w_rt[:, l, k, :] for k in range(KD)], xk, ps[0:NG + NE, 0, :], "logits")
                pe.wait_ge(S("lgT_ready"), l + 1)
                for t in range(NT):
                    m = pe.transpose(ps[:, 1, t * 20:(t + 1) * 20], lgT[:, t * P:(t + 1) * P], ident[0:20, 0:20])
                m.then_inc(S("lg_turned"), 1)
                pe.wait_ge(S("sel_ready"), l + 1)
                selv = sel_bf.rearrange("p (t e) -> p t e", t=NT)
                for t in range(NT):
                    for s in range(t + 1):
                        pe.matmul(ps[:, 2, t * NE:(t + 1) * NE], tri_bf[:, :] if s == t else ones_bf[:, :],
                                  selv[:, s, :], start=(s == 0), stop=(s == t))
                for t in range(NT):
                    m = pe.matmul(ps[0:1, 3, 0:NE], ones_bf[:, 0:1], selv[:, t, :], start=(t == 0), stop=(t == NT - 1))
                m.then_inc(S("places"), 1)
                pe.wait_ge(S("lst_ready"), l + 1)
                pe.transpose(ps[:, 4, 0:NE * NB], lst_f, ident[0:NE * NB, 0:NE * NB]).then_inc(S("lst_turned"), 1)
                pe.wait_ge(S("tok_ready"), l + 1)
                n0 = cidx[("gate", l, 0)]

                def turn_x(n, nth_of_buffer, par):
                    pe.wait_ge(S(f"gathered{l}_{par}"), 16 * (nth_of_buffer + 1))
                    if not isinstance(n, int) or n:
                        pe.wait_ge(S(f"xgT_ready{l}"), n)
                    for k in range(KD):
                        m = pe.transpose(ps[:, 2 + k // 4, (k % 4) * P:(k % 4 + 1) * P],
                                         xg[:, par, k * P:(k + 1) * P], ident[:, :])
                    m.then_inc(S(f"xg_turned{l}"), 1)

                def expert(n, nth_of_buffer, par, ws, there, turn_next):
                    past = not isinstance(n, int) or n
                    pe.wait_ge(S(f"xgT_ready{l}"), n + 1)
                    if past:
                        pe.wait_ge(S(f"sg_ready{l}"), n)
                    pe.wait_ge(*there[0])
                    group([xgT[:, par, k, :] for k in range(KD)], [ws[0][:, k, :] for k in range(KD)],
                          ps[:, 0, :], f"gate_done{l}")
                    if past:
                        pe.wait_ge(S(f"hn_ready{l}"), n)
                    pe.wait_ge(*there[1])
                    group([xgT[:, par, k, :] for k in range(KD)], [ws[1][:, k, :] for k in range(KD)],
                          ps[:, 1, :], f"up_done{l}")
                    if turn_next:
                        turn_x(n + 1, nth_of_buffer + par, 1 - par)
                    pe.wait_ge(S(f"hn_ready{l}"), n + 1)
                    if past:
                        pe.wait_ge(S(f"hT_ready{l}"), n)
                    for k in range(KE):
                        m = pe.transpose(ps[:, 4, k * P:(k + 1) * P], hn[:, k * P:(k + 1) * P], ident[:, :])
                    m.then_inc(S(f"hn_turned{l}"), 1)
                    pe.wait_ge(S(f"hT_ready{l}"), n + 1)
                    if past:
                        pe.wait_ge(S(f"y_act{l}"), n)
                        pe.wait_ge(S(f"y_dve{l}"), n)
                    pe.wait_ge(*there[2])
                    for c in range(2):
                        for k in range(KE):
                            m = pe.matmul(ps[:, 5 + c, :], hT[:, k * P:(k + 1) * P], ws[2][:, k, c * 512:(c + 1) * 512],
                                          start=(k == 0), stop=(k == KE - 1))
                    m.then_inc(S(f"down_done{l}"), 1)

                def ring_expert(n, i, par, turn_next):
                    c = [n0 + 3 * par + m for m in range(3)]
                    there = [(landed(q)[0], 16 * i + landed(q)[1]) for q in c]
                    expert(n, i, par, [as_kn(ring[:, slots[q], :], seq[q][0]) for q in c], there, turn_next)

                turn_x(0, 0, 0)
                ring_expert(0, 0, 0, True)
                ring_expert(1, 0, 1, True)
                with pe.Fori(1, NE // 2 - 1) as i:
                    ring_expert(2 * i, i, 0, True)
                    ring_expert(2 * i + 1, i, 1, True)
                ring_expert(NE - 2, NE // 2 - 1, 0, True)
                ring_expert(NE - 1, NE // 2 - 1, 1, False)
                pe.wait_ge(S("ov_ready"), l + 1)
                n_ov = pe.value_load(ov[0:1, 0:1], min_val=0, max_val=OVMAX)
                with pe.If(n_ov > 0), pe.Fori(0, n_ov) as j:
                    turn_x(j + NE, j + NE // 2, 0)
                    wl = (S(f"ov_weights{l}"), 32 * j + 32)
                    expert(j + NE, j + NE // 2, 0, [as_kn(ow[:, 0, :], "gate"), as_kn(ow[:, 1, :], "up"), as_kn(ow[:, 0, :], "down")],
                           [wl, wl, (S(f"ov_down{l}"), 16 * j + 16)], False)

            moe(0)

            pe.wait_ge(S("y_act0"), NE)
            pe.wait_ge(S("y_dve0"), NE)
            turn_normed(2)
            pe.wait_ge(S("fg_w"), 16)
            x2k = [x2[:, k, :] for k in range(KD)]

            def turn_nat(n):
                pe.wait_ge(S("D_evacB"), n + 1 if n < 8 else n + 9)
                if n >= 2:
                    pe.wait_ge(S("headsT_ready"), n - 1)
                for r in range(4):
                    m = pe.transpose(ps[:, 6 + n % 2, r * P:(r + 1) * P], nat[:, n % 2, r * P:(r + 1) * P], ident[:, :])
                m.then_inc(S("nat_turned"), 1)

            pend = []
            for g, (w, c, i) in enumerate(B_GROUPS):
                bank_free(B_GROUPS, g, "B")
                b = g % 6
                if w == "fg":
                    group([w_fg[:, k, :] for k in range(KD)], x2k, ps[0:HB, b, :], "projB")
                else:
                    src = x2 if c < 4 else xT
                    wt = chunk(cidx[("kv", 0, c) if c < 4 else ("b_in", 0, c - 4)])
                    group([src[:, k, i * P:(i + 1) * P] for k in range(KD)], [wt[:, k, :] for k in range(KD)],
                          ps[:, b, :], "projB")
                if pend and pend[0][0] + 2 <= g:
                    turn_nat(pend.pop(0)[1])
                if w in "kq":
                    pend.append((g, (0 if w == "k" else 8) + (c % 4) * 4 + i))
            for _, n in pend:
                turn_nat(n)
            pe.wait_ge(S("headsT_ready"), 16)
            pe.wait_ge(S("D_evacB"), EVAC["B"].count("D"))

            def spread_c(hd):
                if hd:
                    pe.wait_ge(S("negc_ready"), hd)
                pe.matmul(ps[:, 6, :], ident[0:HB, hd:hd + 1].broadcast_to([HB, P]), cT, start=True, stop=True)\
                    .then_inc(S("c_spread"), 1)

            steps = [(hd, j) for hd in range(HB) for j in range(NT)]

            def score(n):
                hd, j = steps[n]
                o, r = 64 * (hd % 2), hd // 2
                if n >= 2:
                    pe.wait_ge(S("s_used"), n - 1)
                pe.matmul(ps[:, n % 2, 0:(j + 1) * P], qTb[o:o + DH, r, j * P:(j + 1) * P],
                          kTb[o:o + DH, r, 0:(j + 1) * P], start=True, stop=True).then_inc(S("s_ready"), 1)

            def turn_p(n):
                hd, j = steps[n]
                pe.wait_ge(S("p_ready"), n + 1)
                if n >= 2:
                    pe.wait_ge(S("pT_ready"), n - 1)
                for i in range(j + 1):
                    m = pe.transpose(ps[:, 2 + n % 2, i * P:(i + 1) * P], pbuf[:, n % 3, i * P:(i + 1) * P], ident[:, :])
                m.then_inc(S("p_turned"), 1)

            def attend(n):
                hd, j = steps[n]
                o, r = 64 * (hd % 2), hd // 2
                pe.wait_ge(S("pT_ready"), n + 1)
                if hd % 2 == 0 and j == 0 and r >= 2:
                    pe.wait_ge(S("oT_ready"), r - 1)
                for i in range(j + 1):
                    m = pe.matmul(ps[o:o + DH, 4 + r % 2, j * P:(j + 1) * P], vb[:, i, hd * DH:(hd + 1) * DH],
                                  ptb[:, n % 2, i * P:(i + 1) * P], start=(i == 0), stop=(i == j))
                m.then_inc(S("o_ready"), 1)

            spread_c(0)
            for n in range(len(steps) + 3):
                if n < len(steps):
                    if n % NT == 2 and n // NT + 1 < HB:
                        spread_c(n // NT + 1)
                    score(n)
                if 0 <= n - 2 < len(steps):
                    turn_p(n - 2)
                if n >= 3:
                    attend(n - 3)
            for q in range(8):
                c, r = q // 4, q % 4
                wt = chunk(cidx[("b_in", 0, 2 + c)])
                if q >= 4:
                    pe.wait_ge(S("og_read"), q - 3)
                group([wt[:, k, r * P:(r + 1) * P] for k in range(KD)], xk, ps[:, q % 4, :], "ogB")
            pe.wait_ge(S("oT_gated"), 8)
            pe.wait_ge(S("og_read"), 8)
            pe.wait_ge(S("oT_ready"), 8)
            out_proj("b_out", x2, "outB")
            moe(1)

        @block.vector
        def _(dve):
            chain = [0]

            def link(ins):
                chain[0] += 1
                ins.then_inc(S("dve_step"), 1)
                dve.wait_ge(S("dve_step"), chain[0])

            dve.memset(rows[:, :], 0.0).then_inc(S("zeroed"), 1)
            dve.memset(w_gates[:, :, :], 0.0).then_inc(S("zeroed"), 1)
            dve.memset(ones_col[:, :], 1.0)
            dve.wait_ge(S("gains_turned"), 1)
            link(dve.tensor_copy(gains[:, :], ps[:, 0, 0:54]))
            link(dve.tensor_scalar(gate15[:, :], gains[:, 50:51], 1.0 / CAP, None, ALU.mult))
            dve.tensor_copy(stat[:, 95:96], gate15[:, :]).then_inc(S("gains_ready"), 1)

            def norm(i):
                dve.wait_ge(S("rms"), i + 1)
                link(dve.reciprocal(stat[:, 4:8], stat[:, 0:4]))
                for t in range(NT):
                    dst_rows = stage[:, t, :]
                    dve.tensor_scalar(dst_rows, h[:, t, :], stat[:, 4 + t:5 + t], None, ALU.mult)\
                        .then_inc(S("xn_ready"), 1)

            def evac_xT(i, cols, dests):
                for k in range(0, KD, 2):
                    dve.wait_ge(S("xn_turned"), KD * i + k + 1)
                    for c, dd in zip(cols, dests):
                        m = dve.tensor_scalar(dd[:, k, :], ps[:, k, :], gains[:, c + k:c + k + 1], None, ALU.mult)
                    m.then_inc(S("xT_dve"), 1)

            norm(0)
            evac_xT(0, [0], [xT])
            for t in range(NT):
                m = dve.memset(va[:, t, :, DV:DV + 1], 1.0)
            link(m)
            link(dve.memset(g_um, 0.0))

            def evac_a(g):
                w, c, i = A_GROUPS[g]
                dve.wait_ge(S("projA"), g + 1)
                if w == "q":
                    m = dve.tensor_copy(qT[:, i, :], ps[:, g % 6, :])
                elif w == "k":
                    m = dve.tensor_scalar(kT[:, i, :], ps[:, g % 6, :], DQK ** -0.5, None, ALU.mult)
                else:
                    m = dve.tensor_copy(va[:, i, 2 * (c - 2):2 * (c - 2) + 2, 0:DV],
                                        ps[:, g % 6, :].rearrange("p (h v) -> p h v", h=2))
                m.then_inc(S("D_evacA"), 1)

            for g in range(1, 5):
                evac_a(g)
            dve.wait_ge(S("gates_ready"), 1)
            one4 = ones_col[0:4, 0:1].broadcast_to([4, SEQ])
            link(dve.tensor_tensor_scan(g_b, one4, g_lf, 0.0, ALU.mult, ALU.subtract))
            link(dve.scalar_tensor_tensor(out=g_um[0:4, :], in0=g_t[0:4, :], scalar=CAP, in1=g_b, op0=ALU.mult,
                                          op1=ALU.subtract))
            link(dve.tensor_tensor_scan(g_m, g_um[0:4, :], g_um[0:4, :], 0.0, ALU.max, ALU.max))
            dve.tensor_tensor(g_um[32:36, :], g_b, g_m, ALU.add).then_inc(S("um_ready"), 1)
            for g in range(5, 13):
                evac_a(g)
            dve.wait_ge(S("um_turned"), 1)
            umn = arena[:, UMN:UMN + 144].rearrange("p (t c) -> p t c", t=NT)
            dve.tensor_copy(arena[:, UMN:UMN + 144], ps[:, 6, 0:144]).then_inc(S("umn_ready"), 1)
            for hd in range(HA):
                evac_a(13 + hd)
                dve.wait_ge(S("m_spread"), hd + 1)
                for i in range(NT):
                    if i < NT - 1:
                        dve.tensor_copy(dec[:, hd, DO[i] + P:DO[i] + DW[i]], ps[:, 7, (i + 1) * P:])
                    m = dve.tensor_tensor(dec[:, hd, DO[i]:DO[i] + P], ps[:, 7, i * P:(i + 1) * P], mask_st[:, :],
                                          ALU.add)
                m.then_inc(S("m_spread_used"), 1)

            def weigh(hd):
                dve.wait_ge(S("dec_ready"), NT * (hd + 1))
                for i in range(NT):
                    dve.wait_ge(S("st_ready"), NT * hd + i + 1)
                    dd = dec[:, hd, DO[i]:DO[i] + DW[i]]
                    dve.tensor_tensor(dd, ps[:, i, 0:DW[i]], dd, ALU.mult).then_inc(S("pt_ready"), 1)

            weigh(0)
            for hd in range(HA):
                if hd + 1 < HA:
                    weigh(hd + 1)
                dve.wait_ge(S("num_ready"), NT * (hd + 1))
                dve.wait_ge(S("em_ready"), 1)
                link(dve.tensor_copy(stat[:, 8:12], ps[:, 4:8, DV]))
                link(dve.scalar_tensor_tensor(out=stat[:, 12:16], in0=stat[:, 8:12], scalar=-1.0, in1=stat[:, 8:12],
                                              op0=ALU.mult, op1=ALU.max))
                link(dve.tensor_tensor(stat[:, 16:20], stat[:, 12:16], stat[:, 32 + 4 * hd:36 + 4 * hd], ALU.max))
                dve.reciprocal(stat[:, 20:24], stat[:, 16:20]).then_inc(S("rden_ready"), 1)
                dve.wait_ge(S("hrms_ready"), hd + 1)
                link(dve.reciprocal(stat[:, 28:32], stat[:, 24:28]))
                link(dve.tensor_tensor(stat[:, 28:32], stat[:, 28:32], stat[:, 20:24], ALU.mult))
                for j in range(NT):
                    s = so[:, j, hd * DV:(hd + 1) * DV]
                    dve.scalar_tensor_tensor(out=s, in0=ps[:, 4 + j, 0:DV], scalar=stat[:, 28 + j:29 + j], in1=s,
                                             op0=ALU.mult, op1=ALU.mult).then_inc(S("num_used"), 1)
            for k in range(0, KD, 2):
                dve.wait_ge(S("hg_turned"), k + 1)
                dve.tensor_scalar(xT[:, k, :], ps[:, k, :], gains[:, 32 + k:33 + k], None, ALU.mult)\
                    .then_inc(S("hgT_dve"), 1)

            def residual(done, i):
                for c in range(2):
                    for t in range(NT):
                        dve.wait_ge(S(done), NT * c + t + 1)
                        hh = h[:, t, c * 512:(c + 1) * 512]
                        m = dve.tensor_tensor(hh, hh, ps[:, NT * c + t, :], ALU.add)
                        if c == 1:
                            m.then_inc(S("h_final"), 1)

            residual("outA", 1)

            def first_of_max(v, mx, oh):
                link(dve.tensor_reduce(mx, v, AX.X, ALU.max))
                link(dve.tensor_tensor(oh, v, mx.unsqueeze(2).broadcast_to([P, NT, 4]), ALU.is_ge))
                link(dve.tensor_tensor(oh, oh, prio.unsqueeze(1).broadcast_to([P, NT, 4]), ALU.mult))
                link(dve.tensor_reduce(stat[:, 60:64], oh, AX.X, ALU.max))
                link(dve.tensor_tensor(oh, oh, stat[:, 60:64].unsqueeze(2).broadcast_to([P, NT, 4]), ALU.is_ge))

            def moe(l):
                i = 2 * l + 1
                norm(i)
                for q in range(4):
                    dve.memset(prio[:, q:q + 1], float(4 - q))
                for e in range(NE):
                    dve.memset(ebase[:, e:e + 1], float(e * SEQ))
                    for b in range(NB - 1):
                        q = 3 * e + b
                        dve.memset(bt[:, q:q + 1], float((b + 1) * P))
                        dve.memset(id48[:, q:q + 1], float(NB * e + b + 1))
                        dve.memset(e48[:, q:q + 1], float(e))
                for q in range(OVMAX):
                    m = dve.memset(j8[:, q:q + 1], float(q + 1))
                link(m)
                evac_xT(i, [16 + 8 * l], [xT])
                dve.wait_ge(S("lg_turned"), l + 1)
                link(dve.tensor_copy(L, ps[:, 1, 0:80].rearrange("p (t c) -> p t c", t=NT)))
                Lg, Le = L[:, :, 0:4], L[:, :, 4:20].rearrange("p t (g e) -> p t g e", g=NG)
                first_of_max(Lg, stat[:, 40:44], ohg)
                dve.tensor_tensor(gd, Lg, stat[:, 40:44].unsqueeze(2).broadcast_to([P, NT, 4]), ALU.subtract)\
                    .then_inc(S("gd_ready"), 1)
                p4 = prod.rearrange("p (t g e) -> p t g e", t=NT, g=NG)
                link(dve.tensor_tensor(p4, Le, ohg.unsqueeze(3).broadcast_to([P, NT, NG, EG]), ALU.mult))
                link(dve.tensor_reduce(esel, prod.rearrange("p (t g e) -> p t e g", t=NT, g=NG), AX.X, ALU.add))
                first_of_max(esel, stat[:, 44:48], oh1)
                link(dve.scalar_tensor_tensor(out=tmp4, in0=oh1, scalar=-BIG, in1=esel, op0=ALU.mult, op1=ALU.add))
                first_of_max(tmp4, stat[:, 48:52], oh2)
                dve.tensor_tensor(stat[:, 52:56], stat[:, 48:52], stat[:, 44:48], ALU.subtract)\
                    .then_inc(S("gd_ready"), 1)
                for k, oh in enumerate((oh1, oh2)):
                    o4 = ohE[k].rearrange("p (t g e) -> p t g e", t=NT, g=NG)
                    link(dve.tensor_tensor(o4, ohg.unsqueeze(3).broadcast_to([P, NT, NG, EG]),
                                           oh.unsqueeze(2).broadcast_to([P, NT, NG, EG]), ALU.mult))
                dve.tensor_tensor(sel_bf, ohE[0], ohE[1], ALU.add).then_inc(S("sel_ready"), 1)
                dve.wait_ge(S("ge_ready"), 2 * l + 2)
                link(dve.tensor_reduce(stat[:, 64:68], ge, AX.X, ALU.add))
                link(dve.tensor_scalar(stat[:, 68:72], stat[:, 56:60], 1.0, None, ALU.add))
                link(dve.tensor_tensor(stat[:, 64:68], stat[:, 64:68], stat[:, 68:72], ALU.mult))
                link(dve.reciprocal(wts[:, 0, :], stat[:, 64:68]))
                link(dve.tensor_tensor(wts[:, 1, :], wts[:, 0, :], stat[:, 56:60], ALU.mult))
                dve.wait_ge(S("places"), l + 1)
                link(dve.tensor_tensor(posd.rearrange("p (t e) -> p t e", t=NT),
                                       ps[:, 2, 0:64].rearrange("p (t e) -> p t e", t=NT),
                                       ebase.unsqueeze(1).broadcast_to([P, NT, NE]), ALU.add))
                for k in range(2):
                    link(dve.tensor_tensor(prod, posd, ohE[k], ALU.mult))
                    link(dve.tensor_reduce(stat[:, 72:76], prod.rearrange("p (t e) -> p t e", t=NT), AX.X, ALU.add))
                    m = dve.tensor_copy(dst[:, k, :], stat[:, 72:76])
                    if k == 0:
                        link(m)
                m.then_inc(S("places_ready"), 1)
                link(dve.tensor_copy(cnt, ps[0:1, 3, 0:NE]))
                a3 = act48.rearrange("p (e b) -> p e b", b=NB - 1)
                link(dve.tensor_tensor(a3, cnt.unsqueeze(2).broadcast_to([1, NE, NB - 1]),
                                       bt.rearrange("p (e b) -> p e b", b=NB - 1), ALU.is_gt))
                link(dve.tensor_tensor_scan(cs48, ones_col[0:1, 0:1].broadcast_to([1, NOV]), act48, 0.0, ALU.mult,
                                            ALU.add))
                m3 = m384.rearrange("p (j q) -> p j q", j=OVMAX)
                q3 = q384.rearrange("p (j q) -> p j q", j=OVMAX)
                link(dve.tensor_tensor(m3, cs48.unsqueeze(1).broadcast_to([1, OVMAX, NOV]),
                                       j8.unsqueeze(2).broadcast_to([1, OVMAX, NOV]), ALU.is_equal))
                link(dve.tensor_tensor(m3, m3, act48.unsqueeze(1).broadcast_to([1, OVMAX, NOV]), ALU.mult))
                link(dve.memset(ovf, 0.0))
                link(dve.tensor_copy(ovf[:, 0:1], cs48[:, NOV - 1:NOV]))
                for src, o in ((id48, 8), (e48, 16)):
                    link(dve.tensor_tensor(q3, m3, src.unsqueeze(1).broadcast_to([1, OVMAX, NOV]), ALU.mult))
                    link(dve.tensor_reduce(ovf[:, o:o + 8], q3, AX.X, ALU.add))
                dve.tensor_copy(ov[:, :], ovf).then_inc(S("ov_ready"), 1)
                dve.wait_ge(S("lists_loaded"), 16 * (l + 1))
                dve.tensor_copy(lst_f, lst_i.bitcast(I32)).then_inc(S("lst_ready"), 1)
                dve.wait_ge(S("lst_turned"), l + 1)
                link(dve.tensor_copy(cfull, ps[:, 4, 0:NE * NB]))
                link(dve.tensor_copy(ydst[:, :], cfull))
                link(dve.tensor_scalar(cge, cfull, float(SEQ), -float(SEQ), ALU.is_ge, ALU.mult))
                link(dve.tensor_tensor(cge, cge, cfull, ALU.add))
                link(dve.tensor_scalar(cuse, cfull, float(2 * SEQ), None, ALU.is_lt))
                link(dve.tensor_tensor(cres, cge, cuse, ALU.mult))
                dve.tensor_copy(tok[:, :], cres).then_inc(S("tok_ready"), 1)

                def take_x(n, par):
                    dve.wait_ge(S(f"xg_turned{l}"), n + 1)
                    for c in range(2):
                        gk = gains[:, 16 + 8 * l + 4 * c:20 + 8 * l + 4 * c]
                        m = dve.tensor_tensor(xgT[:, par, 4 * c:4 * c + 4, :],
                                              ps[:, 2 + c, :].rearrange("p (k s) -> p k s", k=4),
                                              gk.unsqueeze(2).broadcast_to([P, 4, P]), ALU.mult)
                    m.then_inc(S(f"xgT_ready{l}"), 1)

                def hidden(n):
                    dve.wait_ge(S(f"up_done{l}"), n + 1)
                    dve.wait_ge(S(f"sg_ready{l}"), n + 1)
                    if not isinstance(n, int) or n:
                        dve.wait_ge(S(f"hn_turned{l}"), n)
                    dve.tensor_tensor(hn, sg, ps[:, 1, :], ALU.mult).then_inc(S(f"hn_ready{l}"), 1)

                def take_y(n, par, scattered):
                    dve.wait_ge(S(f"down_done{l}"), n + 1)
                    if scattered is not None:
                        dve.wait_ge(S(f"scattered{l}_{par}"), scattered)
                    dve.tensor_copy(yb[:, par, 512:1024], ps[:, 6, :]).then_inc(S(f"y_dve{l}"), 1)

                take_x(0, 0)

                def expert(n, par, scattered, more=True):
                    hidden(n)
                    if more:
                        take_x(n + 1, 1 - par)
                    take_y(n, par, scattered)

                expert(0, 0, None)
                expert(1, 1, None)
                with dve.Fori(1, NE // 2 - 1) as i2:
                    expert(2 * i2, 0, 16 * i2)
                    expert(2 * i2 + 1, 1, 16 * i2)
                expert(NE - 2, 0, 16 * (NE // 2 - 1))
                expert(NE - 1, 1, 16 * (NE // 2 - 1), False)
                n_ov = dve.value_load(ov[0:1, 0:1], min_val=0, max_val=OVMAX)
                with dve.If(n_ov > 0), dve.Fori(0, n_ov) as j:
                    dve.wait_ge(S(f"scattered{l}_0"), 16 * (j + NE // 2))
                    dve.wait_ge(S(f"pool_held{l}"), 3 * j + 1)
                    q = dve.value_load(ov[0:1, bass.ds(j + 8, 1)], min_val=0, max_val=NE * NB - 1)
                    dve.tensor_copy(fix[:, 0:1], tok[:, bass.ds(q, 1)])
                    dve.tensor_copy(fix[:, 1:2], ydst[:, bass.ds(q, 1)]).then_inc(S(f"fix_ready{l}"), 1)
                    take_x(j + NE, 0)
                    hidden(j + NE)
                    take_y(j + NE, 0, None)
                dve.wait_ge(S(f"scattered{l}_1"), NE // 2 * 16)
                dve.wait_ge(S(f"scattered{l}_0"), (n_ov + NE // 2) * 16)
                dve.tensor_copy(stat[:, 93:94], ones_col[:, :]).then_inc(S("tiles_stored"), 1)
                for t in range(NT):
                    dve.wait_ge(S("y_back"), 16 * (NT * l + t + 1))
                    for k in range(2):
                        m = dve.scalar_tensor_tensor(out=h[:, t, :], in0=yy[:, 2 * t + k, :], scalar=wts[:, k, t:t + 1],
                                                     in1=h[:, t, :], op0=ALU.mult, op1=ALU.add)
                        if k == 0:
                            link(m)
                    m.then_inc(S("h_final"), 1)

            moe(0)

            norm(2)
            evac_xT(2, [40, 8], [x2, xT])
            dve.wait_ge(S("fg_ready"), 1)
            link(dve.scalar_tensor_tensor(out=f_l, in0=f_z, scalar=0.0, in1=f_l, op0=ALU.min, op1=ALU.subtract))
            link(dve.tensor_tensor_scan(cT, ones_col[0:HB, 0:1].broadcast_to([HB, SEQ]), f_l, 0.0, ALU.mult,
                                        ALU.subtract))
            nk = 0
            for g, (w, c, i) in enumerate(B_GROUPS):
                if w == "fg":
                    continue
                if w == "v":
                    dve.wait_ge(S("projB"), g + 1)
                    dve.tensor_copy(vb[:, i, (c - 2) * 512:(c - 1) * 512], ps[:, g % 6, :]).then_inc(S("D_evacB"), 1)
                    continue
                dve.wait_ge(S("sq_ready"), nk + 1)
                dve.tensor_reduce(stat[:, 8:16], sq.rearrange("p (a b) -> p a b", a=8), AX.X, ALU.add)\
                    .then_inc(S("hss_ready"), 1)
                dve.wait_ge(S("hrms2_ready"), nk + 1)
                link(dve.reciprocal(stat[:, 24:32], stat[:, 16:24]))
                if nk >= 2:
                    dve.wait_ge(S("nat_turned"), nk - 1)
                dve.wait_ge(S("projB"), g + 1)
                dve.tensor_tensor(nat[:, nk % 2, :].rearrange("p (a b) -> p a b", a=8),
                                  ps[:, g % 6, :].rearrange("p (a b) -> p a b", a=8),
                                  stat[:, 24:32].unsqueeze(2).broadcast_to([P, 8, DH]), ALU.mult)\
                    .then_inc(S("D_evacB"), 1)
                nk += 1
            dve.wait_ge(S("nat_turned"), 16)

            steps = [(hd, j) for hd in range(HB) for j in range(NT)]

            def max_of(n):
                hd, j = steps[n]
                if j == 0:
                    dve.wait_ge(S("negc_ready"), hd + 1)
                    link(dve.tensor_tensor(negd.rearrange("p (a b) -> p a b", a=NT),
                                           negc[:, hd % 2, :].rearrange("p (a b) -> p a b", a=NT),
                                           mask_ts[:, :].unsqueeze(1).broadcast_to([P, NT, P]), ALU.add))
                dve.wait_ge(S("s_ready"), n + 1)
                if n >= 3:
                    dve.wait_ge(S("p_turned"), n - 2)
                a, b = 64 + n % 4, 68 + n % 4
                if j:
                    link(dve.tensor_tensor_reduce(pbuf[:, n % 3, 0:j * P], ps[:, n % 2, 0:j * P],
                                                  negc[:, hd % 2, 0:j * P], 1.0, -3e38, ALU.add, ALU.max,
                                                  stat[:, a:a + 1]))
                link(dve.tensor_tensor_reduce(pbuf[:, n % 3, j * P:(j + 1) * P], ps[:, n % 2, j * P:(j + 1) * P],
                                              negd[:, j * P:(j + 1) * P], 1.0,
                                              stat[:, a:a + 1] if j else -3e38, ALU.add, ALU.max, stat[:, b:b + 1]))
                dve.tensor_scalar(stat[:, 72 + n % 4:73 + n % 4], stat[:, b:b + 1], -1.0, None, ALU.mult)\
                    .then_inc(S("s_used"), 1)

            def normalise(n):
                hd, j = steps[n]
                dve.wait_ge(S("e_ready"), n + 1)
                link(dve.reciprocal(stat[:, 80 + n % 4:81 + n % 4], stat[:, 76 + n % 4:77 + n % 4]))
                pp = pbuf[:, n % 3, 0:(j + 1) * P]
                dve.tensor_scalar(pp, pp, stat[:, 80 + n % 4:81 + n % 4], None, ALU.mult).then_inc(S("p_ready"), 1)

            for n in range(len(steps) + 1):
                if n < len(steps):
                    max_of(n)
                if n:
                    normalise(n - 1)
                if n >= 12 and (n - 12) % 8 == 0 or n == len(steps):
                    r = (n - 12) // 8 if n < len(steps) else 7
                    if n == len(steps):
                        r = 7
                    dve.wait_ge(S("o_ready"), 8 * (r + 1))
                    dve.tensor_copy(x2[:, r, :], ps[:, 4 + r % 2, :]).then_inc(S("oT_ready"), 1)
            for q in range(8):
                dve.wait_ge(S("og_read"), q + 1)
                dve.tensor_tensor(x2[:, q, :], x2[:, q, :], sg_og[:, q % 2, :], ALU.mult).then_inc(S("oT_gated"), 1)
            residual("outB", 3)
            moe(1)
            dve.wait_ge(S("rms"), 5)
            link(dve.reciprocal(stat[:, 4:8], stat[:, 0:4]))
            dve.wait_ge(S("nf_loaded"), 16)
            for t in range(NT):
                dve.scalar_tensor_tensor(out=fo[:, t, :], in0=h[:, t, :], scalar=stat[:, 4 + t:5 + t], in1=nf,
                                         op0=ALU.mult, op1=ALU.mult).then_inc(S("final_rows"), 1)

        @block.scalar
        def _(act):
            chain = [0]

            def link(ins):
                chain[0] += 1
                ins.then_inc(S("act_step"), 1)
                act.wait_ge(S("act_step"), chain[0])

            act.wait_ge(S("zeroed"), 2)
            rl = S("rows_loaded")
            as8 = lambda v: v.rearrange("(k p) -> k p", p=P)
            n = 0
            for r, v in ((0, as8(norm_mix[0])), (8, as8(norm_mix[1])), (16, as8(norm_ffn[0])), (24, as8(norm_ffn[1])),
                         (32, as8(a_head_gain[0])), (40, as8(kv_norm))):
                act.dma_start(rows[r:r + 8, :], v).then_inc(rl, 16)
            one = lambda v: v.rearrange("(a n) -> a n", a=1)
            for r, c, v in ((48, 0, one(kv_k_gain)), (48, 64, one(kv_k_gain)), (49, 0, b_q_gain), (49, 64, b_q_gain),
                            (50, 0, a_b_gate[:, 0:HA]), (50, 32, a_b_gate[:, HA:2 * HA]), (51, 0, one(kv_b_f)),
                            (52, 0, moe_b_grp[0:1, :]), (52, 4, moe_b_exp[0:1, :]),
                            (53, 0, moe_b_grp[1:2, :]), (53, 4, moe_b_exp[1:2, :])):
                act.dma_start(rows[r:r + 1, c:c + v.shape[1]], v).then_inc(rl, 16)
            gw = a_w_in[0].rearrange("(k p) n -> p k n", p=P)[:, :, 3072:3080]
            act.dma_start(w_gates[:, :, 0:HA], gw[:, :, 0:HA]).then_inc(S("gates_w"), 16)
            act.dma_start(w_gates[:, :, 32:32 + HA], gw[:, :, HA:2 * HA]).then_inc(S("gates_w"), 16)
            act.dma_start(w_fg[:, :, :], wv["kv"][:, :, 2 * D:2 * D + HB]).then_inc(S("fg_w"), 16)
            for l in range(2):
                act.dma_start(w_rt[:, l, :, 0:NG], moe_w_grp[l].rearrange("(k p) n -> p k n", p=P))\
                    .then_inc(S("rt_w"), 16)
                act.dma_start(w_rt[:, l, :, NG:NG + NE], moe_w_exp[l].rearrange("(k p) n -> p k n", p=P))\
                    .then_inc(S("rt_w"), 16)

            def squares(i):
                for t in range(NT):
                    if i == 0:
                        act.wait_ge(S("x_loaded"), 16)
                        act.wait_ge(S("consts"), 1)
                    else:
                        act.wait_ge(S("h_final"), NT * (i - 1) + t + 1)
                    m = act.activation(junk[:, t, :], h[:, t, :], ACT.Square, accum_out=stat[:, 88 + t:89 + t])
                link(m)
                act.activation(stat[:, 0:4], stat[:, 88:92], ACT.Sqrt, scale=1.0 / D, bias=eps_col[:, :])\
                    .then_inc(S("rms"), 1)

            def evac_xT(i, cols, dests):
                for k in range(1, KD, 2):
                    act.wait_ge(S("xn_turned"), KD * i + k + 1)
                    for c, dd in zip(cols, dests):
                        m = act.activation(dd[:, k, :], ps[:, k, :], ACT.Copy, scale=gains[:, c + k:c + k + 1])
                    m.then_inc(S("xT_act"), 1)

            squares(0)
            act.wait_ge(S("gains_ready"), 1)
            evac_xT(0, [0], [xT])
            act.wait_ge(S("projA"), 1)
            act.activation(g_t, ps[0:36, 0, :], ACT.Tanh, scale=1.0 / CAP, bias=gate15[0:36, :])\
                .then_inc(S("A_evacA"), 1)
            act.wait_ge(S("A_evacA"), 1)
            link(act.activation(g_e, g_t[32:36, :], ACT.Exp, scale=-CAP))
            act.activation(g_lf, g_e, ACT.Ln, bias=ones_col[0:4, :]).then_inc(S("gates_ready"), 1)
            act.wait_ge(S("umn_ready"), 1)
            umn = arena[:, UMN:UMN + 144].rearrange("p (t c) -> p t c", t=NT)
            act.activation(stat[:, 32:48].rearrange("p (h t) -> p t h", h=HA), umn[:, :, 32:36], ACT.Exp, scale=-1.0)\
                .then_inc(S("em_ready"), 1)
            for hd in range(HA):
                act.wait_ge(S("m_spread_used"), hd + 1)
                for i in range(NT):
                    dd = dec[:, hd, DO[i]:DO[i] + DW[i]]
                    act.activation(dd, dd, ACT.Exp, scale=-1.0, bias=umn[:, i, hd:hd + 1])\
                        .then_inc(S("dec_ready"), 1)
            for g in range(17, 25):
                w, c, i = A_GROUPS[g]
                act.wait_ge(S("projA"), g + 1)
                act.activation(so[:, i, (c - 4) * 512:(c - 3) * 512], ps[:, g % 6, :], ACT.Sigmoid)\
                    .then_inc(S("A_evacA"), 1)
            for hd in range(HA):
                act.wait_ge(S("rden_ready"), hd + 1)
                for j in range(NT):
                    m = act.activation(sqa[:, j, :], ps[:, 4 + j, 0:DV], ACT.Square, scale=stat[:, 20 + j:21 + j],
                                       accum_out=stat[:, 84 + j:85 + j])
                link(m)
                act.activation(stat[:, 24:28], stat[:, 84:88], ACT.Sqrt, scale=1.0 / DV, bias=eps_col[:, :])\
                    .then_inc(S("hrms_ready"), 1)
            for k in range(1, KD, 2):
                act.wait_ge(S("hg_turned"), k + 1)
                act.activation(xT[:, k, :], ps[:, k, :], ACT.Copy, scale=gains[:, 32 + k:33 + k])\
                    .then_inc(S("hgT_act"), 1)

            def moe(l):
                i = 2 * l + 1
                squares(i)
                evac_xT(i, [16 + 8 * l], [xT])
                act.wait_ge(S("logits"), l + 1)
                act.activation(lgT, ps[0:20, 0, :], ACT.Identity, bias=gains[0:20, 52 + l:53 + l])\
                    .then_inc(S("lgT_ready"), 1)
                act.wait_ge(S("gd_ready"), 2 * l + 1)
                act.activation(ge, gd, ACT.Exp).then_inc(S("ge_ready"), 1)
                act.wait_ge(S("gd_ready"), 2 * l + 2)
                act.activation(stat[:, 56:60], stat[:, 52:56], ACT.Exp).then_inc(S("ge_ready"), 1)

                def expert(n, par, scattered):
                    act.wait_ge(S(f"gate_done{l}"), n + 1)
                    if not isinstance(n, int) or n:
                        act.wait_ge(S(f"hn_ready{l}"), n)
                    act.activation(sg, ps[:, 0, :], ACT.Silu).then_inc(S(f"sg_ready{l}"), 1)
                    act.wait_ge(S(f"hn_turned{l}"), n + 1)
                    if not isinstance(n, int) or n:
                        act.wait_ge(S(f"down_done{l}"), n)
                    act.activation(hT, ps[:, 4, :], ACT.Copy).then_inc(S(f"hT_ready{l}"), 1)
                    act.wait_ge(S(f"down_done{l}"), n + 1)
                    if scattered is not None:
                        act.wait_ge(S(f"scattered{l}_{par}"), scattered)
                    act.activation(yb[:, par, 0:512], ps[:, 5, :], ACT.Copy).then_inc(S(f"y_act{l}"), 1)

                expert(0, 0, None)
                expert(1, 1, None)
                with act.Fori(1, NE // 2) as i2:
                    expert(2 * i2, 0, 16 * i2)
                    expert(2 * i2 + 1, 1, 16 * i2)
                act.wait_ge(S("ov_ready"), l + 1)
                n_ov = act.value_load(ov[0:1, 0:1], min_val=0, max_val=OVMAX)
                with act.If(n_ov > 0), act.Fori(0, n_ov) as j:
                    expert(j + NE, 0, None)

            moe(0)

            squares(2)
            evac_xT(2, [40, 8], [x2, xT])
            act.wait_ge(S("projB"), 1)
            act.activation(f_z, ps[0:HB, 0, :], ACT.Identity, bias=gains[0:HB, 51:52]).then_inc(S("A_evacB"), 1)
            act.wait_ge(S("A_evacB"), 1)
            link(act.activation(f_a, f_z, ACT.Abs))
            link(act.activation(f_e, f_a, ACT.Exp, scale=-1.0))
            act.activation(f_l, f_e, ACT.Ln, bias=ones_col[0:HB, :]).then_inc(S("fg_ready"), 1)

            def take_heads(n):
                act.wait_ge(S("nat_turned"), n + 1)
                q = n >= 8
                c, i = (n % 8) // 4, n % 4
                dd = (qTb if q else kTb)[:, 4 * c:4 * c + 4, i * P:(i + 1) * P]
                act.activation(dd, ps[:, 6 + n % 2, :].rearrange("p (r t) -> p r t", r=4), ACT.Copy,
                               scale=qg_col if q else gains[:, 48:49]).then_inc(S("headsT_ready"), 1)

            qg_col = stat[:, 92:93]
            link(act.activation(qg_col, gains[:, 49:50], ACT.Copy, scale=DH ** -0.5))
            nk = 0
            for g, (w, c, i) in enumerate(B_GROUPS):
                if w in ("fg", "v"):
                    continue
                act.wait_ge(S("projB"), g + 1)
                if nk:
                    act.wait_ge(S("hss_ready"), nk)
                act.activation(sq, ps[:, g % 6, :], ACT.Square).then_inc(S("sq_ready"), 1)
                act.wait_ge(S("hss_ready"), nk + 1)
                act.activation(stat[:, 16:24], stat[:, 8:16], ACT.Sqrt, scale=1.0 / DH, bias=eps_col[:, :])\
                    .then_inc(S("hrms2_ready"), 1)
                nk += 1
                if nk > 2:
                    take_heads(nk - 3)
            take_heads(14)
            take_heads(15)

            steps = [(hd, j) for hd in range(HB) for j in range(NT)]

            def take_c(hd):
                act.wait_ge(S("c_spread"), hd + 1)
                if hd >= 2:
                    act.wait_ge(S("s_used"), NT * (hd - 1))
                act.activation(negc[:, hd % 2, :], ps[:, 6, :], ACT.Copy).then_inc(S("negc_ready"), 1)

            act.wait_ge(S("fg_ready"), 1)
            act.wait_ge(S("D_evacB"), EVAC["B"].count("D"))
            take_c(0)
            for n in range(len(steps) + 2):
                if n < len(steps):
                    hd, j = steps[n]
                    act.wait_ge(S("s_used"), n + 1)
                    pp = pbuf[:, n % 3, 0:(j + 1) * P]
                    act.activation(pp, pp, ACT.Exp, bias=stat[:, 72 + n % 4:73 + n % 4],
                                   accum_out=stat[:, 76 + n % 4:77 + n % 4]).then_inc(S("e_ready"), 1)
                    if n % NT == 2 and hd + 1 < HB:
                        take_c(hd + 1)
                if n >= 2:
                    hd, j = steps[n - 2]
                    act.wait_ge(S("p_turned"), n - 1)
                    if n >= 4:
                        act.wait_ge(S("o_ready"), n - 3)
                    act.activation(ptb[:, n % 2, 0:(j + 1) * P], ps[:, 2 + n % 2, 0:(j + 1) * P], ACT.Copy)\
                        .then_inc(S("pT_ready"), 1)
            for q in range(8):
                act.wait_ge(S("ogB"), q + 1)
                if q >= 2:
                    act.wait_ge(S("oT_gated"), q - 1)
                act.activation(sg_og[:, q % 2, :], ps[:, q % 4, :], ACT.Sigmoid).then_inc(S("og_read"), 1)
            moe(1)
            squares(4)


ROWS_DMAS = 17
ARENA = 18600
UMN = 17424
EVAC = {"A": ["A"] + ["D"] * 16 + ["A"] * 8, "B": ["A"] + ["D"] * 24}


_INS = ['x', 'norm_mix', 'norm_ffn', 'a_w_in', 'a_b_gate', 'a_head_gain', 'a_w_out', 'kv_norm', 'kv_w', 'kv_b_f',
        'kv_k_gain', 'b_w_in', 'b_q_gain', 'b_w_out', 'moe_w_grp', 'moe_b_grp', 'moe_w_exp', 'moe_b_exp',
        'moe_w_gate', 'moe_w_up', 'moe_w_down', 'norm_final']
_OUTS = [((1, SEQ, D), 'float32')]


def kernel(**inputs):
    import numpy as _np
    import concourse.bacc as _bacc
    from concourse import mybir as _mybir
    from concourse.bass_utils import run_bass_kernel_spmd as _run

    nc = _bacc.Bacc("TRN2", target_bir_lowering=False, num_devices=1)
    arrays, args = {}, []
    for name in _INS:
        a = _np.ascontiguousarray(inputs[name])
        arrays[f"in_{name}_dram"] = a
        args.append(nc.dram_tensor(f"in_{name}_dram", a.shape, _mybir.dt.from_np(a.dtype), kind="ExternalInput").ap())
    for i, (shape, dtype) in enumerate(_OUTS):
        dt = _mybir.dt.from_np(_np.dtype(dtype))
        args.append(nc.dram_tensor(f"out_{i}_dram", shape, dt, kind="ExternalOutput").ap())
    trunk(nc, *args)
    r = _run(nc, [arrays], core_ids=[0])
    return r.results[0]["out_0_dram"]
```

```python
from contextlib import ExitStack

import concourse.bass as bass
from concourse import mybir

P = 128
F32 = mybir.dt.float32
BF16 = mybir.dt.bfloat16
I32 = mybir.dt.int32
F32R = mybir.dt.float32r
ALU = mybir.AluOpType
ACT = mybir.ActivationFunctionType
AX = mybir.AxisListType

SEQ, D = 512, 1024
NT = SEQ // P
KD = D // P
EPS = 1e-6
HA, DQK, DV = 4, 128, 256
CAP = 15.0
HB, DH = 16, 64
NG, EG = 4, 4
NE = NG * EG
DE = 512
KE = DE // P
W = 512
KH = 4
PC = KH * W
RAW, SPLIT = 4, 3
BIG = 1e30
LISTS = NE * SEQ
NB = SEQ // P
NOV = NE * (NB - 1)
OVMAX = 8
NOCODE = 2 * LISTS


def plan_pieces():
    two = lambda w, l, i: [(w, l, i, 0), (w, l, i, 1)]
    mix_a = [q for c in range(6) for q in two("a_in", 0, c)] + [q for c in range(2) for q in two("a_out", 0, c)]
    mix_b = [q for w, n in (("kv", 4), ("b_in", 4), ("b_out", 2)) for c in range(n) for q in two(w, 0, c)]

    def moe(l):
        seq = two("gate", l, 0) + two("up", l, 0)
        for e in range(1, NE):
            seq += two("gate", l, e) + two("up", l, e) + two("down", l, e - 1)
        return seq + two("down", l, NE - 1)

    seq = mix_a + moe(0) + mix_b + moe(1)
    raw = [n % RAW for n in range(len(seq))]
    b0 = seq.index(("b_out", 0, 0, 0))
    raw[b0:b0 + 4] = [2, 3, 0, 1]
    return seq, raw


def trunk(nc, x, norm_mix, norm_ffn, a_w_in, a_b_gate, a_head_gain, a_w_out, kv_norm, kv_w, kv_b_f, kv_k_gain,
          b_w_in, b_q_gain, b_w_out, moe_w_grp, moe_b_grp, moe_w_exp, moe_b_exp, moe_w_gate, moe_w_up,
          moe_w_down, norm_final, out):
    seq, raw_slot = plan_pieces()
    pidx = {k: n for n, k in enumerate(seq)}
    nth = [raw_slot[:n].count(raw_slot[n]) for n in range(len(seq))]
    before = [max([m for m in range(n) if raw_slot[m] == raw_slot[n]], default=None) for n in range(len(seq))]

    xd = [nc.dram_tensor(f"normed_{l}", [SEQ, D], F32, kind="Internal").ap() for l in range(2)]
    codes_d = [nc.dram_tensor(f"lists_{l}", [LISTS, 1], I32, kind="Internal").ap() for l in range(2)]
    yd = [nc.dram_tensor(f"expert_out_{l}", [2 * SEQ, D], F32, kind="Internal").ap() for l in range(2)]

    with ExitStack() as ctx:
        def sb(name, shape, dt=F32):
            return ctx.enter_context(nc.sbuf_tensor(name, shape, dt))

        sems = {}

        def S(name):
            if name not in sems:
                sems[name] = ctx.enter_context(nc.semaphore(name))
            return sems[name]

        ps = ctx.enter_context(nc.psum_tensor("ps", [P, 8, 512], F32))
        h = sb("h", [P, NT, D])
        xr = sb("xr", [P, 2 * KD * SEQ], F32R)
        raw = sb("raw", [P, RAW, PC])
        wr = sb("wr", [P, SPLIT, 2, PC], F32R)
        ws = sb("ws", [P, 2, WSN], F32R)
        xh, xl = (xr[:, a * KD * SEQ:(a + 1) * KD * SEQ].rearrange("p (k t) -> p k t", k=KD) for a in range(2))
        xgr = [[xr[:, n * 2048 + a * 1024:n * 2048 + (a + 1) * 1024].rearrange("p (k s) -> p k s", k=KD)
                for a in range(2)] for n in range(2)]
        hr = [xr[:, 4096 + a * DE:4096 + (a + 1) * DE] for a in range(2)]
        arena = sb("arena", [P, ARENA])
        ident = sb("ident", [P, P])
        mask_ts = sb("mask_ts", [P, P])
        mask_st = sb("mask_st", [P, P])
        tri_bf = sb("tri_bf", [P, P], BF16)
        ones_bf = sb("ones_bf", [P, P], BF16)
        rows = sb("rows", [54, P])
        gains = sb("gains", [P, 54])
        gate15 = sb("gate15", [P, 1])
        eps_col = sb("eps_col", [P, 1])
        ones_col = sb("ones_col", [P, 1])
        held = sb("held", [P, 8])
        w_gates = sb("w_gates", [P, KD, 36])
        w_fg = sb("w_fg", [P, KD, HB])
        w_rt = sb("w_rt", [P, 2, KD, NG + NE])
        stat = sb("stat", [P, 96])
        place_codes = sb("place_codes", [P, 2, NT], I32)
        dst = sb("dst", [P, 2, NT], I32)
        tok = sb("tok", [P, NE * NB], I32)
        ydst = sb("ydst", [P, NE * NB], I32)
        fix = sb("fix", [P, 2], I32)
        ov = sb("ov", [1, 24], I32)
        wts = sb("wts", [P, 2, NT])

        top = [0]

        def cut(n, shape=None, parts=P, at=None):
            o = top[0] if at is None else at
            if at is None:
                top[0] = o + n
            assert o + n <= ARENA, o + n
            v = arena[0:parts, o:o + n]
            return v.rearrange(*shape[:1], **shape[1]) if shape else v

        top[0] = 0
        qT = cut(HA * SEQ, ("p (h t) -> p h t", dict(h=HA)))
        kT = cut(HA * SEQ, ("p (h t) -> p h t", dict(h=HA)))
        va = cut(NT * HA * (DV + 1), ("p (t h v) -> p t h v", dict(t=NT, h=HA)))
        so = cut(NT * D, ("p (t d) -> p t d", dict(t=NT)))
        dec = cut(HA * 1280, ("p (h c) -> p h c", dict(h=HA)))
        g_t = arena[0:36, 8208:8208 + 512]
        g_e = arena[0:4, 8208 + 512:8208 + 1024]
        g_lf = arena[0:4, 8208 + 1024:8208 + 1536]
        g_b = arena[0:4, 8208 + 1536:8208 + 2048]
        g_um = arena[0:36, 8208 + 2048:8208 + 2560]
        g_m = arena[0:4, 8208 + 2560:8208 + 3072]
        sqa = xr[:, 0:NT * DV].rearrange("p (t v) -> p t v", t=NT)
        stage = arena[:, 0:NT * D].rearrange("p (t d) -> p t d", t=NT)
        stage_b = arena[:, 4096:4096 + NT * D].rearrange("p (t d) -> p t d", t=NT)
        junk = arena[:, 8192:8192 + NT * D].rearrange("p (t d) -> p t d", t=NT)
        top[0] = 0
        kTb = cut(8 * SEQ, ("p (r t) -> p r t", dict(r=8)))
        qTb = cut(8 * SEQ, ("p (r t) -> p r t", dict(r=8)))
        vb = cut(NT * D, ("p (t d) -> p t d", dict(t=NT)))
        cT = cut(SEQ, parts=HB)
        p_at = top[0]
        pbuf = cut(3 * 512, ("p (n c) -> p n c", dict(n=3)))
        ptb = cut(2 * 512, ("p (n c) -> p n c", dict(n=2)))
        negc = cut(2 * 512, ("p (n c) -> p n c", dict(n=2)))
        negd = cut(512)
        negd2 = cut(512)
        nat = arena[:, p_at:p_at + 1024].rearrange("p (n c) -> p n c", n=2)
        sq = arena[:, p_at + 1024:p_at + 1536]
        f_z = arena[0:HB, p_at + 1536:p_at + 2048]
        f_a = arena[0:HB, p_at + 2048:p_at + 2560]
        f_e = arena[0:HB, p_at + 2560:p_at + 3072]
        f_l = arena[0:HB, p_at + 3072:p_at + 3584]
        og_t = [raw[:, c, :].rearrange("p (k t) -> p k t", k=4) for c in range(2)]
        xg = arena[:, 0:2048].rearrange("p (n d) -> p n d", n=2)
        yb = arena[:, 2048:4096].rearrange("p (n d) -> p n d", n=2)
        gain_bc = arena[:, 4096:4096 + D]
        sg = arena[:, 5120:5632]
        hn = arena[:, 5632:6144]
        yy = arena[:, 7680:7680 + 8192].rearrange("p (n d) -> p n d", n=8)
        ow = arena[:, 7680:7680 + 8192].rearrange("p (n c) -> p n c", n=4)
        r0 = 7680
        lgT = arena[0:NG + NE, r0:r0 + 512]
        rt = lambda o, n: arena[:, r0 + 512 + o:r0 + 512 + o + n]
        L = rt(0, NT * 20).rearrange("p (t c) -> p t c", t=NT)
        gd = rt(80, 16).rearrange("p (t g) -> p t g", t=NT)
        ge = rt(96, 16).rearrange("p (t g) -> p t g", t=NT)
        ohg = rt(112, 16).rearrange("p (t g) -> p t g", t=NT)
        tmp4 = rt(128, 16).rearrange("p (t g) -> p t g", t=NT)
        esel = rt(144, 16).rearrange("p (t g) -> p t g", t=NT)
        oh1 = rt(160, 16).rearrange("p (t g) -> p t g", t=NT)
        oh2 = rt(176, 16).rearrange("p (t g) -> p t g", t=NT)
        prod = rt(192, 64)
        ohE = [rt(256, 64), rt(320, 64)]
        posd = rt(384, 64)
        prio = rt(448, 4)
        ebase = rt(452, 16)
        lst_i = arena[0:NE * NB, r0 + 1100:r0 + 1228]
        lst_f = arena[0:NE * NB, r0 + 1228:r0 + 1356]
        cfull = rt(1000, 64)
        cge = rt(1064, 64)
        cuse = rt(1128, 64)
        cres = rt(1192, 64)
        sel_bf = arena[:, r0 + 1800:r0 + 1800 + 32].bitcast(BF16)
        cnt = arena[0:1, r0 + 1900:r0 + 1916]
        bt = arena[0:1, r0 + 1920:r0 + 1968]
        act48 = arena[0:1, r0 + 1968:r0 + 2016]
        cs48 = arena[0:1, r0 + 2016:r0 + 2064]
        id48 = arena[0:1, r0 + 2064:r0 + 2112]
        e48 = arena[0:1, r0 + 2112:r0 + 2160]
        j8 = arena[0:1, r0 + 2160:r0 + 2168]
        m384 = arena[0:1, r0 + 2200:r0 + 2584]
        q384 = arena[0:1, r0 + 2600:r0 + 2984]
        ovf = arena[0:1, r0 + 3000:r0 + 3024]
        nf = arena[:, 0:D]
        fo = arena[:, 4096:4096 + NT * D].rearrange("p (t d) -> p t d", t=NT)

        DW = [512, 384, 256, 128]
        DO = [0, 512, 896, 1152]

        block = ctx.enter_context(nc.Block())

        halves = lambda v: v.rearrange("(a k p) n -> a p k n", a=2, p=P)
        wv = {
            "a_in": halves(a_w_in[0]), "a_out": halves(a_w_out[0]), "kv": halves(kv_w), "b_in": halves(b_w_in[0]),
            "b_out": halves(b_w_out[0]),
            "gate": moe_w_gate.rearrange("l e (a k p) n -> l e a p k n", a=2, p=P),
            "up": moe_w_up.rearrange("l e (a k p) n -> l e a p k n", a=2, p=P),
            "down": moe_w_down.rearrange("l e (k p) (a n) -> l e a p k n", a=2, p=P),
        }

        def kn(flat):
            return flat.rearrange("p (k n) -> p k n", k=KH)

        def landed(n):
            return S(f"raw_in_slot{raw_slot[n]}"), 16 * (nth[n] + 1)

        release = {}
        A_GROUPS = [("gates", None, 0)] + [("q", 0, i) for i in range(4)] + [("k", 1, i) for i in range(4)] + \
            [(w, c, i) for w, cc in (("v", (2, 3)), ("o", (4, 5))) for c in cc for i in range(NT)]
        B_GROUPS = [("fg", None, 0)] + [(w, c, i) for w, cc in (("k", (0, 1)), ("v", (2, 3)), ("q", (4, 5)))
                                        for c in cc for i in range(NT)]
        chunks = [k[:3] for k in seq if k[0] not in ("gate", "up", "down") and k[3] == 0]
        for m, (w, l, c) in enumerate(chunks):
            release[pidx[(w, l, c, 0)]] = ("half_used", m + 1)
            last = {"a_in": ("projA", 4 * c + 5), "a_out": ("outA", NT * (c + 1)), "kv": ("projB", 4 * c + 5),
                    "b_in": ("projB", 4 * c + 21) if c < 2 else ("ogB", 4 * (c - 1)), "b_out": ("outB", NT * (c + 1))}
            release[pidx[(w, l, c, 1)]] = last[w]
        for l in range(2):
            for e in range(NE):
                for w in ("gate", "up", "down"):
                    for a in range(2):
                        release[pidx[(w, l, e, a)]] = (f"{w}{a}_done{l}", e + 1)

        TURN = [("gate", 0), ("gate", 1), ("up", 0), ("up", 1), ("down", 0), ("down", 1)]

        def part(eng, which, dst_, src, done, waits):
            for name, v in waits:
                eng.wait_ge(S(name), v)
            if which == 0:
                m = eng.activation(dst_[0], src, ACT.Copy)
            else:
                m = eng.tensor_tensor(dst_[1], src, dst_[0].bitcast(F32), ALU.subtract)
            m.then_inc(S(done), 1)

        def split(eng, which, p):
            if which == 0:
                waits = [release[p - SPLIT]] if p >= SPLIT else []
                eng.wait_ge(*landed(p))
            else:
                waits = [("hi_ready", p + 1)]
            part(eng, which, (wr[:, p % SPLIT, 0, :], wr[:, p % SPLIT, 1, :]), raw[:, raw_slot[p], :],
                 ("hi_ready", "lo_ready")[which], waits)

        def split_turn(eng, which, l, n, i, base, q):
            p = base + 12 * i
            if which == 0:
                (w, a), d = TURN[(q - SPLIT) % 6], (q - SPLIT) // 6
                v = n + d + 1 - (1 if w == "down" else 0)
                sem_, v0 = landed(base)
                eng.wait_ge(sem_, v0 + (12 // RAW) * 16 * i)
                waits = [(f"{w}{a}_done{l}", v)]
            else:
                waits = [("hi_ready", p + 1)]
            part(eng, which, (wr[:, base % SPLIT, 0, :], wr[:, base % SPLIT, 1, :]), raw[:, raw_slot[base], :],
                 ("hi_ready", "lo_ready")[which], waits)

        def split_further(eng, which, l, j, o):
            if which == 0:
                if o < 4:
                    waits = [(f"ov_first{l}", 64 * j + 64)]
                else:
                    waits = [(f"ov_down{l}", 32 * j + 32)]
                if o >= SPLIT:
                    w, a = TURN[o - SPLIT]
                    waits += [(f"{w}{a}_done{l}", j + NE + 1)]
            else:
                waits = [(f"ov_hi{l}", 6 * j + o + 1)]
            part(eng, which, (wr[:, o % SPLIT, 0, :], wr[:, o % SPLIT, 1, :]), ow[:, o % 4, :],
                 (f"ov_hi{l}", f"ov_lo{l}")[which], waits)

        def after_chunk(eng, which, w, l, c, last):
            p = pidx[(w, l, c, 0)] + SPLIT + last
            split(eng, which, p)

        def small(eng, which, flat, n):
            if which == 0:
                eng.activation(ws[:, 0, 0:n], flat, ACT.Copy).then_inc(S("ws_hi"), 1)
            else:
                eng.tensor_tensor(ws[:, 1, 0:n], flat, ws[:, 0, 0:n].bitcast(F32), ALU.subtract)\
                    .then_inc(S("ws_lo"), 1)

        @block.sync
        def _(sp):
            sp.dma_start(h[:, :, :], x[0].rearrange("(t p) d -> p t d", p=P)).then_inc(S("x_loaded"), 16)
            sp.wait_ge(S("x_loaded"), 16)

            def load(n):
                kind, l, i, a = seq[n]
                if before[n] is not None:
                    sp.wait_ge(S("lo_ready"), before[n] + 1)
                if kind == "b_out" and raw_slot[n] < 2 or n == pidx[("gate", 1, 0, 0)]:
                    sp.wait_ge(S("oT_ready"), 8)
                src = wv[kind][l, i, a] if kind in ("gate", "up", "down") else wv[kind][a, :, :, i * W:(i + 1) * W]
                sp.dma_start(kn(raw[:, raw_slot[n], :]), src).then_inc(landed(n)[0], 16)

            for n in range(pidx[("gate", 0, 2, 0)]):
                load(n)
            for l in range(2):
                n0 = pidx[("gate", l, 2, 0)]
                with sp.Fori(0, NE // 2 - 1) as i:
                    for q in range(12):
                        w, _, e, a = seq[n0 + q]
                        sp.wait_ge(S("lo_ready"), 12 * i + before[n0 + q] + 1)
                        sp.dma_start(kn(raw[:, raw_slot[n0 + q], :]), wv[w][l, 2 * i + e, a])\
                            .then_inc(landed(n0 + q)[0], 16)
                load(pidx[("down", l, NE - 1, 0)])
                load(pidx[("down", l, NE - 1, 1)])
                sp.wait_ge(S("ov_ready"), l + 1)
                n_ov = sp.value_load(ov[0:1, 0:1], min_val=0, max_val=OVMAX)
                with sp.If(n_ov > 0), sp.Fori(0, n_ov) as j:
                    sp.wait_ge(S(f"scattered{l}_0"), 16 * (j + NE // 2))
                    sp.wait_ge(S(f"scattered{l}_1"), NE // 2 * 16)
                    ex = sp.value_load(ov[0:1, bass.ds(j + 16, 1)], min_val=0, max_val=NE - 1)
                    for o, (w, a) in enumerate(TURN[:4]):
                        sp.dma_start(kn(ow[:, o, :]), wv[w][l, ex, a]).then_inc(S(f"ov_first{l}"), 16)
                    sp.wait_ge(S(f"ov_lo{l}"), 6 * j + 2)
                    for o, (w, a) in enumerate(TURN[4:]):
                        sp.dma_start(kn(ow[:, o, :]), wv[w][l, ex, a]).then_inc(S(f"ov_down{l}"), 16)
                if l == 0:
                    for n in range(pidx[("kv", 0, 0, 0)], pidx[("gate", 1, 2, 0)]):
                        load(n)
            for t in range(NT):
                sp.wait_ge(S("final_rows"), t + 1)
                sp.dma_start(out[0, t * P:(t + 1) * P, :], fo[:, t, :]).then_inc(S("stored"), 16)
            sp.wait_ge(S("stored"), 16 * NT)

        @block.gpsimd
        def _(pool):
            chain = [0]

            def link(ins):
                chain[0] += 1
                ins.then_inc(S("pool_step"), 1)
                pool.wait_ge(S("pool_step"), chain[0])

            pool.memset(ident[:, :], 0.0)
            pool.memset(mask_ts[:, :], 0.0)
            pool.memset(mask_st[:, :], 0.0)
            pool.memset(tri_bf[:, :], 1.0)
            pool.memset(ones_bf[:, :], 1.0)
            link(pool.memset(eps_col[:, :], EPS))
            pool.affine_select(out=ident[:, :], in_=ident[:, :], compare_op=ALU.not_equal, fill=1.0, base=0,
                               pattern=[[-1, P]], channel_multiplier=1)
            pool.affine_select(out=mask_ts[:, :], in_=mask_ts[:, :], compare_op=ALU.is_ge, fill=-BIG, base=0,
                               pattern=[[-1, P]], channel_multiplier=1)
            pool.affine_select(out=mask_st[:, :], in_=mask_st[:, :], compare_op=ALU.is_ge, fill=BIG, base=0,
                               pattern=[[1, P]], channel_multiplier=-1)
            pool.affine_select(out=tri_bf[:, :], in_=tri_bf[:, :], compare_op=ALU.is_gt, fill=0.0, base=0,
                               pattern=[[1, P]], channel_multiplier=-1)
            pool.iota(place_codes[:, :, :], pattern=[[SEQ, 2], [P, NT]], base=0, channel_multiplier=1)
            pool.iota(tok[:, :], pattern=[[0, NE * NB]], base=NOCODE, channel_multiplier=0)\
                .then_inc(S("consts"), 1)
            pool.wait_ge(S("consts"), 1)
            for l in range(2):
                pool.dma_start(codes_d[l].rearrange("(p c) a -> p (c a)", p=P), tok[:, :]).then_inc(S("lists_empty"), 16)
            for l in range(2):
                pool.wait_ge(S("num_used" if l == 0 else "oT_ready"), NT * HA if l == 0 else 8)
                pool.dma_start(gain_bc, norm_ffn[l:l + 1, :].broadcast_to([P, D])).then_inc(S("gain_bc"), 16)
                for t in range(NT):
                    pool.wait_ge(S("xn_ready"), NT * (2 * l + 1) + t + 1)
                    pool.dma_start(xd[l][t * P:(t + 1) * P, :], stage[:, t, :]).then_inc(S("rows_stored"), 16)
                pool.wait_ge(S("lists_empty"), 32)
                pool.wait_ge(S("places_ready"), l + 1)
                for k in range(2):
                    for t in range(NT):
                        pool.indirect_dma_start(codes_d[l], bass.IndirectOffsetOnAxis(ap=dst[:, k, t:t + 1], axis=0),
                                                place_codes[:, k, t:t + 1], None, bounds_check=LISTS - 1,
                                                oob_is_err=False).then_inc(S("codes_stored"), 16)
                pool.wait_ge(S("codes_stored"), 16 * 2 * NT * (l + 1))
                pool.dma_start(lst_i.bitcast(I32), codes_d[l].rearrange("(r c) a -> r (c a)", c=P))\
                    .then_inc(S("lists_loaded"), 16)
                pool.wait_ge(S("rows_stored"), 16 * NT * (l + 1))
                pool.wait_ge(S("tok_ready"), l + 1)

                def gather(idx, par):
                    pool.indirect_dma_start(xg[:, par, :], None, xd[l], bass.IndirectOffsetOnAxis(ap=idx, axis=0),
                                            bounds_check=SEQ - 1, oob_is_err=False).then_inc(S(f"gathered{l}_{par}"), 16)

                def scatter(idx, par):
                    pool.indirect_dma_start(yd[l], bass.IndirectOffsetOnAxis(ap=idx, axis=0), yb[:, par, :], None,
                                            bounds_check=2 * SEQ - 1, oob_is_err=False)\
                        .then_inc(S(f"scattered{l}_{par}"), 16)

                gather(tok[:, 0:1], 0)
                gather(tok[:, NB:NB + 1], 1)
                for e in range(NE):
                    if e + 2 < NE:
                        pool.wait_ge(S(f"xg_turned{l}"), e + 1)
                        gather(tok[:, NB * (e + 2):NB * (e + 2) + 1], e % 2)
                    pool.wait_ge(S(f"y0_ready{l}"), e + 1)
                    pool.wait_ge(S(f"y1_ready{l}"), e + 1)
                    scatter(ydst[:, NB * e:NB * e + 1], e % 2)
                n_ov = pool.value_load(ov[0:1, 0:1], min_val=0, max_val=OVMAX)

                def hold(q):
                    pool.tensor_tensor(held[:, 4 * l + q:4 * l + q + 1], ones_col[:, :], ones_col[:, :], ALU.mult)\
                        .then_inc(S(f"pool_held{l}"), 1)

                hold(3)
                with pool.If(n_ov > 0), pool.Fori(0, n_ov) as j:
                    pool.wait_ge(S(f"fix_ready{l}"), j + 1)
                    hold(0)
                    gather(fix[:, 0:1], 0)
                    pool.wait_ge(S(f"y0_ready{l}"), j + NE + 1)
                    hold(1)
                    pool.wait_ge(S(f"y1_ready{l}"), j + NE + 1)
                    hold(2)
                    scatter(fix[:, 1:2], 0)
                pool.wait_ge(S("tiles_stored"), l + 1)
                for t in range(NT):
                    pool.dma_start(yy[:, 2 * t:2 * t + 2, :],
                                   yd[l].rearrange("(k t p) d -> t p k d", k=2, p=P)[t]).then_inc(S(f"y_back{t}"), 16)
            pool.wait_ge(S("h_final"), NT * 4)
            pool.dma_start(nf, norm_final.rearrange("(a d) -> a d", a=1).broadcast_to([P, D]))\
                .then_inc(S("nf_loaded"), 16)
            pool.wait_ge(S("nf_loaded"), 16)

        @block.tensor
        def _(pe):
            pe.wait_ge(S("consts"), 1)
            pe.wait_ge(S("zeroed"), 3)
            pe.wait_ge(S("rows_loaded"), 16 * ROWS_DMAS)
            pe.transpose(ps[:, 0, 0:54], rows[:, :], ident[0:54, 0:54]).then_inc(S("gains_turned"), 1)

            def turn_normed(j, src, waits=True):
                for t in range(NT):
                    if waits:
                        pe.wait_ge(S("xn_ready"), NT * waits_at[j] + t + 1)
                    for k in range(KD):
                        m = pe.transpose(ps[:, k, t * P:(t + 1) * P], src[:, t, k * P:(k + 1) * P], ident[:, :])
                        if t == NT - 1:
                            m.then_inc(S("xn_turned"), 1)

            waits_at = [0, 1, 2, 2, 3]

            def mm3(outp, a, b, start, stop):
                pe.matmul(outp, a[0], b[0], start=start, stop=False)
                pe.matmul(outp, a[0], b[1], start=False, stop=False)
                return pe.matmul(outp, a[1], b[0], start=False, stop=stop)

            def xr_at(k, cols=slice(0, SEQ)):
                return xh[:, k, cols], xl[:, k, cols]

            def small_group(which, width, outp, done, j):
                pe.wait_ge(S("ws_lo"), which + 1)
                for k in range(KD):
                    pe.wait_ge(S("xT_lo"), KD * j + k + 1)
                    m = mm3(outp, (ws[:, 0, width * k:width * k + P], ws[:, 1, width * k:width * k + P]), xr_at(k),
                            k == 0, k == KD - 1)
                m.then_inc(S(done), 1)

            def piece(n):
                pe.wait_ge(S("lo_ready"), n + 1)
                return kn(wr[:, n % SPLIT, 0, :]), kn(wr[:, n % SPLIT, 1, :])

            def chunk(w, c, outs, weight_first, done, before_bank=None, before_k=None, after=None):
                n = pidx[(w, 0, c, 0)]
                for a in range(2):
                    wp = piece(n + a)
                    for i in range(4):
                        if a == 0 and before_bank:
                            before_bank(i)
                        for kk in range(KH):
                            k = KH * a + kk
                            if before_k and i == 0:
                                before_k(k)
                            if weight_first:
                                cols = slice(i * P, (i + 1) * P)
                                m = mm3(outs[i], (wp[0][:, kk, cols], wp[1][:, kk, cols]), xr_at(k),
                                        k == 0, k == KD - 1)
                            else:
                                m = mm3(outs[i], xr_at(k, slice(i * P, (i + 1) * P)), (wp[0][:, kk, :], wp[1][:, kk, :]),
                                        k == 0, k == KD - 1)
                        if a == 0 and i == 3:
                            m.then_inc(S("half_used"), 1)
                        if a == 1:
                            m.then_inc(S(done), 1)
                            if after:
                                after(i)

            def bank_free(g, mixer):
                if g >= 6:
                    eng = EVAC[mixer][g - 6]
                    pe.wait_ge(S(f"{eng}_evac{mixer}"), EVAC[mixer][:g - 5].count(eng))

            pe.wait_ge(S("gains_ready"), 1)
            turn_normed(0, stage)
            small_group(0, 36, ps[:, 0, :], "projA", 0)

            def between_a(g):
                if g == 12:
                    pe.wait_ge(S("um_ready"), 1)
                    for t in range(NT):
                        m = pe.transpose(ps[:, 6, t * 36:(t + 1) * 36], g_um[:, t * P:(t + 1) * P], ident[0:36, 0:36])
                    m.then_inc(S("um_turned"), 1)
                if 13 <= g < 13 + HA:
                    if g > 13:
                        pe.wait_ge(S("m_spread_used"), g - 13)
                    pe.matmul(ps[:, 7, :], ident[0:4, g - 13:g - 12].broadcast_to([4, P]), g_m,
                              start=True, stop=True).then_inc(S("m_spread"), 1)

            for c in range(6):
                g0 = 4 * c + 1
                chunk("a_in", c, [ps[:, (g0 + i) % 6, :] for i in range(4)], c < 2, "projA",
                      before_bank=lambda i: bank_free(g0 + i, "A"), after=lambda i: between_a(g0 + i))
            pe.wait_ge(S("D_evacA"), EVAC["A"].count("D"))
            pe.wait_ge(S("A_evacA"), EVAC["A"].count("A"))

            def scores_a(hd):
                for i in range(NT):
                    if hd:
                        pe.wait_ge(S("pt_ready"), NT * (hd - 1) + i + 1)
                    pe.matmul(ps[:, i, 0:DW[i]], kT[:, hd, i * P:(i + 1) * P], qT[:, hd, i * P:], start=True,
                              stop=True).then_inc(S("st_ready"), 1)

            pe.wait_ge(S("m_spread_used"), HA)
            scores_a(0)
            for hd in range(HA):
                if hd + 1 < HA:
                    scores_a(hd + 1)
                pe.wait_ge(S("pt_ready"), NT * (hd + 1))
                for j in range(NT):
                    if hd:
                        pe.wait_ge(S("num_used"), NT * (hd - 1) + j + 1)
                    for i in range(j + 1):
                        o = DO[i] + (j - i) * P
                        m = pe.matmul(ps[:, 4 + j, 0:DV + 1], dec[:, hd, o:o + P], va[:, i, hd, :],
                                      start=(i == 0), stop=(i == j))
                    m.then_inc(S("num_ready"), 1)
            pe.wait_ge(S("num_used"), NT * HA)
            for k in range(KD):
                for t in range(NT):
                    m = pe.transpose(ps[:, k, t * P:(t + 1) * P], so[:, t, k * P:(k + 1) * P], ident[:, :])
                m.then_inc(S("hg_turned"), 1)

            def out_proj(w, done, x_there):
                for c in range(2):
                    chunk(w, c, [ps[:, NT * c + t, :] for t in range(NT)], False, done,
                          before_k=x_there if c == 0 else None)

            out_proj("a_out", "outA", lambda k: pe.wait_ge(S("hgT_lo"), k + 1))

            def moe(l):
                i = 2 * l + 1
                pe.wait_ge(S("h_final"), NT * i)
                turn_normed(1 + 3 * l, stage)
                small_group(1 + 2 * l, NG + NE, ps[:, 0, :], "logits", 1 + 3 * l)
                pe.wait_ge(S("lgT_ready"), l + 1)
                for t in range(NT):
                    m = pe.transpose(ps[:, 1, t * 20:(t + 1) * 20], lgT[:, t * P:(t + 1) * P], ident[0:20, 0:20])
                m.then_inc(S("lg_turned"), 1)
                pe.wait_ge(S("sel_ready"), l + 1)
                selv = sel_bf.rearrange("p (t e) -> p t e", t=NT)
                for t in range(NT):
                    for s in range(t + 1):
                        pe.matmul(ps[:, 2, t * NE:(t + 1) * NE], tri_bf[:, :] if s == t else ones_bf[:, :],
                                  selv[:, s, :], start=(s == 0), stop=(s == t))
                for t in range(NT):
                    m = pe.matmul(ps[0:1, 3, 0:NE], ones_bf[:, 0:1], selv[:, t, :], start=(t == 0), stop=(t == NT - 1))
                m.then_inc(S("places"), 1)
                pe.wait_ge(S("lst_ready"), l + 1)
                pe.transpose(ps[:, 4, 0:NE * NB], lst_f, ident[0:NE * NB, 0:NE * NB]).then_inc(S("lst_turned"), 1)
                pe.wait_ge(S("tok_ready"), l + 1)
                def turn_x(n, nth_of_buffer, par):
                    pe.wait_ge(S(f"gathered{l}_{par}"), 16 * (nth_of_buffer + 1))
                    if not isinstance(n, int) or n:
                        pe.wait_ge(S(f"xg_lo{l}"), n)
                    for k in range(KD):
                        m = pe.transpose(ps[:, 2 + k // 4, (k % 4) * P:(k % 4 + 1) * P],
                                         xg[:, par, k * P:(k + 1) * P], ident[:, :])
                    m.then_inc(S(f"xg_turned{l}"), 1)

                def gate_up(n, par, wait_piece, slot0):
                    past = not isinstance(n, int) or n
                    pe.wait_ge(S(f"xg_lo{l}"), n + 1)
                    for q, (w, a) in enumerate(TURN[:4]):
                        if past and a == 0:
                            pe.wait_ge(S(f"{('sg', 'hn')[q // 2]}_ready{l}"), n)
                        wait_piece(q)
                        wp = [kn(wr[:, (slot0 + q) % SPLIT, b, :]) for b in range(2)]
                        for kk in range(KH):
                            k = KH * a + kk
                            m = mm3(ps[:, q // 2, :], (xgr[par][0][:, k, :], xgr[par][1][:, k, :]),
                                    (wp[0][:, kk, :], wp[1][:, kk, :]), k == 0, k == KD - 1)
                        m.then_inc(S(f"{w}{a}_done{l}"), 1)

                def turn_h(n):
                    pe.wait_ge(S(f"hn_ready{l}"), n + 1)
                    if not isinstance(n, int) or n:
                        pe.wait_ge(S(f"h_lo{l}"), n)
                    for k in range(KE):
                        m = pe.transpose(ps[:, 4, k * P:(k + 1) * P], hn[:, k * P:(k + 1) * P], ident[:, :])
                    m.then_inc(S(f"hn_turned{l}"), 1)

                def down(n, wait_piece, slot0):
                    pe.wait_ge(S(f"h_lo{l}"), n + 1)
                    for a in range(2):
                        if not isinstance(n, int) or n:
                            pe.wait_ge(S(f"y{a}_ready{l}"), n)
                        wait_piece(4 + a)
                        wp = [kn(wr[:, (slot0 + a) % SPLIT, b, :]) for b in range(2)]
                        for k in range(KE):
                            m = mm3(ps[:, 5 + a, :], (hr[0][:, k * P:(k + 1) * P], hr[1][:, k * P:(k + 1) * P]),
                                    (wp[0][:, k, :], wp[1][:, k, :]), k == 0, k == KE - 1)
                        m.then_inc(S(f"down{a}_done{l}"), 1)

                turn_x(0, 0, 0)
                p0 = pidx[("gate", l, 0, 0)]
                gate_up(0, 0, lambda q: pe.wait_ge(S("lo_ready"), p0 + q + 1), p0)
                turn_x(1, 0, 1)
                turn_h(0)

                def turn(n, i, par, more=True):
                    base = pidx[("gate", l, par, 0)] if par else pidx[("gate", l, 2, 0)] - 12
                    there = lambda q: pe.wait_ge(S("lo_ready"), 12 * i + base + q + 1)
                    gate_up(n, par, there, base)
                    if more:
                        turn_x(n + 1, i + par, 1 - par)
                    down(n - 1, there, base + 4)
                    turn_h(n)

                turn(1, 0, 1)
                with pe.Fori(1, NE // 2 - 1) as i:
                    turn(2 * i, i, 0)
                    turn(2 * i + 1, i, 1)
                turn(NE - 2, NE // 2 - 1, 0)
                turn(NE - 1, NE // 2 - 1, 1, False)
                pl = pidx[("down", l, NE - 1, 0)]
                down(NE - 1, lambda q: pe.wait_ge(S("lo_ready"), pl + q - 4 + 1), pl)
                pe.wait_ge(S("ov_ready"), l + 1)
                n_ov = pe.value_load(ov[0:1, 0:1], min_val=0, max_val=OVMAX)
                with pe.If(n_ov > 0), pe.Fori(0, n_ov) as j:
                    turn_x(j + NE, j + NE // 2, 0)
                    there = lambda q: pe.wait_ge(S(f"ov_lo{l}"), 6 * j + q + 1)
                    gate_up(j + NE, 0, there, 0)
                    turn_h(j + NE)
                    down(j + NE, there, 4)

            moe(0)

            turn_normed(2, stage_b)
            small_group(2, HB, ps[:, 0, :], "projB", 2)

            def turn_nat(n):
                pe.wait_ge(S("D_evacB"), n + 1 if n < 8 else n + 9)
                if n >= 2:
                    pe.wait_ge(S("headsT_ready"), n - 1)
                for r in range(4):
                    m = pe.transpose(ps[:, 6 + n % 2, r * P:(r + 1) * P], nat[:, n % 2, r * P:(r + 1) * P], ident[:, :])
                m.then_inc(S("nat_turned"), 1)

            pend = []

            def between_b(g):
                w, c, i = B_GROUPS[g]
                if pend and pend[0][0] + 2 <= g:
                    turn_nat(pend.pop(0)[1])
                if w in "kq":
                    pend.append((g, (0 if w == "k" else 8) + (c % 4) * 4 + i))

            for c in range(4):
                g0 = 4 * c + 1
                chunk("kv", c, [ps[:, (g0 + i) % 6, :] for i in range(4)], False, "projB",
                      before_bank=lambda i: bank_free(g0 + i, "B"), after=lambda i: between_b(g0 + i))
            pe.wait_ge(S("D_evacB"), 16)
            pe.wait_ge(S("headsT_ready"), 8)
            turn_normed(3, stage_b, waits=False)
            for c in range(2):
                g0 = 4 * c + 17
                chunk("b_in", c, [ps[:, (g0 + i) % 6, :] for i in range(4)], False, "projB",
                      before_bank=lambda i: bank_free(g0 + i, "B"),
                      before_k=(lambda k: pe.wait_ge(S("xT_lo"), KD * 4)) if c == 0 else None,
                      after=lambda i: between_b(g0 + i))
            for _, n in pend:
                turn_nat(n)
            for c in range(2):
                chunk("b_in", 2 + c, [ps[:, i, :] for i in range(4)], True, "ogB",
                      before_bank=(lambda i: pe.wait_ge(S("D_evacB"), 24)) if c == 0 else
                      (lambda i: pe.wait_ge(S("og_ready"), i + 1)))
            pe.wait_ge(S("og_ready"), 8)
            pe.wait_ge(S("headsT_ready"), 16)
            pe.wait_ge(S("D_evacB"), EVAC["B"].count("D"))

            def spread_c(hd):
                if hd:
                    pe.wait_ge(S("negc_ready"), hd)
                pe.matmul(ps[:, 6, :], ident[0:HB, hd:hd + 1].broadcast_to([HB, P]), cT, start=True, stop=True)\
                    .then_inc(S("c_spread"), 1)

            steps = [(hd, j) for hd in range(HB) for j in range(NT)]

            def score(n):
                hd, j = steps[n]
                o, r = 64 * (hd % 2), hd // 2
                if n >= 2:
                    pe.wait_ge(S("s_used"), n - 1)
                pe.matmul(ps[:, n % 2, 0:(j + 1) * P], qTb[o:o + DH, r, j * P:(j + 1) * P],
                          kTb[o:o + DH, r, 0:(j + 1) * P], start=True, stop=True).then_inc(S("s_ready"), 1)

            def turn_p(n):
                hd, j = steps[n]
                pe.wait_ge(S("p_ready"), n + 1)
                if n >= 2:
                    pe.wait_ge(S("pT_ready"), n - 1)
                for i in range(j + 1):
                    m = pe.transpose(ps[:, 2 + n % 2, i * P:(i + 1) * P], pbuf[:, n % 3, i * P:(i + 1) * P], ident[:, :])
                m.then_inc(S("p_turned"), 1)

            def attend(n):
                hd, j = steps[n]
                o, r = 64 * (hd % 2), hd // 2
                pe.wait_ge(S("pT_ready"), n + 1)
                if hd % 2 == 0 and j == 0 and r >= 2:
                    pe.wait_ge(S("oT_ready"), r - 1)
                for i in range(j + 1):
                    m = pe.matmul(ps[o:o + DH, 4 + r % 2, j * P:(j + 1) * P], vb[:, i, hd * DH:(hd + 1) * DH],
                                  ptb[:, n % 2, i * P:(i + 1) * P], start=(i == 0), stop=(i == j))
                m.then_inc(S("o_ready"), 1)

            spread_c(0)
            for n in range(len(steps) + 3):
                if n < len(steps):
                    if n % NT == 2 and n // NT + 1 < HB:
                        spread_c(n // NT + 1)
                    score(n)
                if 0 <= n - 2 < len(steps):
                    turn_p(n - 2)
                if n >= 3:
                    attend(n - 3)
            out_proj("b_out", "outB", lambda k: pe.wait_ge(S("oT_lo"), k + 1))
            moe(1)

        @block.vector
        def _(dve):
            chain = [0]

            def link(ins):
                chain[0] += 1
                ins.then_inc(S("dve_step"), 1)
                dve.wait_ge(S("dve_step"), chain[0])

            dve.memset(rows[:, :], 0.0).then_inc(S("zeroed"), 1)
            dve.memset(w_gates[:, :, :], 0.0).then_inc(S("zeroed"), 1)
            dve.memset(ones_col[:, :], 1.0)
            dve.memset(ws[:, :, :].bitcast(F32), 0.0).then_inc(S("zeroed"), 1)
            dve.wait_ge(S("gains_turned"), 1)
            link(dve.tensor_copy(gains[:, :], ps[:, 0, 0:54]))
            link(dve.tensor_scalar(gate15[:, :], gains[:, 50:51], 1.0 / CAP, None, ALU.mult))
            dve.tensor_copy(stat[:, 95:96], gate15[:, :]).then_inc(S("gains_ready"), 1)

            def norm(i, rows_, gained=False):
                dve.wait_ge(S("rms"), i + 1)
                link(dve.reciprocal(stat[:, 4:8], stat[:, 0:4]))
                if gained:
                    dve.wait_ge(S("gain_bc"), 16 * (i + 1) // 2)
                for t in range(NT):
                    if gained:
                        m = dve.scalar_tensor_tensor(out=rows_[:, t, :], in0=h[:, t, :], scalar=stat[:, 4 + t:5 + t],
                                                     in1=gain_bc, op0=ALU.mult, op1=ALU.mult)
                    else:
                        m = dve.tensor_scalar(rows_[:, t, :], h[:, t, :], stat[:, 4 + t:5 + t], None, ALU.mult)
                    m.then_inc(S("xn_ready"), 1)

            def low_xT(j, col):
                for k in range(KD):
                    dve.wait_ge(S("xT_hi"), KD * j + k + 1)
                    hi = xh[:, k, :].bitcast(F32)
                    if col is None:
                        m = dve.tensor_tensor(xl[:, k, :], ps[:, k, :], hi, ALU.subtract)
                    else:
                        m = dve.scalar_tensor_tensor(out=xl[:, k, :], in0=ps[:, k, :],
                                                     scalar=gains[:, col + k:col + k + 1], in1=hi, op0=ALU.mult,
                                                     op1=ALU.subtract)
                    m.then_inc(S("xT_lo"), 1)

            norm(0, stage)
            dve.wait_ge(S("ws_hi"), 1)
            small(dve, 1, w_gates[:, :, :].rearrange("p k n -> p (k n)"), KD * 36)
            low_xT(0, 0)
            for p in range(SPLIT):
                split(dve, 1, p)
            for t in range(NT):
                m = dve.memset(va[:, t, :, DV:DV + 1], 1.0)
            link(m)
            link(dve.memset(g_um, 0.0))

            def evac_a(g):
                w, c, i = A_GROUPS[g]
                dve.wait_ge(S("projA"), g + 1)
                if w == "q":
                    m = dve.tensor_copy(qT[:, i, :], ps[:, g % 6, :])
                elif w == "k":
                    m = dve.tensor_scalar(kT[:, i, :], ps[:, g % 6, :], DQK ** -0.5, None, ALU.mult)
                else:
                    m = dve.tensor_copy(va[:, i, 2 * (c - 2):2 * (c - 2) + 2, 0:DV],
                                        ps[:, g % 6, :].rearrange("p (h v) -> p h v", h=2))
                m.then_inc(S("D_evacA"), 1)

            def chunk_a(c):
                after_chunk(dve, 1, "a_in", 0, c, 0)
                for g in range(4 * c + 1, 4 * c + 5):
                    evac_a(g)
                after_chunk(dve, 1, "a_in", 0, c, 1)

            chunk_a(0)
            dve.wait_ge(S("gates_ready"), 1)
            one4 = ones_col[0:4, 0:1].broadcast_to([4, SEQ])
            link(dve.tensor_tensor_scan(g_b, one4, g_lf, 0.0, ALU.mult, ALU.subtract))
            link(dve.scalar_tensor_tensor(out=g_um[0:4, :], in0=g_t[0:4, :], scalar=CAP, in1=g_b, op0=ALU.mult,
                                          op1=ALU.subtract))
            link(dve.tensor_tensor_scan(g_m, g_um[0:4, :], g_um[0:4, :], 0.0, ALU.max, ALU.max))
            dve.tensor_tensor(g_um[32:36, :], g_b, g_m, ALU.add).then_inc(S("um_ready"), 1)
            dve.wait_ge(S("ws_hi"), 2)
            small(dve, 1, w_rt[:, 0, :, :].rearrange("p k n -> p (k n)"), KD * (NG + NE))
            chunk_a(1)
            chunk_a(2)
            dve.wait_ge(S("um_turned"), 1)
            umn = arena[:, UMN:UMN + 144].rearrange("p (t c) -> p t c", t=NT)
            dve.tensor_copy(arena[:, UMN:UMN + 144], ps[:, 6, 0:144]).then_inc(S("umn_ready"), 1)
            after_chunk(dve, 1, "a_in", 0, 3, 0)
            for hd in range(HA):
                evac_a(13 + hd)
                dve.wait_ge(S("m_spread"), hd + 1)
                for i in range(NT):
                    if i < NT - 1:
                        dve.tensor_copy(dec[:, hd, DO[i] + P:DO[i] + DW[i]], ps[:, 7, (i + 1) * P:])
                    m = dve.tensor_tensor(dec[:, hd, DO[i]:DO[i] + P], ps[:, 7, i * P:(i + 1) * P], mask_st[:, :],
                                          ALU.add)
                m.then_inc(S("m_spread_used"), 1)
            after_chunk(dve, 1, "a_in", 0, 3, 1)
            for c in (4, 5):
                after_chunk(dve, 1, "a_in", 0, c, 0)
                after_chunk(dve, 1, "a_in", 0, c, 1)

            def weigh(hd):
                dve.wait_ge(S("dec_ready"), NT * (hd + 1))
                for i in range(NT):
                    dve.wait_ge(S("st_ready"), NT * hd + i + 1)
                    dd = dec[:, hd, DO[i]:DO[i] + DW[i]]
                    dve.tensor_tensor(dd, ps[:, i, 0:DW[i]], dd, ALU.mult).then_inc(S("pt_ready"), 1)

            weigh(0)
            for hd in range(HA):
                if hd + 1 < HA:
                    weigh(hd + 1)
                dve.wait_ge(S("num_ready"), NT * (hd + 1))
                dve.wait_ge(S("em_ready"), 1)
                link(dve.tensor_copy(stat[:, 8:12], ps[:, 4:8, DV]))
                link(dve.scalar_tensor_tensor(out=stat[:, 12:16], in0=stat[:, 8:12], scalar=-1.0, in1=stat[:, 8:12],
                                              op0=ALU.mult, op1=ALU.max))
                link(dve.tensor_tensor(stat[:, 16:20], stat[:, 12:16], stat[:, 32 + 4 * hd:36 + 4 * hd], ALU.max))
                dve.reciprocal(stat[:, 20:24], stat[:, 16:20]).then_inc(S("rden_ready"), 1)
                dve.wait_ge(S("hrms_ready"), hd + 1)
                link(dve.reciprocal(stat[:, 28:32], stat[:, 24:28]))
                link(dve.tensor_tensor(stat[:, 28:32], stat[:, 28:32], stat[:, 20:24], ALU.mult))
                for j in range(NT):
                    s = so[:, j, hd * DV:(hd + 1) * DV]
                    dve.scalar_tensor_tensor(out=s, in0=ps[:, 4 + j, 0:DV], scalar=stat[:, 28 + j:29 + j], in1=s,
                                             op0=ALU.mult, op1=ALU.mult).then_inc(S("num_used"), 1)
            for k in range(KD):
                dve.wait_ge(S("hgT_hi"), k + 1)
                dve.scalar_tensor_tensor(out=xl[:, k, :], in0=ps[:, k, :], scalar=gains[:, 32 + k:33 + k],
                                         in1=xh[:, k, :].bitcast(F32), op0=ALU.mult, op1=ALU.subtract)\
                    .then_inc(S("hgT_lo"), 1)

            def residual(w, done):
                for c in range(2):
                    after_chunk(dve, 1, w, 0, c, 0)
                    for t in range(NT):
                        dve.wait_ge(S(done), NT * c + t + 1)
                        hh = h[:, t, c * 512:(c + 1) * 512]
                        m = dve.tensor_tensor(hh, hh, ps[:, NT * c + t, :], ALU.add)
                        if c == 1:
                            m.then_inc(S("h_final"), 1)
                    after_chunk(dve, 1, w, 0, c, 1)

            residual("a_out", "outA")

            def first_of_max(v, mx, oh):
                link(dve.tensor_reduce(mx, v, AX.X, ALU.max))
                link(dve.tensor_tensor(oh, v, mx.unsqueeze(2).broadcast_to([P, NT, 4]), ALU.is_ge))
                link(dve.tensor_tensor(oh, oh, prio.unsqueeze(1).broadcast_to([P, NT, 4]), ALU.mult))
                link(dve.tensor_reduce(stat[:, 60:64], oh, AX.X, ALU.max))
                link(dve.tensor_tensor(oh, oh, stat[:, 60:64].unsqueeze(2).broadcast_to([P, NT, 4]), ALU.is_ge))

            def moe(l):
                i = 2 * l + 1
                norm(i, stage, True)
                for q in range(4):
                    dve.memset(prio[:, q:q + 1], float(4 - q))
                for e in range(NE):
                    dve.memset(ebase[:, e:e + 1], float(e * SEQ))
                    for b in range(NB - 1):
                        q = 3 * e + b
                        dve.memset(bt[:, q:q + 1], float((b + 1) * P))
                        dve.memset(id48[:, q:q + 1], float(NB * e + b + 1))
                        dve.memset(e48[:, q:q + 1], float(e))
                for q in range(OVMAX):
                    m = dve.memset(j8[:, q:q + 1], float(q + 1))
                link(m)
                low_xT(1 + 3 * l, None)
                dve.wait_ge(S("lg_turned"), l + 1)
                link(dve.tensor_copy(L, ps[:, 1, 0:80].rearrange("p (t c) -> p t c", t=NT)))
                Lg, Le = L[:, :, 0:4], L[:, :, 4:20].rearrange("p t (g e) -> p t g e", g=NG)
                first_of_max(Lg, stat[:, 40:44], ohg)
                dve.tensor_tensor(gd, Lg, stat[:, 40:44].unsqueeze(2).broadcast_to([P, NT, 4]), ALU.subtract)\
                    .then_inc(S("gd_ready"), 1)
                p4 = prod.rearrange("p (t g e) -> p t g e", t=NT, g=NG)
                link(dve.tensor_tensor(p4, Le, ohg.unsqueeze(3).broadcast_to([P, NT, NG, EG]), ALU.mult))
                link(dve.tensor_reduce(esel, prod.rearrange("p (t g e) -> p t e g", t=NT, g=NG), AX.X, ALU.add))
                first_of_max(esel, stat[:, 44:48], oh1)
                link(dve.scalar_tensor_tensor(out=tmp4, in0=oh1, scalar=-BIG, in1=esel, op0=ALU.mult, op1=ALU.add))
                first_of_max(tmp4, stat[:, 48:52], oh2)
                dve.tensor_tensor(stat[:, 52:56], stat[:, 48:52], stat[:, 44:48], ALU.subtract)\
                    .then_inc(S("gd_ready"), 1)
                for k, oh in enumerate((oh1, oh2)):
                    o4 = ohE[k].rearrange("p (t g e) -> p t g e", t=NT, g=NG)
                    link(dve.tensor_tensor(o4, ohg.unsqueeze(3).broadcast_to([P, NT, NG, EG]),
                                           oh.unsqueeze(2).broadcast_to([P, NT, NG, EG]), ALU.mult))
                dve.tensor_tensor(sel_bf, ohE[0], ohE[1], ALU.add).then_inc(S("sel_ready"), 1)
                if l == 0:
                    dve.wait_ge(S("ws_hi"), 3)
                    small(dve, 1, w_fg[:, :, :].rearrange("p k n -> p (k n)"), KD * HB)
                dve.wait_ge(S("ge_ready"), 2 * l + 2)
                link(dve.tensor_reduce(stat[:, 64:68], ge, AX.X, ALU.add))
                link(dve.tensor_scalar(stat[:, 68:72], stat[:, 56:60], 1.0, None, ALU.add))
                link(dve.tensor_tensor(stat[:, 64:68], stat[:, 64:68], stat[:, 68:72], ALU.mult))
                link(dve.reciprocal(wts[:, 0, :], stat[:, 64:68]))
                link(dve.tensor_tensor(wts[:, 1, :], wts[:, 0, :], stat[:, 56:60], ALU.mult))
                dve.wait_ge(S("places"), l + 1)
                link(dve.tensor_tensor(posd.rearrange("p (t e) -> p t e", t=NT),
                                       ps[:, 2, 0:64].rearrange("p (t e) -> p t e", t=NT),
                                       ebase.unsqueeze(1).broadcast_to([P, NT, NE]), ALU.add))
                for k in range(2):
                    link(dve.tensor_tensor(prod, posd, ohE[k], ALU.mult))
                    link(dve.tensor_reduce(stat[:, 72:76], prod.rearrange("p (t e) -> p t e", t=NT), AX.X, ALU.add))
                    m = dve.tensor_copy(dst[:, k, :], stat[:, 72:76])
                    if k == 0:
                        link(m)
                m.then_inc(S("places_ready"), 1)
                link(dve.tensor_copy(cnt, ps[0:1, 3, 0:NE]))
                a3 = act48.rearrange("p (e b) -> p e b", b=NB - 1)
                link(dve.tensor_tensor(a3, cnt.unsqueeze(2).broadcast_to([1, NE, NB - 1]),
                                       bt.rearrange("p (e b) -> p e b", b=NB - 1), ALU.is_gt))
                link(dve.tensor_tensor_scan(cs48, ones_col[0:1, 0:1].broadcast_to([1, NOV]), act48, 0.0, ALU.mult,
                                            ALU.add))
                m3 = m384.rearrange("p (j q) -> p j q", j=OVMAX)
                q3 = q384.rearrange("p (j q) -> p j q", j=OVMAX)
                link(dve.tensor_tensor(m3, cs48.unsqueeze(1).broadcast_to([1, OVMAX, NOV]),
                                       j8.unsqueeze(2).broadcast_to([1, OVMAX, NOV]), ALU.is_equal))
                link(dve.tensor_tensor(m3, m3, act48.unsqueeze(1).broadcast_to([1, OVMAX, NOV]), ALU.mult))
                link(dve.memset(ovf, 0.0))
                link(dve.tensor_copy(ovf[:, 0:1], cs48[:, NOV - 1:NOV]))
                for src, o in ((id48, 8), (e48, 16)):
                    link(dve.tensor_tensor(q3, m3, src.unsqueeze(1).broadcast_to([1, OVMAX, NOV]), ALU.mult))
                    link(dve.tensor_reduce(ovf[:, o:o + 8], q3, AX.X, ALU.add))
                dve.tensor_copy(ov[:, :], ovf).then_inc(S("ov_ready"), 1)
                dve.wait_ge(S("lists_loaded"), 16 * (l + 1))
                dve.tensor_copy(lst_f, lst_i.bitcast(I32)).then_inc(S("lst_ready"), 1)
                dve.wait_ge(S("lst_turned"), l + 1)
                link(dve.tensor_copy(cfull, ps[:, 4, 0:NE * NB]))
                link(dve.tensor_copy(ydst[:, :], cfull))
                link(dve.tensor_scalar(cge, cfull, float(SEQ), -float(SEQ), ALU.is_ge, ALU.mult))
                link(dve.tensor_tensor(cge, cge, cfull, ALU.add))
                link(dve.tensor_scalar(cuse, cfull, float(2 * SEQ), None, ALU.is_lt))
                link(dve.tensor_tensor(cres, cge, cuse, ALU.mult))
                dve.tensor_copy(tok[:, :], cres).then_inc(S("tok_ready"), 1)

                def low_x(n, par):
                    dve.wait_ge(S(f"xg_hi{l}"), n + 1)
                    dve.tensor_tensor(xgr[par][1].rearrange("p (a k) s -> p a (k s)", a=2), ps[:, 2:4, :],
                                      xgr[par][0].bitcast(F32).rearrange("p (a k) s -> p a (k s)", a=2),
                                      ALU.subtract).then_inc(S(f"xg_lo{l}"), 1)

                def hidden(n):
                    dve.wait_ge(S(f"up1_done{l}"), n + 1)
                    dve.wait_ge(S(f"sg_ready{l}"), n + 1)
                    if not isinstance(n, int) or n:
                        dve.wait_ge(S(f"hn_turned{l}"), n)
                    dve.tensor_tensor(hn, sg, ps[:, 1, :], ALU.mult).then_inc(S(f"hn_ready{l}"), 1)

                def low_h(n):
                    dve.wait_ge(S(f"h_hi{l}"), n + 1)
                    dve.tensor_tensor(hr[1], ps[:, 4, :], hr[0].bitcast(F32), ALU.subtract)\
                        .then_inc(S(f"h_lo{l}"), 1)

                p0 = pidx[("gate", l, 0, 0)]
                low_x(0, 0)
                split(dve, 1, p0 + 3)
                split(dve, 1, p0 + 4)
                split(dve, 1, p0 + 5)
                hidden(0)
                low_x(1, 1)
                split(dve, 1, p0 + 6)

                def turn(n, i, par, more=True):
                    base = pidx[("gate", l, par, 0)] if par else pidx[("gate", l, 2, 0)] - 12
                    low_h(n - 1)
                    for q in (3, 4, 5):
                        split_turn(dve, 1, l, n, i, base + q, q)
                    hidden(n)
                    split_turn(dve, 1, l, n, i, base + 6, 6)
                    if more:
                        low_x(n + 1, 1 - par)
                    split_turn(dve, 1, l, n, i, base + 7, 7)
                    if more:
                        split_turn(dve, 1, l, n, i, base + 8, 8)

                turn(1, 0, 1)
                with dve.Fori(1, NE // 2 - 1) as i2:
                    turn(2 * i2, i2, 0)
                    turn(2 * i2 + 1, i2, 1)
                turn(NE - 2, NE // 2 - 1, 0)
                turn(NE - 1, NE // 2 - 1, 1, False)
                low_h(NE - 1)
                n_ov = dve.value_load(ov[0:1, 0:1], min_val=0, max_val=OVMAX)
                with dve.If(n_ov > 0), dve.Fori(0, n_ov) as j:
                    dve.wait_ge(S(f"scattered{l}_0"), 16 * (j + NE // 2))
                    dve.wait_ge(S(f"pool_held{l}"), 3 * j + 1)
                    q = dve.value_load(ov[0:1, bass.ds(j + 8, 1)], min_val=0, max_val=NE * NB - 1)
                    dve.tensor_copy(fix[:, 0:1], tok[:, bass.ds(q, 1)])
                    dve.tensor_copy(fix[:, 1:2], ydst[:, bass.ds(q, 1)]).then_inc(S(f"fix_ready{l}"), 1)
                    low_x(j + NE, 0)
                    for o in range(4):
                        split_further(dve, 1, l, j, o)
                    hidden(j + NE)
                    low_h(j + NE)
                    split_further(dve, 1, l, j, 4)
                    split_further(dve, 1, l, j, 5)
                dve.wait_ge(S(f"scattered{l}_1"), NE // 2 * 16)
                dve.wait_ge(S(f"scattered{l}_0"), (n_ov + NE // 2) * 16)
                dve.tensor_copy(stat[:, 93:94], ones_col[:, :]).then_inc(S("tiles_stored"), 1)
                if l == 0:
                    for p in range(SPLIT):
                        split(dve, 1, pidx[("kv", 0, 0, 0)] + p)
                for t in range(NT):
                    dve.wait_ge(S(f"y_back{t}"), 16 * (l + 1))
                    for k in range(2):
                        m = dve.scalar_tensor_tensor(out=h[:, t, :], in0=yy[:, 2 * t + k, :], scalar=wts[:, k, t:t + 1],
                                                     in1=h[:, t, :], op0=ALU.mult, op1=ALU.add)
                        if k == 0:
                            link(m)
                    m.then_inc(S("h_final"), 1)

            moe(0)

            norm(2, stage_b)
            low_xT(2, 40)
            dve.wait_ge(S("fg_ready"), 1)
            link(dve.scalar_tensor_tensor(out=f_l, in0=f_z, scalar=0.0, in1=f_l, op0=ALU.min, op1=ALU.subtract))
            link(dve.tensor_tensor_scan(cT, ones_col[0:HB, 0:1].broadcast_to([HB, SEQ]), f_l, 0.0, ALU.mult,
                                        ALU.subtract))
            nk = 0
            for g, (w, c, i) in enumerate(B_GROUPS):
                if w == "fg":
                    continue
                wc = ("kv", 0, c) if c < 4 else ("b_in", 0, c - 4)
                if i == 0:
                    after_chunk(dve, 1, *wc, 0)
                if w == "v":
                    dve.wait_ge(S("projB"), g + 1)
                    dve.tensor_copy(vb[:, i, (c - 2) * 512:(c - 1) * 512], ps[:, g % 6, :]).then_inc(S("D_evacB"), 1)
                    if i == 3:
                        after_chunk(dve, 1, *wc, 1)
                        if c == 3:
                            low_xT(3, 8)
                    continue
                dve.wait_ge(S("sq_ready"), nk + 1)
                dve.tensor_reduce(stat[:, 8:16], sq.rearrange("p (a b) -> p a b", a=8), AX.X, ALU.add)\
                    .then_inc(S("hss_ready"), 1)
                dve.wait_ge(S("hrms2_ready"), nk + 1)
                link(dve.reciprocal(stat[:, 24:32], stat[:, 16:24]))
                if nk >= 2:
                    dve.wait_ge(S("nat_turned"), nk - 1)
                dve.wait_ge(S("projB"), g + 1)
                dve.tensor_tensor(nat[:, nk % 2, :].rearrange("p (a b) -> p a b", a=8),
                                  ps[:, g % 6, :].rearrange("p (a b) -> p a b", a=8),
                                  stat[:, 24:32].unsqueeze(2).broadcast_to([P, 8, DH]), ALU.mult)\
                    .then_inc(S("D_evacB"), 1)
                if i == 3:
                    after_chunk(dve, 1, *wc, 1)
                nk += 1
            dve.wait_ge(S("nat_turned"), 16)
            dve.wait_ge(S("ws_hi"), 4)
            small(dve, 1, w_rt[:, 1, :, :].rearrange("p k n -> p (k n)"), KD * (NG + NE))
            for c in (2, 3):
                after_chunk(dve, 1, "b_in", 0, c, 0)
                if c == 2:
                    after_chunk(dve, 1, "b_in", 0, c, 1)

            steps = [(hd, j) for hd in range(HB) for j in range(NT)]

            def max_of(n):
                hd, j = steps[n]
                if j == 0:
                    dve.wait_ge(S("negc_ready"), hd + 1)
                    link(dve.tensor_tensor(negd.rearrange("p (a b) -> p a b", a=NT),
                                           negc[:, hd % 2, :].rearrange("p (a b) -> p a b", a=NT),
                                           mask_ts[:, :].unsqueeze(1).broadcast_to([P, NT, P]), ALU.add))
                dve.wait_ge(S("s_ready"), n + 1)
                if n >= 3:
                    dve.wait_ge(S("p_turned"), n - 2)
                a, b = 64 + n % 4, 68 + n % 4
                if j:
                    link(dve.tensor_tensor_reduce(pbuf[:, n % 3, 0:j * P], ps[:, n % 2, 0:j * P],
                                                  negc[:, hd % 2, 0:j * P], 1.0, -3e38, ALU.add, ALU.max,
                                                  stat[:, a:a + 1]))
                link(dve.tensor_tensor_reduce(pbuf[:, n % 3, j * P:(j + 1) * P], ps[:, n % 2, j * P:(j + 1) * P],
                                              negd[:, j * P:(j + 1) * P], 1.0,
                                              stat[:, a:a + 1] if j else -3e38, ALU.add, ALU.max, stat[:, b:b + 1]))
                dve.tensor_scalar(stat[:, 72 + n % 4:73 + n % 4], stat[:, b:b + 1], -1.0, None, ALU.mult)\
                    .then_inc(S("s_used"), 1)

            def normalise(n):
                hd, j = steps[n]
                dve.wait_ge(S("e_ready"), n + 1)
                link(dve.reciprocal(stat[:, 80 + n % 4:81 + n % 4], stat[:, 76 + n % 4:77 + n % 4]))
                pp = pbuf[:, n % 3, 0:(j + 1) * P]
                dve.tensor_scalar(pp, pp, stat[:, 80 + n % 4:81 + n % 4], None, ALU.mult).then_inc(S("p_ready"), 1)

            def low_o(r):
                dve.wait_ge(S("oT_hi"), r + 1)
                dve.tensor_tensor(xl[:, r, :], negd2, xh[:, r, :].bitcast(F32), ALU.subtract)\
                    .then_inc(S("oT_lo"), 1)

            for n in range(len(steps) + 1):
                if n < len(steps):
                    max_of(n)
                if n:
                    normalise(n - 1)
                if n >= 12 and (n - 12) % 8 == 0 or n == len(steps):
                    r = (n - 12) // 8 if n < len(steps) else 7
                    dve.wait_ge(S("o_ready"), 8 * (r + 1))
                    og = og_t[r // 4][:, r % 4, :]
                    if r:
                        dve.wait_ge(S("oT_hi"), r)
                    dve.tensor_tensor(negd2, ps[:, 4 + r % 2, :], og, ALU.mult).then_inc(S("oT_ready"), 1)
                if n >= 13 and (n - 13) % 8 == 0 or n == len(steps):
                    low_o((n - 13) // 8 if n < len(steps) else 7)
            after_chunk(dve, 1, "b_in", 0, 3, 1)
            residual("b_out", "outB")
            moe(1)
            dve.wait_ge(S("rms"), 5)
            link(dve.reciprocal(stat[:, 4:8], stat[:, 0:4]))
            dve.wait_ge(S("nf_loaded"), 16)
            for t in range(NT):
                dve.scalar_tensor_tensor(out=fo[:, t, :], in0=h[:, t, :], scalar=stat[:, 4 + t:5 + t], in1=nf,
                                         op0=ALU.mult, op1=ALU.mult).then_inc(S("final_rows"), 1)

        @block.scalar
        def _(act):
            chain = [0]

            def link(ins):
                chain[0] += 1
                ins.then_inc(S("act_step"), 1)
                act.wait_ge(S("act_step"), chain[0])

            act.wait_ge(S("zeroed"), 3)
            rl = S("rows_loaded")
            as8 = lambda v: v.rearrange("(k p) -> k p", p=P)
            n = 0
            for r, v in ((0, as8(norm_mix[0])), (8, as8(norm_mix[1])), (16, as8(norm_ffn[0])), (24, as8(norm_ffn[1])),
                         (32, as8(a_head_gain[0])), (40, as8(kv_norm))):
                act.dma_start(rows[r:r + 8, :], v).then_inc(rl, 16)
            one = lambda v: v.rearrange("(a n) -> a n", a=1)
            for r, c, v in ((48, 0, one(kv_k_gain)), (48, 64, one(kv_k_gain)), (49, 0, b_q_gain), (49, 64, b_q_gain),
                            (50, 0, a_b_gate[:, 0:HA]), (50, 32, a_b_gate[:, HA:2 * HA]), (51, 0, one(kv_b_f)),
                            (52, 0, moe_b_grp[0:1, :]), (52, 4, moe_b_exp[0:1, :]),
                            (53, 0, moe_b_grp[1:2, :]), (53, 4, moe_b_exp[1:2, :])):
                act.dma_start(rows[r:r + 1, c:c + v.shape[1]], v).then_inc(rl, 16)
            act.wait_ge(rl, 16 * ROWS_DMAS)
            gw = a_w_in[0].rearrange("(k p) n -> p k n", p=P)[:, :, 3072:3080]
            act.dma_start(w_gates[:, :, 0:HA], gw[:, :, 0:HA]).then_inc(S("gates_w"), 16)
            act.dma_start(w_gates[:, :, 32:32 + HA], gw[:, :, HA:2 * HA]).then_inc(S("gates_w"), 16)
            act.dma_start(w_fg[:, :, :], kv_w.rearrange("(k p) n -> p k n", p=P)[:, :, 2 * D:2 * D + HB]).then_inc(S("fg_w"), 16)
            for l in range(2):
                act.dma_start(w_rt[:, l, :, 0:NG], moe_w_grp[l].rearrange("(k p) n -> p k n", p=P))\
                    .then_inc(S("rt_w"), 16)
                act.dma_start(w_rt[:, l, :, NG:NG + NE], moe_w_exp[l].rearrange("(k p) n -> p k n", p=P))\
                    .then_inc(S("rt_w"), 16)

            def squares(i):
                for t in range(NT):
                    if i == 0:
                        act.wait_ge(S("x_loaded"), 16)
                        act.wait_ge(S("consts"), 1)
                    else:
                        act.wait_ge(S("h_final"), NT * (i - 1) + t + 1)
                    m = act.activation(junk[:, t, :], h[:, t, :], ACT.Square, accum_out=stat[:, 88 + t:89 + t])
                link(m)
                act.activation(stat[:, 0:4], stat[:, 88:92], ACT.Sqrt, scale=1.0 / D, bias=eps_col[:, :])\
                    .then_inc(S("rms"), 1)

            def high_xT(j, col):
                for k in range(KD):
                    act.wait_ge(S("xn_turned"), KD * j + k + 1)
                    act.activation(xh[:, k, :], ps[:, k, :], ACT.Copy,
                                   scale=1.0 if col is None else gains[:, col + k:col + k + 1])\
                        .then_inc(S("xT_hi"), 1)

            squares(0)
            act.wait_ge(S("gates_w"), 32)
            small(act, 0, w_gates[:, :, :].rearrange("p k n -> p (k n)"), KD * 36)
            act.wait_ge(S("gains_ready"), 1)
            high_xT(0, 0)
            for p in range(SPLIT):
                split(act, 0, p)
            act.wait_ge(S("projA"), 1)
            act.activation(g_t, ps[0:36, 0, :], ACT.Tanh, scale=1.0 / CAP, bias=gate15[0:36, :])\
                .then_inc(S("A_evacA"), 1)
            act.wait_ge(S("A_evacA"), 1)
            link(act.activation(g_e, g_t[32:36, :], ACT.Exp, scale=-CAP))
            act.activation(g_lf, g_e, ACT.Ln, bias=ones_col[0:4, :]).then_inc(S("gates_ready"), 1)
            act.wait_ge(S("rt_w"), 64)
            small(act, 0, w_rt[:, 0, :, :].rearrange("p k n -> p (k n)"), KD * (NG + NE))
            for c in range(3):
                after_chunk(act, 0, "a_in", 0, c, 0)
                after_chunk(act, 0, "a_in", 0, c, 1)
            act.wait_ge(S("umn_ready"), 1)
            umn = arena[:, UMN:UMN + 144].rearrange("p (t c) -> p t c", t=NT)
            act.activation(stat[:, 32:48].rearrange("p (h t) -> p t h", h=HA), umn[:, :, 32:36], ACT.Exp, scale=-1.0)\
                .then_inc(S("em_ready"), 1)
            after_chunk(act, 0, "a_in", 0, 3, 0)
            for hd in range(HA):
                act.wait_ge(S("m_spread_used"), hd + 1)
                for i in range(NT):
                    dd = dec[:, hd, DO[i]:DO[i] + DW[i]]
                    act.activation(dd, dd, ACT.Exp, scale=-1.0, bias=umn[:, i, hd:hd + 1])\
                        .then_inc(S("dec_ready"), 1)
            after_chunk(act, 0, "a_in", 0, 3, 1)
            for g in range(17, 25):
                w, c, i = A_GROUPS[g]
                if i == 0:
                    after_chunk(act, 0, "a_in", 0, c, 0)
                act.wait_ge(S("projA"), g + 1)
                act.activation(so[:, i, (c - 4) * 512:(c - 3) * 512], ps[:, g % 6, :], ACT.Sigmoid)\
                    .then_inc(S("A_evacA"), 1)
                if i == 3:
                    after_chunk(act, 0, "a_in", 0, c, 1)
            for hd in range(HA):
                act.wait_ge(S("rden_ready"), hd + 1)
                for j in range(NT):
                    m = act.activation(sqa[:, j, :], ps[:, 4 + j, 0:DV], ACT.Square, scale=stat[:, 20 + j:21 + j],
                                       accum_out=stat[:, 84 + j:85 + j])
                link(m)
                act.activation(stat[:, 24:28], stat[:, 84:88], ACT.Sqrt, scale=1.0 / DV, bias=eps_col[:, :])\
                    .then_inc(S("hrms_ready"), 1)
            for k in range(KD):
                act.wait_ge(S("hg_turned"), k + 1)
                act.activation(xh[:, k, :], ps[:, k, :], ACT.Copy, scale=gains[:, 32 + k:33 + k])\
                    .then_inc(S("hgT_hi"), 1)
            for c in range(2):
                after_chunk(act, 0, "a_out", 0, c, 0)
                after_chunk(act, 0, "a_out", 0, c, 1)

            def moe(l):
                i = 2 * l + 1
                squares(i)
                high_xT(1 + 3 * l, None)
                act.wait_ge(S("logits"), l + 1)
                act.activation(lgT, ps[0:20, 0, :], ACT.Identity, bias=gains[0:20, 52 + l:53 + l])\
                    .then_inc(S("lgT_ready"), 1)
                act.wait_ge(S("gd_ready"), 2 * l + 1)
                act.activation(ge, gd, ACT.Exp).then_inc(S("ge_ready"), 1)
                act.wait_ge(S("gd_ready"), 2 * l + 2)
                act.activation(stat[:, 56:60], stat[:, 52:56], ACT.Exp).then_inc(S("ge_ready"), 1)

                if l == 0:
                    act.wait_ge(S("fg_w"), 16)
                    small(act, 0, w_fg[:, :, :].rearrange("p k n -> p (k n)"), KD * HB)

                def high_x(n, par):
                    act.wait_ge(S(f"xg_turned{l}"), n + 1)
                    act.activation(xgr[par][0].rearrange("p (a k) s -> p a (k s)", a=2), ps[:, 2:4, :], ACT.Copy)\
                        .then_inc(S(f"xg_hi{l}"), 1)

                def gate(n):
                    act.wait_ge(S(f"gate1_done{l}"), n + 1)
                    if not isinstance(n, int) or n:
                        act.wait_ge(S(f"hn_ready{l}"), n)
                    act.activation(sg, ps[:, 0, :], ACT.Silu).then_inc(S(f"sg_ready{l}"), 1)

                def high_h(n):
                    act.wait_ge(S(f"hn_turned{l}"), n + 1)
                    act.activation(hr[0], ps[:, 4, :], ACT.Copy).then_inc(S(f"h_hi{l}"), 1)

                def take_y(n, a, par, scattered=None):
                    act.wait_ge(S(f"down{a}_done{l}"), n + 1)
                    if scattered is not None:
                        act.wait_ge(S(f"scattered{l}_{par}"), scattered)
                    act.activation(yb[:, par, a * 512:(a + 1) * 512], ps[:, 5 + a, :], ACT.Copy)\
                        .then_inc(S(f"y{a}_ready{l}"), 1)

                p0 = pidx[("gate", l, 0, 0)]
                high_x(0, 0)
                split(act, 0, p0 + 3)
                gate(0)
                split(act, 0, p0 + 4)
                split(act, 0, p0 + 5)
                high_x(1, 1)
                split(act, 0, p0 + 6)

                def turn(n, i, par, scattered, more=True):
                    base = pidx[("gate", l, par, 0)] if par else pidx[("gate", l, 2, 0)] - 12
                    high_h(n - 1)
                    split_turn(act, 0, l, n, i, base + 3, 3)
                    split_turn(act, 0, l, n, i, base + 4, 4)
                    gate(n)
                    split_turn(act, 0, l, n, i, base + 5, 5)
                    split_turn(act, 0, l, n, i, base + 6, 6)
                    if more:
                        high_x(n + 1, 1 - par)
                    split_turn(act, 0, l, n, i, base + 7, 7)
                    take_y(n - 1, 0, 1 - par, scattered)
                    if more:
                        split_turn(act, 0, l, n, i, base + 8, 8)
                    take_y(n - 1, 1, 1 - par, scattered)

                turn(1, 0, 1, None)
                turn(2, 1, 0, None)
                turn(3, 1, 1, 16)
                with act.Fori(2, NE // 2 - 1) as i2:
                    turn(2 * i2, i2, 0, 16 * i2 - 16)
                    turn(2 * i2 + 1, i2, 1, 16 * i2)
                turn(NE - 2, NE // 2 - 1, 0, 16 * (NE // 2 - 2))
                turn(NE - 1, NE // 2 - 1, 1, 16 * (NE // 2 - 1), False)
                high_h(NE - 1)
                take_y(NE - 1, 0, 1, 16 * (NE // 2 - 1))
                take_y(NE - 1, 1, 1, 16 * (NE // 2 - 1))
                act.wait_ge(S("ov_ready"), l + 1)
                n_ov = act.value_load(ov[0:1, 0:1], min_val=0, max_val=OVMAX)
                with act.If(n_ov > 0), act.Fori(0, n_ov) as j:
                    high_x(j + NE, 0)
                    for o in range(4):
                        split_further(act, 0, l, j, o)
                    gate(j + NE)
                    high_h(j + NE)
                    split_further(act, 0, l, j, 4)
                    split_further(act, 0, l, j, 5)
                    take_y(j + NE, 0, 0)
                    take_y(j + NE, 1, 0)
                if l == 0:
                    for p in range(SPLIT):
                        split(act, 0, pidx[("kv", 0, 0, 0)] + p)

            moe(0)

            squares(2)
            high_xT(2, 40)
            act.wait_ge(S("projB"), 1)
            act.activation(f_z, ps[0:HB, 0, :], ACT.Identity, bias=gains[0:HB, 51:52]).then_inc(S("A_evacB"), 1)
            act.wait_ge(S("A_evacB"), 1)
            link(act.activation(f_a, f_z, ACT.Abs))
            link(act.activation(f_e, f_a, ACT.Exp, scale=-1.0))
            act.activation(f_l, f_e, ACT.Ln, bias=ones_col[0:HB, :]).then_inc(S("fg_ready"), 1)

            def take_heads(n):
                act.wait_ge(S("nat_turned"), n + 1)
                q = n >= 8
                c, i = (n % 8) // 4, n % 4
                dd = (qTb if q else kTb)[:, 4 * c:4 * c + 4, i * P:(i + 1) * P]
                act.activation(dd, ps[:, 6 + n % 2, :].rearrange("p (r t) -> p r t", r=4), ACT.Copy,
                               scale=qg_col if q else gains[:, 48:49]).then_inc(S("headsT_ready"), 1)

            qg_col = stat[:, 92:93]
            link(act.activation(qg_col, gains[:, 49:50], ACT.Copy, scale=DH ** -0.5))
            nk = 0
            for g, (w, c, i) in enumerate(B_GROUPS):
                if w == "fg":
                    continue
                wc = ("kv", 0, c) if c < 4 else ("b_in", 0, c - 4)
                if i == 0:
                    after_chunk(act, 0, *wc, 0)
                if w == "v":
                    if i == 3:
                        after_chunk(act, 0, *wc, 1)
                        if c == 2:
                            take_heads(6)
                            take_heads(7)
                        if c == 3:
                            high_xT(3, 8)
                    continue
                act.wait_ge(S("projB"), g + 1)
                if nk:
                    act.wait_ge(S("hss_ready"), nk)
                act.activation(sq, ps[:, g % 6, :], ACT.Square).then_inc(S("sq_ready"), 1)
                act.wait_ge(S("hss_ready"), nk + 1)
                act.activation(stat[:, 16:24], stat[:, 8:16], ACT.Sqrt, scale=1.0 / DH, bias=eps_col[:, :])\
                    .then_inc(S("hrms2_ready"), 1)
                nk += 1
                if nk > 2 and nk not in (9, 10):
                    take_heads(nk - 3)
                if i == 3:
                    after_chunk(act, 0, *wc, 1)
            take_heads(14)
            take_heads(15)
            small(act, 0, w_rt[:, 1, :, :].rearrange("p k n -> p (k n)"), KD * (NG + NE))
            for c in range(2):
                after_chunk(act, 0, "b_in", 0, 2 + c, 0)
                for q in range(4):
                    act.wait_ge(S("ogB"), 4 * c + q + 1)
                    act.activation(og_t[c][:, q, :], ps[:, q, :], ACT.Sigmoid).then_inc(S("og_ready"), 1)
                if c == 0:
                    after_chunk(act, 0, "b_in", 0, 2, 1)

            steps = [(hd, j) for hd in range(HB) for j in range(NT)]

            def take_c(hd):
                act.wait_ge(S("c_spread"), hd + 1)
                if hd >= 2:
                    act.wait_ge(S("s_used"), NT * (hd - 1))
                act.activation(negc[:, hd % 2, :], ps[:, 6, :], ACT.Copy).then_inc(S("negc_ready"), 1)

            act.wait_ge(S("fg_ready"), 1)
            act.wait_ge(S("D_evacB"), EVAC["B"].count("D"))
            take_c(0)
            for n in range(len(steps) + 2):
                if n < len(steps):
                    hd, j = steps[n]
                    act.wait_ge(S("s_used"), n + 1)
                    pp = pbuf[:, n % 3, 0:(j + 1) * P]
                    act.activation(pp, pp, ACT.Exp, bias=stat[:, 72 + n % 4:73 + n % 4],
                                   accum_out=stat[:, 76 + n % 4:77 + n % 4]).then_inc(S("e_ready"), 1)
                    if n % NT == 2 and hd + 1 < HB:
                        take_c(hd + 1)
                if n >= 2:
                    hd, j = steps[n - 2]
                    act.wait_ge(S("p_turned"), n - 1)
                    if n >= 4:
                        act.wait_ge(S("o_ready"), n - 3)
                    act.activation(ptb[:, n % 2, 0:(j + 1) * P], ps[:, 2 + n % 2, 0:(j + 1) * P], ACT.Copy)\
                        .then_inc(S("pT_ready"), 1)
                if n >= 12 and (n - 12) % 8 == 0 or n == len(steps) + 1:
                    r = (n - 12) // 8 if n < len(steps) else 7
                    act.wait_ge(S("oT_ready"), r + 1)
                    act.activation(xh[:, r, :], negd2, ACT.Copy).then_inc(S("oT_hi"), 1)
            after_chunk(act, 0, "b_in", 0, 3, 1)
            for c in range(2):
                after_chunk(act, 0, "b_out", 0, c, 0)
                after_chunk(act, 0, "b_out", 0, c, 1)
            moe(1)
            squares(4)


ROWS_DMAS = 17
ARENA = 17568
WSN = 384
UMN = 17424
EVAC = {"A": ["A"] + ["D"] * 16 + ["A"] * 8, "B": ["A"] + ["D"] * 24}


_INS = ['x', 'norm_mix', 'norm_ffn', 'a_w_in', 'a_b_gate', 'a_head_gain', 'a_w_out', 'kv_norm', 'kv_w', 'kv_b_f',
        'kv_k_gain', 'b_w_in', 'b_q_gain', 'b_w_out', 'moe_w_grp', 'moe_b_grp', 'moe_w_exp', 'moe_b_exp',
        'moe_w_gate', 'moe_w_up', 'moe_w_down', 'norm_final']
_OUTS = [((1, SEQ, D), 'float32')]


def kernel(**inputs):
    import numpy as _np
    import concourse.bacc as _bacc
    from concourse import mybir as _mybir
    from concourse.bass_utils import run_bass_kernel_spmd as _run

    nc = _bacc.Bacc("TRN2", target_bir_lowering=False, num_devices=1)
    arrays, args = {}, []
    for name in _INS:
        a = _np.ascontiguousarray(inputs[name])
        arrays[f"in_{name}_dram"] = a
        args.append(nc.dram_tensor(f"in_{name}_dram", a.shape, _mybir.dt.from_np(a.dtype), kind="ExternalInput").ap())
    for i, (shape, dtype) in enumerate(_OUTS):
        dt = _mybir.dt.from_np(_np.dtype(dtype))
        args.append(nc.dram_tensor(f"out_{i}_dram", shape, dt, kind="ExternalOutput").ap())
    trunk(nc, *args)
    r = _run(nc, [arrays], core_ids=[0])
    return r.results[0]["out_0_dram"]
```

```python
from contextlib import ExitStack

import concourse.bass as bass
from concourse import mybir

P = 128
F32 = mybir.dt.float32
BF16 = mybir.dt.bfloat16
I32 = mybir.dt.int32
F32R = mybir.dt.float32r
ALU = mybir.AluOpType
ACT = mybir.ActivationFunctionType
AX = mybir.AxisListType

SEQ, D = 512, 1024
NT = SEQ // P
KD = D // P
EPS = 1e-6
HA, DQK, DV = 4, 128, 256
CAP = 15.0
HB, DH = 16, 64
NG, EG = 4, 4
NE = NG * EG
DE = 512
KE = DE // P
W = 512
KH = 4
PC = KH * W
RAW, SPLIT = 4, 3
RAW_MOE = 6
BIG = 1e30
TILE = 96
NB = -(-SEQ // TILE)
NOV = NE * (NB - 1)
OVMAX = (2 * SEQ - 1) // TILE
NOCODE = 4 * SEQ


def plan_pieces():
    two = lambda w, l, i: [(w, l, i, 0), (w, l, i, 1)]
    mix_a = [q for c in range(6) for q in two("a_in", 0, c)] + [q for c in range(2) for q in two("a_out", 0, c)]
    mix_b = [q for w, n in (("kv", 4), ("b_in", 4), ("b_out", 2)) for c in range(n) for q in two(w, 0, c)]

    def moe(l):
        seq = two("gate", l, 0) + two("up", l, 0)
        for e in range(1, NE):
            seq += two("gate", l, e) + two("up", l, e) + two("down", l, e - 1)
        return seq + two("down", l, NE - 1)

    seq = mix_a + moe(0) + mix_b + moe(1)
    raw = [n % r for phase, r in ((mix_a, RAW), (moe(0), RAW_MOE), (mix_b, RAW), (moe(1), RAW_MOE))
           for n in range(len(phase))]
    b0 = seq.index(("b_out", 0, 0, 0))
    raw[b0:b0 + 4] = [2, 3, 0, 1]
    return seq, raw


def trunk(nc, x, norm_mix, norm_ffn, a_w_in, a_b_gate, a_head_gain, a_w_out, kv_norm, kv_w, kv_b_f, kv_k_gain,
          b_w_in, b_q_gain, b_w_out, moe_w_grp, moe_b_grp, moe_w_exp, moe_b_exp, moe_w_gate, moe_w_up,
          moe_w_down, norm_final, out):
    seq, raw_slot = plan_pieces()
    pidx = {k: n for n, k in enumerate(seq)}
    nth = [raw_slot[:n].count(raw_slot[n]) for n in range(len(seq))]
    before = [max([m for m in range(n) if raw_slot[m] == raw_slot[n]], default=None) for n in range(len(seq))]

    xd = [nc.dram_tensor(f"normed_{l}", [SEQ, D], F32, kind="Internal").ap() for l in range(2)]
    cd = nc.dram_tensor("neg_c", [HB, SEQ], F32, kind="Internal").ap()
    yd = [nc.dram_tensor(f"expert_out_{l}", [2 * SEQ, D], F32, kind="Internal").ap() for l in range(2)]

    with ExitStack() as ctx:
        def sb(name, shape, dt=F32):
            return ctx.enter_context(nc.sbuf_tensor(name, shape, dt))

        sems = {}

        def S(name):
            if name not in sems:
                sems[name] = ctx.enter_context(nc.semaphore(name))
            return sems[name]

        ps = ctx.enter_context(nc.psum_tensor("ps", [P, 8, 512], F32))
        h = sb("h", [P, NT, D])
        xr = sb("xr", [P, 2 * KD * SEQ], F32R)
        raw = sb("raw", [P, RAW, PC])
        wr = sb("wr", [P, SPLIT, 2, PC], F32R)
        ws = sb("ws", [P, 2, WSN], F32R)
        xh, xl = (xr[:, a * KD * SEQ:(a + 1) * KD * SEQ].rearrange("p (k t) -> p k t", k=KD) for a in range(2))
        xgr = [[xr[:, n * 2048 + a * 1024:n * 2048 + (a + 1) * 1024].rearrange("p (k s) -> p k s", k=KD)
                for a in range(2)] for n in range(2)]
        hr = [xr[:, 4096 + a * DE:4096 + (a + 1) * DE] for a in range(2)]
        arena = sb("arena", [P, ARENA])
        ident = sb("ident", [P, P])
        mask_ts = sb("mask_ts", [P, P])
        mask_st = sb("mask_st", [P, P])
        tri_bf = sb("tri_bf", [P, P], BF16)
        ones_bf = sb("ones_bf", [P, P], BF16)
        rows = arena[0:52, 12304:12304 + P]
        gains = sb("gains", [P, 52])
        gate15 = sb("gate15", [P, 1])
        eps_col = sb("eps_col", [P, 1])
        ones_col = sb("ones_col", [P, 1])
        held = sb("held", [P, 8])
        w_gates = sb("w_gates", [P, KD, 36])
        w_fg = sb("w_fg", [P, KD, HB])
        w_rt = sb("w_rt", [P, 2, KD, NG + NE])
        stat = sb("stat", [P, 96])
        rbias = sb("rbias", [P, 2, NG + NE])
        rc = sb("rc", [P, 123])
        edges = rc[:, 0:NB + 1]
        prio = rc[:, 7:11]
        code_hi = rc[:, 11:19]
        code_lo = rc[:, 19:27]
        place = rc[:, 27:123]
        tok = sb("tok", [TILE, NE * NB], I32)
        ydst = sb("ydst", [TILE, NE * NB], I32)
        fix = sb("fix", [TILE, 2], I32)
        ov = sb("ov", [1, 48], I32)
        wts = sb("wts", [P, 2, NT])

        top = [0]

        def cut(n, shape=None, parts=P):
            o = top[0]
            top[0] = o + n
            assert o + n <= ARENA, o + n
            v = arena[0:parts, o:o + n]
            return v.rearrange(*shape[:1], **shape[1]) if shape else v

        top[0] = 0
        qT = cut(HA * SEQ, ("p (h t) -> p h t", dict(h=HA)))
        kT = cut(HA * SEQ, ("p (h t) -> p h t", dict(h=HA)))
        va = cut(NT * HA * (DV + 1), ("p (t h v) -> p t h v", dict(t=NT, h=HA)))
        so = cut(NT * D, ("p (t d) -> p t d", dict(t=NT)))
        dec = cut(HA * 1280, ("p (h c) -> p h c", dict(h=HA)))
        g_t = arena[0:36, 8208:8208 + 512]
        g_e = arena[0:4, 8208 + 512:8208 + 1024]
        g_lf = arena[0:4, 8208 + 1024:8208 + 1536]
        g_b = arena[0:4, 8208 + 1536:8208 + 2048]
        g_um = arena[0:36, 8208 + 2048:8208 + 2560]
        g_m = arena[0:4, 8208 + 2560:8208 + 3072]
        sqa = xr[:, 0:NT * DV].rearrange("p (t v) -> p t v", t=NT)
        stage = arena[:, 0:NT * D].rearrange("p (t d) -> p t d", t=NT)
        stage_b = arena[:, 4096:4096 + NT * D].rearrange("p (t d) -> p t d", t=NT)
        junk = arena[:, 8192:8192 + NT * D].rearrange("p (t d) -> p t d", t=NT)
        top[0] = 0
        kTb = cut(8 * SEQ, ("p (r t) -> p r t", dict(r=8)))
        qTb = cut(8 * SEQ, ("p (r t) -> p r t", dict(r=8)))
        vb = cut(NT * D, ("p (t d) -> p t d", dict(t=NT)))
        cT = cut(SEQ, parts=HB)
        p_at = top[0]
        top[0] += 5 * 512
        pbuf, ptb = (raw[:, 2 + q, :].rearrange("p (n c) -> p n c", n=4) for q in range(2))
        negc = cut(2 * 512, ("p (n c) -> p n c", dict(n=2)))
        negd = cut(512)
        negd2 = cut(512)
        nat = arena[:, p_at:p_at + 1024].rearrange("p (n c) -> p n c", n=2)
        sq = arena[:, p_at + 1024:p_at + 1536]
        f_z = arena[0:HB, p_at + 1536:p_at + 2048]
        f_a = arena[0:HB, p_at + 2048:p_at + 2560]
        f_e = arena[0:HB, p_at + 2560:p_at + 3072]
        f_l = arena[0:HB, p_at + 3072:p_at + 3584]
        score_bank = lambda n: (0, 1, 6)[n % 3]
        pT_bank = lambda n: (2, 3, 7)[n % 3]
        og_t = [raw[:, c, :].rearrange("p (k t) -> p k t", k=4) for c in range(2)]
        xg = arena[:, 0:2048].rearrange("p (n d) -> p n d", n=2)
        yb = arena[:, 2048:4096].rearrange("p (n d) -> p n d", n=2)
        gain_bc = arena[:, 4096:4096 + D]
        sg = arena[:, 5120:5632]
        hn = arena[:, 5632:6144]
        yy = arena[:, 7680:7680 + 8192].rearrange("p (n d) -> p n d", n=8)
        ow = arena[:, 7680:7680 + 8192].rearrange("p (n c) -> p n c", n=4)
        r0 = 7680
        rt = lambda o, n: arena[:, r0 + o:r0 + o + n]
        L = rt(0, NT * 20).rearrange("p (t c) -> p t c", t=NT)
        gd = rt(80, 16).rearrange("p (t g) -> p t g", t=NT)
        ge = rt(96, 16).rearrange("p (t g) -> p t g", t=NT)
        ohg = rt(112, 16).rearrange("p (t g) -> p t g", t=NT)
        tmp4 = rt(128, 16).rearrange("p (t g) -> p t g", t=NT)
        esel = rt(144, 16).rearrange("p (t g) -> p t g", t=NT)
        oh12 = rt(160, 32).rearrange("p (k t g) -> p k t g", k=2, t=NT)
        prod = rt(192, 128)
        oh_e = rt(320, 128)
        oh_b = rt(448, 56).rearrange("p (c b) -> p c b", b=NB + 1)
        reach = rt(504, 56).rearrange("p (c b) -> p c b", b=NB + 1)
        oh_bc = [rt(560 + 48 * q, 48).rearrange("p (c b) -> p c b", b=NB) for q in range(2)]
        oh_place = rt(656, TILE * NT).bitcast(BF16).rearrange("p (c j) -> p c j", c=2 * NT)
        oh_tile = [rt(1040 + q * NE * NB * NT, NE * NB * NT).bitcast(BF16).rearrange("p (c q) -> p c q", c=2 * NT)
                   for q in range(2)]
        listed = lambda o: arena[0:TILE, r0 + o:r0 + o + NE * NB]
        cfull, cneg, ctok, cdst = (listed(1808 + 96 * q) for q in range(4))
        sel_bf = rt(2192, 32).bitcast(BF16)
        row0 = lambda o, n: arena[0:1, r0 + o:r0 + o + n]
        cnt = row0(2224, NE)
        reached = row0(2240, NOV)
        so_far = row0(2320, NOV)
        jth = row0(2400, OVMAX * NOV)
        taken = row0(3200, OVMAX * NOV)
        ovf = row0(4000, 48)
        further_i = row0(4048, 3 * NOV + OVMAX).bitcast(I32)
        further = row0(4298, 3 * NOV + OVMAX)
        starts, list_tiles, experts = (further[:, NOV * q:NOV * (q + 1)] for q in range(3))
        nth_further = further[:, 3 * NOV:]
        rc_i = arena[:, 17000:17123].bitcast(I32)
        assert r0 + 4548 <= 12544
        raw_at = lambda n: raw[:, n, :] if n < RAW else arena[:, 12544 + (n - RAW) * PC:12544 + (n - RAW + 1) * PC]
        hT = arena[:, 12544:12544 + NT * D].rearrange("p (t k c) -> p t k c", t=NT, k=KD)
        nf = arena[:, 0:D]
        fo = arena[:, 4096:4096 + NT * D].rearrange("p (t d) -> p t d", t=NT)

        DW = [512, 384, 256, 128]
        DO = [0, 512, 896, 1152]

        block = ctx.enter_context(nc.Block())

        halves = lambda v: v.rearrange("(a k p) n -> a p k n", a=2, p=P)
        wv = {
            "a_in": halves(a_w_in[0]), "a_out": halves(a_w_out[0]), "kv": halves(kv_w), "b_in": halves(b_w_in[0]),
            "b_out": halves(b_w_out[0]),
            "gate": moe_w_gate.rearrange("l e (a k p) n -> l e a p k n", a=2, p=P),
            "up": moe_w_up.rearrange("l e (a k p) n -> l e a p k n", a=2, p=P),
            "down": moe_w_down.rearrange("l e (k p) (a n) -> l e a p k n", a=2, p=P),
        }

        def kn(flat):
            return flat.rearrange("p (k n) -> p k n", k=KH)

        def landed(n):
            return S(f"raw_in_slot{raw_slot[n]}"), 16 * (nth[n] + 1)

        release = {}
        A_GROUPS = [("gates", None, 0)] + [("q", 0, i) for i in range(4)] + [("k", 1, i) for i in range(4)] + \
            [(w, c, i) for w, cc in (("v", (2, 3)), ("o", (4, 5))) for c in cc for i in range(NT)]
        B_GROUPS = [("fg", None, 0)] + [(w, c, i) for w, cc in (("k", (0, 1)), ("v", (2, 3)), ("q", (4, 5)))
                                        for c in cc for i in range(NT)]
        chunks = [k[:3] for k in seq if k[0] not in ("gate", "up", "down") and k[3] == 0]
        for m, (w, l, c) in enumerate(chunks):
            release[pidx[(w, l, c, 0)]] = ("half_used", m + 1)
            last = {"a_in": ("projA", 4 * c + 5), "a_out": ("outA", NT * (c + 1)), "kv": ("projB", 4 * c + 5),
                    "b_in": ("projB", 4 * c + 21) if c < 2 else ("ogB", 4 * (c - 1)), "b_out": ("outB", NT * (c + 1))}
            release[pidx[(w, l, c, 1)]] = last[w]
        for l in range(2):
            for e in range(NE):
                for w in ("gate", "up", "down"):
                    for a in range(2):
                        release[pidx[(w, l, e, a)]] = (f"{w}{a}_done{l}", e + 1)

        TURN = [("gate", 0), ("gate", 1), ("up", 0), ("up", 1), ("down", 0), ("down", 1)]

        def part(eng, which, dst_, src, done, waits):
            for name, v in waits:
                eng.wait_ge(S(name), v)
            if which == 0:
                m = eng.activation(dst_[0], src, ACT.Copy)
            else:
                m = eng.tensor_tensor(dst_[1], src, dst_[0].bitcast(F32), ALU.subtract)
            m.then_inc(S(done), 1)

        def split(eng, which, p):
            if which == 0:
                waits = [release[p - SPLIT]] if p >= SPLIT else []
                eng.wait_ge(*landed(p))
            else:
                waits = [("hi_ready", p + 1)]
            part(eng, which, (wr[:, p % SPLIT, 0, :], wr[:, p % SPLIT, 1, :]), raw_at(raw_slot[p]),
                 ("hi_ready", "lo_ready")[which], waits)

        def split_turn(eng, which, l, n, i, base, q):
            p = base + 12 * i
            if which == 0:
                (w, a), d = TURN[(q - SPLIT) % 6], (q - SPLIT) // 6
                v = n + d + 1 - (1 if w == "down" else 0)
                sem_, v0 = landed(base)
                eng.wait_ge(sem_, v0 + (12 // RAW_MOE) * 16 * i)
                waits = [(f"{w}{a}_done{l}", v)]
            else:
                waits = [("hi_ready", p + 1)]
            part(eng, which, (wr[:, base % SPLIT, 0, :], wr[:, base % SPLIT, 1, :]), raw_at(raw_slot[base]),
                 ("hi_ready", "lo_ready")[which], waits)

        def split_further(eng, which, l, j, o):
            if which == 0:
                if o < 4:
                    waits = [(f"ov_first{l}", 64 * j + 64)]
                else:
                    waits = [(f"ov_down{l}", 32 * j + 32)]
                if o >= SPLIT:
                    w, a = TURN[o - SPLIT]
                    waits += [(f"{w}{a}_done{l}", j + NE + 1)]
            else:
                waits = [(f"ov_hi{l}", 6 * j + o + 1)]
            part(eng, which, (wr[:, o % SPLIT, 0, :], wr[:, o % SPLIT, 1, :]), ow[:, o % 4, :],
                 (f"ov_hi{l}", f"ov_lo{l}")[which], waits)

        def after_chunk(eng, which, w, l, c, last):
            p = pidx[(w, l, c, 0)] + SPLIT + last
            split(eng, which, p)

        def small(eng, which, flat, n):
            if which == 0:
                eng.activation(ws[:, 0, 0:n], flat, ACT.Copy).then_inc(S("ws_hi"), 1)
            else:
                eng.tensor_tensor(ws[:, 1, 0:n], flat, ws[:, 0, 0:n].bitcast(F32), ALU.subtract)\
                    .then_inc(S("ws_lo"), 1)

        @block.sync
        def _(sp):
            for t in range(NT):
                sp.dma_start(h[:, t, :], x[0, t * P:(t + 1) * P, :]).then_inc(S(f"x_loaded{t}"), 16)
            sp.wait_ge(S("zeroed"), 3)
            gw = a_w_in[0].rearrange("(k p) n -> p k n", p=P)[:, :, 3072:3080]
            sp.dma_start(w_gates[:, :, 0:HA], gw[:, :, 0:HA]).then_inc(S("gates_w"), 16)
            sp.dma_start(w_gates[:, :, 32:32 + HA], gw[:, :, HA:2 * HA]).then_inc(S("gates_w"), 16)
            as8 = lambda v: v.rearrange("(k p) -> k p", p=P)
            as16 = lambda v: v.rearrange("l (k p) -> (l k) p", p=P)
            for r, n_rows, v in ((0, 16, as16(norm_mix)), (16, 16, as16(norm_ffn)), (32, 8, as8(a_head_gain[0])),
                                 (40, 8, as8(kv_norm))):
                sp.dma_start(rows[r:r + n_rows, :], v).then_inc(S("rows_loaded"), 16)
            one = lambda v: v.rearrange("(a n) -> a n", a=1)
            for r, c, v in ((48, 0, one(kv_k_gain)), (48, 64, one(kv_k_gain)), (49, 0, b_q_gain), (49, 64, b_q_gain),
                            (50, 0, a_b_gate[:, 0:HA]), (50, 32, a_b_gate[:, HA:2 * HA]), (51, 0, one(kv_b_f))):
                sp.dma_start(rows[r:r + 1, c:c + v.shape[1]], v).then_inc(S("rows_loaded"), 16)

            def load(n):
                kind, l, i, a = seq[n]
                if before[n] is not None:
                    sp.wait_ge(S("lo_ready"), before[n] + 1)
                if n == pidx[("kv", 0, 2, 0)]:
                    sp.wait_ge(S("y_back3"), 16)
                if raw_slot[n] >= RAW and (before[n] is None or seq[before[n]][1] != l):
                    sp.wait_ge(S("logits"), NT * (l + 1))
                if n == pidx[("b_out", 0, 1, 0)]:
                    sp.wait_ge(S("fg_ready"), 2)
                    sp.dma_start(cd[:, :], cT).then_inc(S("stored"), 16)
                    sp.wait_ge(S("stored"), 16)
                    for hd in range(HB):
                        if hd >= 2:
                            sp.wait_ge(S("s_used"), NT * (hd - 1))
                        sp.dma_start(negc[:, hd % 2, :], cd[hd:hd + 1, :].broadcast_to([P, SEQ]))\
                            .then_inc(S(f"negc_in{hd % 2}"), 16)
                if kind == "b_out" and raw_slot[n] < 2 or n == pidx[("gate", 1, 0, 0)]:
                    sp.wait_ge(S("oT_ready"), 8)
                src = wv[kind][l, i, a] if kind in ("gate", "up", "down") else wv[kind][a, :, :, i * W:(i + 1) * W]
                sp.dma_start(kn(raw_at(raw_slot[n])), src).then_inc(landed(n)[0], 16)

            for n in range(pidx[("gate", 0, 2, 0)]):
                load(n)
            for l in range(2):
                n0 = pidx[("gate", l, 2, 0)]
                with sp.Fori(0, NE // 2 - 1) as i:
                    for q in range(12):
                        w, _, e, a = seq[n0 + q]
                        sp.wait_ge(S("lo_ready"), 12 * i + before[n0 + q] + 1)
                        sp.dma_start(kn(raw_at(raw_slot[n0 + q])), wv[w][l, 2 * i + e, a])\
                            .then_inc(landed(n0 + q)[0], 16)
                load(pidx[("down", l, NE - 1, 0)])
                load(pidx[("down", l, NE - 1, 1)])
                sp.wait_ge(S("ov_ready"), l + 1)
                n_ov = sp.value_load(ov[0:1, 0:1], min_val=0, max_val=OVMAX)
                with sp.If(n_ov > 0), sp.Fori(0, n_ov) as j:
                    sp.wait_ge(S(f"scattered{l}_0"), 16 * (j + NE // 2))
                    sp.wait_ge(S(f"scattered{l}_1"), NE // 2 * 16)
                    ex = sp.value_load(ov[0:1, bass.ds(j + 32, 1)], min_val=0, max_val=NE - 1)
                    for o, (w, a) in enumerate(TURN[:4]):
                        sp.dma_start(kn(ow[:, o, :]), wv[w][l, ex, a]).then_inc(S(f"ov_first{l}"), 16)
                    sp.wait_ge(S(f"ov_lo{l}"), 6 * j + 2)
                    for o, (w, a) in enumerate(TURN[4:]):
                        sp.dma_start(kn(ow[:, o, :]), wv[w][l, ex, a]).then_inc(S(f"ov_down{l}"), 16)
                if l == 0:
                    for n in range(pidx[("kv", 0, 0, 0)], pidx[("gate", 1, 2, 0)]):
                        load(n)
            for t in range(NT):
                sp.wait_ge(S("final_rows"), t + 1)
                sp.dma_start(out[0, t * P:(t + 1) * P, :], fo[:, t, :]).then_inc(S("stored"), 16)
            sp.wait_ge(S("stored"), 16 * (NT + 1))

        @block.gpsimd
        def _(pool):
            chain = [0]

            def link(ins):
                chain[0] += 1
                ins.then_inc(S("pool_step"), 1)
                pool.wait_ge(S("pool_step"), chain[0])

            pool.memset(ident[:, :], 0.0)
            pool.memset(mask_ts[:, :], 0.0)
            pool.memset(mask_st[:, :], 0.0)
            pool.memset(tri_bf[:, :], 1.0)
            pool.memset(ones_bf[:, :], 1.0)
            link(pool.memset(eps_col[:, :], EPS))
            pool.affine_select(out=ident[:, :], in_=ident[:, :], compare_op=ALU.not_equal, fill=1.0, base=0,
                               pattern=[[-1, P]], channel_multiplier=1)
            pool.affine_select(out=mask_ts[:, :], in_=mask_ts[:, :], compare_op=ALU.is_ge, fill=-BIG, base=0,
                               pattern=[[-1, P]], channel_multiplier=1)
            pool.affine_select(out=mask_st[:, :], in_=mask_st[:, :], compare_op=ALU.is_ge, fill=BIG, base=0,
                               pattern=[[1, P]], channel_multiplier=-1)
            pool.affine_select(out=tri_bf[:, :], in_=tri_bf[:, :], compare_op=ALU.is_gt, fill=0.0, base=0,
                               pattern=[[1, P]], channel_multiplier=-1)
            pool.iota(rc_i[:, 0:NB + 1], pattern=[[TILE, NB + 1]], base=0, channel_multiplier=0)
            pool.iota(rc_i[:, 7:11], pattern=[[-1, 4]], base=4, channel_multiplier=0)
            pool.iota(rc_i[:, 11:19], pattern=[[SEQ, 2], [P, NT]], base=0, channel_multiplier=0)
            pool.iota(rc_i[:, 19:27], pattern=[[0, 2 * NT]], base=1, channel_multiplier=1)
            pool.iota(rc_i[:, 27:123], pattern=[[1, TILE]], base=-TILE, channel_multiplier=0)\
                .then_inc(S("consts"), 1)
            for l in range(2):
                pool.wait_ge(S("num_used" if l == 0 else "oT_ready"), NT * HA if l == 0 else 8)
                pool.dma_start(gain_bc, norm_ffn[l:l + 1, :].broadcast_to([P, D])).then_inc(S("gain_bc"), 16)
                pool.wait_ge(S("gain_bc"), 16 * (l + 1))
                for t in range(NT):
                    pool.wait_ge(S("ffn_scaled"), NT * l + t + 1)
                    pool.tensor_tensor(stage[:, t, :], stage[:, t, :], gain_bc, ALU.mult).then_inc(S("ffn_rows"), 1)
                pool.iota(further_i[:, 0:NOV], pattern=[[0, NE], [TILE, NB - 1]], base=TILE, channel_multiplier=0)
                pool.iota(further_i[:, NOV:2 * NOV], pattern=[[NB, NE], [1, NB - 1]], base=1, channel_multiplier=0)
                pool.iota(further_i[:, 2 * NOV:3 * NOV], pattern=[[1, NE], [0, NB - 1]], base=0, channel_multiplier=0)
                pool.iota(further_i[:, 3 * NOV:3 * NOV + OVMAX], pattern=[[1, OVMAX]], base=1, channel_multiplier=0)\
                    .then_inc(S("further_consts"), 1)
                pool.wait_ge(S("rows_stored"), 16 * NT * (l + 1))
                pool.wait_ge(S("tok_ready"), 2 * l + 1)

                def gather(idx, par):
                    pool.indirect_dma_start(xg[0:TILE, par, :], None, xd[l], bass.IndirectOffsetOnAxis(ap=idx, axis=0),
                                            bounds_check=SEQ - 1, oob_is_err=False).then_inc(S(f"gathered{l}_{par}"), 16)

                def scatter(idx, par):
                    pool.indirect_dma_start(yd[l], bass.IndirectOffsetOnAxis(ap=idx, axis=0), yb[0:TILE, par, :], None,
                                            bounds_check=2 * SEQ - 1, oob_is_err=False)\
                        .then_inc(S(f"scattered{l}_{par}"), 16)

                gather(tok[:, 0:1], 0)
                gather(tok[:, NB:NB + 1], 1)
                for e in range(NE):
                    if e + 2 < NE:
                        pool.wait_ge(S(f"xg_turned{l}"), e + 1)
                        gather(tok[:, NB * (e + 2):NB * (e + 2) + 1], e % 2)
                    if e == 0:
                        pool.wait_ge(S("tok_ready"), 2 * l + 2)
                    pool.wait_ge(S(f"y0_ready{l}"), e + 1)
                    pool.wait_ge(S(f"y1_ready{l}"), e + 1)
                    scatter(ydst[:, NB * e:NB * e + 1], e % 2)
                n_ov = pool.value_load(ov[0:1, 0:1], min_val=0, max_val=OVMAX)

                def hold(q):
                    pool.tensor_tensor(held[:, 4 * l + q:4 * l + q + 1], ones_col[:, :], ones_col[:, :], ALU.mult)\
                        .then_inc(S(f"pool_held{l}"), 1)

                hold(3)
                with pool.If(n_ov > 0), pool.Fori(0, n_ov) as j:
                    pool.wait_ge(S(f"fix_ready{l}"), j + 1)
                    hold(0)
                    gather(fix[:, 0:1], 0)
                    pool.wait_ge(S(f"y0_ready{l}"), j + NE + 1)
                    hold(1)
                    pool.wait_ge(S(f"y1_ready{l}"), j + NE + 1)
                    hold(2)
                    scatter(fix[:, 1:2], 0)
                pool.wait_ge(S("tiles_stored"), l + 1)
                if l == 1:
                    pool.dma_start(nf, norm_final.rearrange("(a d) -> a d", a=1).broadcast_to([P, D]))\
                        .then_inc(S("gain_bc"), 16)
                for t in range(NT):
                    pool.dma_start(yy[:, 2 * t:2 * t + 2, :],
                                   yd[l].rearrange("(k t p) d -> t p k d", k=2, p=P)[t]).then_inc(S(f"y_back{t}"), 16)
            pool.wait_ge(S("gain_bc"), 48)

        @block.tensor
        def _(pe):
            pe.wait_ge(S("consts"), 1)
            pe.wait_ge(S("zeroed"), 3)
            pe.wait_ge(S("rows_loaded"), 16 * ROWS_DMAS)
            pe.transpose(ps[:, 0, 0:52], rows, ident[0:52, 0:52]).then_inc(S("gains_turned"), 1)

            def turn_normed(j, src, waits=True):
                for t in range(NT):
                    if waits:
                        pe.wait_ge(S("xn_ready"), NT * waits_at[j] + t + 1)
                    for k in range(KD):
                        m = pe.transpose(ps[:, k, t * P:(t + 1) * P], src[:, t, k * P:(k + 1) * P], ident[:, :])
                        if t == NT - 1:
                            m.then_inc(S("xn_turned"), 1)

            waits_at = [0, 1, 1]

            def mm3(outp, a, b, start, stop):
                pe.matmul(outp, a[0], b[0], start=start, stop=False)
                pe.matmul(outp, a[0], b[1], start=False, stop=False)
                return pe.matmul(outp, a[1], b[0], start=False, stop=stop)

            def xr_at(k, cols=slice(0, SEQ)):
                return xh[:, k, cols], xl[:, k, cols]

            def small_group(which, width, outp, done, j):
                pe.wait_ge(S("ws_lo"), which + 1)
                for k in range(KD):
                    pe.wait_ge(S("xT_lo"), KD * j + k + 1)
                    m = mm3(outp, (ws[:, 0, width * k:width * k + P], ws[:, 1, width * k:width * k + P]), xr_at(k),
                            k == 0, k == KD - 1)
                m.then_inc(S(done), 1)

            def piece(n):
                pe.wait_ge(S("lo_ready"), n + 1)
                return kn(wr[:, n % SPLIT, 0, :]), kn(wr[:, n % SPLIT, 1, :])

            def chunk(w, c, outs, weight_first, done, before_bank=None, before_k=None, after=None):
                n = pidx[(w, 0, c, 0)]
                for a in range(2):
                    wp = piece(n + a)
                    for i in range(4):
                        if a == 0 and before_bank:
                            before_bank(i)
                        for kk in range(KH):
                            k = KH * a + kk
                            if before_k and i == 0:
                                before_k(k)
                            if weight_first:
                                cols = slice(i * P, (i + 1) * P)
                                m = mm3(outs[i], (wp[0][:, kk, cols], wp[1][:, kk, cols]), xr_at(k),
                                        k == 0, k == KD - 1)
                            else:
                                m = mm3(outs[i], xr_at(k, slice(i * P, (i + 1) * P)), (wp[0][:, kk, :], wp[1][:, kk, :]),
                                        k == 0, k == KD - 1)
                        if a == 0 and i == 3:
                            m.then_inc(S("half_used"), 1)
                        if a == 1:
                            m.then_inc(S(done), 1)
                            if after:
                                after(i)

            def bank_free(g, mixer):
                if g >= 6:
                    eng = EVAC[mixer][g - 6]
                    pe.wait_ge(S(f"{eng}_evac{mixer}"), EVAC[mixer][:g - 5].count(eng))

            pe.wait_ge(S("gains_ready"), 1)
            turn_normed(0, stage)
            small_group(0, 36, ps[:, 0, :], "projA", 0)

            def between_a(g):
                if g == 12:
                    pe.wait_ge(S("um_ready"), 1)
                    for t in range(NT):
                        m = pe.transpose(ps[:, 6, t * 36:(t + 1) * 36], g_um[:, t * P:(t + 1) * P], ident[0:36, 0:36])
                    m.then_inc(S("um_turned"), 1)
                if 13 <= g < 13 + HA:
                    if g > 13:
                        pe.wait_ge(S("m_spread_used"), g - 13)
                    pe.matmul(ps[:, 7, :], ident[0:4, g - 13:g - 12].broadcast_to([4, P]), g_m,
                              start=True, stop=True).then_inc(S("m_spread"), 1)

            for c in range(6):
                g0 = 4 * c + 1
                chunk("a_in", c, [ps[:, (g0 + i) % 6, :] for i in range(4)], c < 2, "projA",
                      before_bank=lambda i: bank_free(g0 + i, "A"), after=lambda i: between_a(g0 + i))
            pe.wait_ge(S("D_evacA"), EVAC["A"].count("D"))
            pe.wait_ge(S("A_evacA"), EVAC["A"].count("A"))

            def scores_a(hd):
                for i in range(NT):
                    if hd:
                        pe.wait_ge(S("pt_ready"), NT * (hd - 1) + i + 1)
                    pe.matmul(ps[:, i, 0:DW[i]], kT[:, hd, i * P:(i + 1) * P], qT[:, hd, i * P:], start=True,
                              stop=True).then_inc(S("st_ready"), 1)

            pe.wait_ge(S("m_spread_used"), HA)
            scores_a(0)
            for hd in range(HA):
                if hd + 1 < HA:
                    scores_a(hd + 1)
                pe.wait_ge(S("pt_ready"), NT * (hd + 1))
                for j in range(NT):
                    if hd:
                        pe.wait_ge(S("num_used"), NT * (hd - 1) + j + 1)
                    for i in range(j + 1):
                        o = DO[i] + (j - i) * P
                        m = pe.matmul(ps[:, 4 + j, 0:DV + 1], dec[:, hd, o:o + P], va[:, i, hd, :],
                                      start=(i == 0), stop=(i == j))
                    m.then_inc(S("num_ready"), 1)
            for k in range(KD):
                pe.wait_ge(S("hg_ready"), k // 2 + 1)
                if k >= NT:
                    pe.wait_ge(S("num_used"), NT * (HA - 1) + k - NT + 1)
                for t in range(NT):
                    m = pe.transpose(ps[:, k, t * P:(t + 1) * P], so[:, t, k * P:(k + 1) * P], ident[:, :])
                m.then_inc(S("hg_turned"), 1)

            def out_proj(w, done, x_there, l):
                def turn_rows(t):
                    pe.wait_ge(S("h_final"), NT * (2 * l + 1) - NT + t + 1)
                    for k in range(KD):
                        m = pe.transpose(ps[:, 2 * t + k // 4, (k % 4) * P:(k % 4 + 1) * P],
                                         h[:, t, k * P:(k + 1) * P], ident[:, :])
                    m.then_inc(S("h_turned"), 1)

                for c in range(2):
                    chunk(w, c, [ps[:, NT * c + t, :] for t in range(NT)], False, done,
                          before_k=x_there if c == 0 else None,
                          after=(lambda i: turn_rows(i - 2) if i >= 2 else None) if c == 1 else None)
                turn_rows(2)
                turn_rows(3)

            out_proj("a_out", "outA", lambda k: pe.wait_ge(S("hgT_lo"), k + 1), 0)

            def moe(l):
                pe.wait_ge(S("router_w"), 2)
                for t in range(NT):
                    pe.wait_ge(S("hT_ready"), NT * l + t + 1)
                    for k in range(KD):
                        m = pe.matmul(ps[:, 2 * t, 0:NG + NE], hT[:, t, k, :], w_rt[:, l, k, :], start=(k == 0),
                                      stop=(k == KD - 1))
                    m.then_inc(S("logits"), 1)
                pe.wait_ge(S("sel_ready"), l + 1)
                selv = sel_bf.rearrange("p (t e) -> p t e", t=NT)
                for t in range(NT):
                    for s in range(t + 1):
                        m = pe.matmul(ps[:, 1, t * NE:(t + 1) * NE], tri_bf[:, :] if s == t else ones_bf[:, :],
                                      selv[:, s, :], start=(s == 0), stop=(s == t))
                m.then_inc(S("places"), 1)
                for t in range(NT):
                    m = pe.matmul(ps[0:1, 7, 0:NE], ones_bf[:, 0:1], selv[:, t, :], start=(t == 0), stop=(t == NT - 1))
                m.then_inc(S("places"), 1)
                pe.wait_ge(S("oh_ready"), l + 1)
                for c in range(2 * NT):
                    for q in range(2):
                        m = pe.matmul(ps[0:TILE, 5, 0:NE * NB], oh_place[:, c, :], oh_tile[q][:, c, :],
                                      start=(c + q == 0), stop=(c == 2 * NT - 1 and q == 1))
                m.then_inc(S("lists"), 1)
                pe.wait_ge(S("tok_ready"), 2 * l + 1)

                def turn_x(n, nth_of_buffer, par):
                    pe.wait_ge(S(f"gathered{l}_{par}"), 16 * (nth_of_buffer + 1))
                    if not isinstance(n, int) or n:
                        pe.wait_ge(S(f"xg_lo{l}"), n)
                    for k in range(KD):
                        m = pe.transpose(ps[:, 2 + k // 4, (k % 4) * P:(k % 4 + 1) * P],
                                         xg[:, par, k * P:(k + 1) * P], ident[:, :])
                    m.then_inc(S(f"xg_turned{l}"), 1)

                def gate_up(n, par, wait_piece, slot0):
                    past = not isinstance(n, int) or n
                    pe.wait_ge(S(f"xg_lo{l}"), n + 1)
                    for q, (w, a) in enumerate(TURN[:4]):
                        if past and a == 0:
                            pe.wait_ge(S(f"{('sg', 'hn')[q // 2]}_ready{l}"), n)
                        wait_piece(q)
                        wp = [kn(wr[:, (slot0 + q) % SPLIT, b, :]) for b in range(2)]
                        for kk in range(KH):
                            k = KH * a + kk
                            m = mm3(ps[:, q // 2, :], (xgr[par][0][:, k, :], xgr[par][1][:, k, :]),
                                    (wp[0][:, kk, :], wp[1][:, kk, :]), k == 0, k == KD - 1)
                        m.then_inc(S(f"{w}{a}_done{l}"), 1)

                def turn_h(n):
                    pe.wait_ge(S(f"hn_ready{l}"), n + 1)
                    if not isinstance(n, int) or n:
                        pe.wait_ge(S(f"h_lo{l}"), n)
                    for k in range(KE):
                        m = pe.transpose(ps[:, 4, k * P:(k + 1) * P], hn[:, k * P:(k + 1) * P], ident[:, :])
                    m.then_inc(S(f"hn_turned{l}"), 1)

                def down(n, wait_piece, slot0):
                    pe.wait_ge(S(f"h_lo{l}"), n + 1)
                    for a in range(2):
                        if not isinstance(n, int) or n:
                            pe.wait_ge(S(f"y{a}_ready{l}"), n)
                        wait_piece(4 + a)
                        wp = [kn(wr[:, (slot0 + a) % SPLIT, b, :]) for b in range(2)]
                        for k in range(KE):
                            m = mm3(ps[:, 5 + a, :], (hr[0][:, k * P:(k + 1) * P], hr[1][:, k * P:(k + 1) * P]),
                                    (wp[0][:, k, :], wp[1][:, k, :]), k == 0, k == KE - 1)
                        m.then_inc(S(f"down{a}_done{l}"), 1)

                turn_x(0, 0, 0)
                p0 = pidx[("gate", l, 0, 0)]
                gate_up(0, 0, lambda q: pe.wait_ge(S("lo_ready"), p0 + q + 1), p0)
                turn_x(1, 0, 1)
                turn_h(0)

                def turn(n, i, par, more=True):
                    base = pidx[("gate", l, par, 0)] if par else pidx[("gate", l, 2, 0)] - 12
                    there = lambda q: pe.wait_ge(S("lo_ready"), 12 * i + base + q + 1)
                    gate_up(n, par, there, base)
                    if more:
                        turn_x(n + 1, i + par, 1 - par)
                    down(n - 1, there, base + 4)
                    turn_h(n)

                turn(1, 0, 1)
                with pe.Fori(1, NE // 2 - 1) as i:
                    turn(2 * i, i, 0)
                    turn(2 * i + 1, i, 1)
                turn(NE - 2, NE // 2 - 1, 0)
                turn(NE - 1, NE // 2 - 1, 1, False)
                pl = pidx[("down", l, NE - 1, 0)]
                down(NE - 1, lambda q: pe.wait_ge(S("lo_ready"), pl + q - 4 + 1), pl)
                pe.wait_ge(S("ov_ready"), l + 1)
                n_ov = pe.value_load(ov[0:1, 0:1], min_val=0, max_val=OVMAX)
                with pe.If(n_ov > 0), pe.Fori(0, n_ov) as j:
                    turn_x(j + NE, j + NE // 2, 0)
                    there = lambda q: pe.wait_ge(S(f"ov_lo{l}"), 6 * j + q + 1)
                    gate_up(j + NE, 0, there, 0)
                    turn_h(j + NE)
                    down(j + NE, there, 4)

            moe(0)

            turn_normed(1, stage_b)
            small_group(1, HB, ps[:, 0, :], "projB", 1)

            def turn_nat(n):
                pe.wait_ge(S("D_evacB"), n + 1 if n < 8 else n + 9)
                if n >= 2:
                    pe.wait_ge(S("headsT_ready"), n - 1)
                for r in range(4):
                    m = pe.transpose(ps[:, 6 + n % 2, r * P:(r + 1) * P], nat[:, n % 2, r * P:(r + 1) * P], ident[:, :])
                m.then_inc(S("nat_turned"), 1)

            pend = []

            def between_b(g):
                w, c, i = B_GROUPS[g]
                if pend and pend[0][0] + 2 <= g:
                    turn_nat(pend.pop(0)[1])
                if w in "kq":
                    pend.append((g, (0 if w == "k" else 8) + (c % 4) * 4 + i))

            for c in range(4):
                g0 = 4 * c + 1
                chunk("kv", c, [ps[:, (g0 + i) % 6, :] for i in range(4)], False, "projB",
                      before_bank=lambda i: bank_free(g0 + i, "B"), after=lambda i: between_b(g0 + i))
            pe.wait_ge(S("D_evacB"), 16)
            pe.wait_ge(S("headsT_ready"), 8)
            turn_normed(2, stage_b, waits=False)
            for c in range(2):
                g0 = 4 * c + 17
                chunk("b_in", c, [ps[:, (g0 + i) % 6, :] for i in range(4)], False, "projB",
                      before_bank=lambda i: bank_free(g0 + i, "B"),
                      before_k=(lambda k: pe.wait_ge(S("xT_lo"), KD * 3)) if c == 0 else None,
                      after=lambda i: between_b(g0 + i))
            for _, n in pend:
                turn_nat(n)
            for c in range(2):
                chunk("b_in", 2 + c, [ps[:, i, :] for i in range(4)], True, "ogB",
                      before_bank=(lambda i: pe.wait_ge(S("D_evacB"), 24)) if c == 0 else
                      (lambda i: pe.wait_ge(S("og_ready"), i + 1)))
            pe.wait_ge(S("og_ready"), 8)
            pe.wait_ge(S("headsT_ready"), 16)
            pe.wait_ge(S("D_evacB"), EVAC["B"].count("D"))

            steps = [(hd, j) for hd in range(HB) for j in FOX_TILES]

            def score(n):
                hd, j = steps[n]
                o, r = 64 * (hd % 2), hd // 2
                if n >= 3:
                    pe.wait_ge(S("s_used"), n - 2)
                pe.matmul(ps[:, score_bank(n), 0:(j + 1) * P], qTb[o:o + DH, r, j * P:(j + 1) * P],
                          kTb[o:o + DH, r, 0:(j + 1) * P], start=True, stop=True).then_inc(S("s_ready"), 1)

            def turn_p(n):
                hd, j = steps[n]
                pe.wait_ge(S("p_ready"), n + 1)
                if n >= 3:
                    pe.wait_ge(S("pT_ready"), n - 2)
                for i in range(j + 1):
                    m = pe.transpose(ps[:, pT_bank(n), i * P:(i + 1) * P], pbuf[:, n % 4, i * P:(i + 1) * P],
                                     ident[:, :])
                m.then_inc(S("p_turned"), 1)

            def attend(n):
                hd, j = steps[n]
                o, r = 64 * (hd % 2), hd // 2
                pe.wait_ge(S("pT_ready"), n + 1)
                if hd % 2 == 0 and n % NT == 0 and r >= 2:
                    pe.wait_ge(S("oT_ready"), r - 1)
                for i in range(j + 1):
                    m = pe.matmul(ps[o:o + DH, 4 + r % 2, j * P:(j + 1) * P], vb[:, i, hd * DH:(hd + 1) * DH],
                                  ptb[:, n % 4, i * P:(i + 1) * P], start=(i == 0), stop=(i == j))
                m.then_inc(S("o_ready"), 1)

            for n in range(len(steps) + ATTEND_LAG):
                if n < len(steps):
                    score(n)
                if 0 <= n - TURN_LAG < len(steps):
                    turn_p(n - TURN_LAG)
                if n >= ATTEND_LAG:
                    attend(n - ATTEND_LAG)
            out_proj("b_out", "outB", lambda k: pe.wait_ge(S("oT_lo"), k + 1), 1)
            moe(1)

        @block.vector
        def _(dve):
            chain = [0]

            def link(ins):
                chain[0] += 1
                ins.then_inc(S("dve_step"), 1)
                dve.wait_ge(S("dve_step"), chain[0])

            dve.memset(rows, 0.0).then_inc(S("zeroed"), 1)
            dve.memset(w_gates[:, :, :], 0.0).then_inc(S("zeroed"), 1)
            dve.memset(ones_col[:, :], 1.0)
            dve.memset(ws[:, :, :].bitcast(F32), 0.0).then_inc(S("zeroed"), 1)
            dve.wait_ge(S("gains_turned"), 1)
            link(dve.tensor_copy(gains[:, :], ps[:, 0, 0:52]))
            dve.wait_ge(S("consts"), 1)
            dve.tensor_copy(rc[:, :], rc_i)
            link(dve.tensor_scalar(gate15[:, :], gains[:, 50:51], 1.0 / CAP, None, ALU.mult))
            dve.tensor_copy(stat[:, 95:96], gate15[:, :]).then_inc(S("gains_ready"), 1)

            def norm_tile(i, t, rows_):
                dve.wait_ge(S("rms_tile"), NT * i + t + 1)
                link(dve.reciprocal(stat[:, 4 + t:5 + t], stat[:, t:t + 1]))
                dve.tensor_scalar(rows_[:, t, :], h[:, t, :], stat[:, 4 + t:5 + t], None, ALU.mult)\
                    .then_inc(S("xn_ready"), 1)

            def low_xT(j, col):
                for k in range(KD):
                    dve.wait_ge(S("xT_hi"), KD * j + k + 1)
                    hi = xh[:, k, :].bitcast(F32)
                    m = dve.scalar_tensor_tensor(out=xl[:, k, :], in0=ps[:, k, :],
                                                 scalar=gains[:, col + k:col + k + 1], in1=hi, op0=ALU.mult,
                                                 op1=ALU.subtract)
                    m.then_inc(S("xT_lo"), 1)

            for t in range(NT):
                norm_tile(0, t, stage)
            dve.wait_ge(S("ws_hi"), 1)
            small(dve, 1, w_gates[:, :, :].rearrange("p k n -> p (k n)"), KD * 36)
            split(dve, 1, 0)
            low_xT(0, 0)
            for p in range(1, SPLIT):
                split(dve, 1, p)
            for t in range(NT):
                m = dve.memset(va[:, t, :, DV:DV + 1], 1.0)
            link(m)
            link(dve.memset(g_um, 0.0))

            def evac_a(g):
                w, c, i = A_GROUPS[g]
                dve.wait_ge(S("projA"), g + 1)
                if w == "q":
                    m = dve.tensor_copy(qT[:, i, :], ps[:, g % 6, :])
                elif w == "k":
                    m = dve.tensor_scalar(kT[:, i, :], ps[:, g % 6, :], DQK ** -0.5, None, ALU.mult)
                else:
                    m = dve.tensor_copy(va[:, i, 2 * (c - 2):2 * (c - 2) + 2, 0:DV],
                                        ps[:, g % 6, :].rearrange("p (h v) -> p h v", h=2))
                m.then_inc(S("D_evacA"), 1)

            def chunk_a(c):
                after_chunk(dve, 1, "a_in", 0, c, 0)
                for g in range(4 * c + 1, 4 * c + 5):
                    evac_a(g)
                after_chunk(dve, 1, "a_in", 0, c, 1)

            chunk_a(0)
            dve.wait_ge(S("gates_ready"), 1)
            one4 = ones_col[0:4, 0:1].broadcast_to([4, SEQ])
            link(dve.tensor_tensor_scan(g_b, one4, g_lf, 0.0, ALU.mult, ALU.subtract))
            link(dve.scalar_tensor_tensor(out=g_um[0:4, :], in0=g_t[0:4, :], scalar=CAP, in1=g_b, op0=ALU.mult,
                                          op1=ALU.subtract))
            link(dve.tensor_tensor_scan(g_m, g_um[0:4, :], g_um[0:4, :], 0.0, ALU.max, ALU.max))
            dve.tensor_tensor(g_um[32:36, :], g_b, g_m, ALU.add).then_inc(S("um_ready"), 1)
            dve.wait_ge(S("rt_w"), 128)
            for l in range(2):
                dve.tensor_tensor(w_rt[:, l, :, :], w_rt[:, l, :, :],
                                  gains[:, 16 + KD * l:16 + KD * (l + 1)].unsqueeze(2).broadcast_to([P, KD, NG + NE]),
                                  ALU.mult).then_inc(S("router_w"), 1)
            chunk_a(1)
            chunk_a(2)
            dve.wait_ge(S("um_turned"), 1)
            umn = arena[:, UMN:UMN + 144].rearrange("p (t c) -> p t c", t=NT)
            dve.tensor_copy(arena[:, UMN:UMN + 144], ps[:, 6, 0:144]).then_inc(S("umn_ready"), 1)
            after_chunk(dve, 1, "a_in", 0, 3, 0)
            for hd in range(HA):
                evac_a(13 + hd)
                dve.wait_ge(S("m_spread"), hd + 1)
                for i in range(NT):
                    if i < NT - 1:
                        dve.tensor_copy(dec[:, hd, DO[i] + P:DO[i] + DW[i]], ps[:, 7, (i + 1) * P:])
                    m = dve.tensor_tensor(dec[:, hd, DO[i]:DO[i] + P], ps[:, 7, i * P:(i + 1) * P], mask_st[:, :],
                                          ALU.add)
                m.then_inc(S("m_spread_used"), 1)
            after_chunk(dve, 1, "a_in", 0, 3, 1)
            for c in (4, 5):
                after_chunk(dve, 1, "a_in", 0, c, 0)
                after_chunk(dve, 1, "a_in", 0, c, 1)

            def weigh(hd):
                dve.wait_ge(S("dec_ready"), NT * (hd + 1))
                for i in range(NT):
                    dve.wait_ge(S("st_ready"), NT * hd + i + 1)
                    dd = dec[:, hd, DO[i]:DO[i] + DW[i]]
                    dve.tensor_tensor(dd, ps[:, i, 0:DW[i]], dd, ALU.mult).then_inc(S("pt_ready"), 1)

            den_of = lambda hd: stat[:, 20:24] if hd % 2 else stat[:, 64:68]
            sum_of = lambda hd: stat[:, 84:88] if hd % 2 else stat[:, 72:76]
            rms_of = lambda hd: stat[:, 24:28] if hd % 2 else stat[:, 68:72]

            def take_num(hd):
                for j in range(NT):
                    dve.wait_ge(S("num_squared"), NT * hd + j + 1)
                    m = dve.tensor_copy(stat[:, 8 + j:9 + j], ps[:, 4 + j, DV:DV + 1])
                    s = so[:, j, hd * DV:(hd + 1) * DV]
                    dve.tensor_tensor(s, ps[:, 4 + j, 0:DV], s, ALU.mult).then_inc(S("num_used"), 1)
                dve.wait_ge(S("num_used"), NT * (hd + 1))
                link(dve.scalar_tensor_tensor(out=stat[:, 12:16], in0=stat[:, 8:12], scalar=-1.0, in1=stat[:, 8:12],
                                              op0=ALU.mult, op1=ALU.max))
                link(dve.tensor_tensor(stat[:, 16:20], stat[:, 12:16], stat[:, 32 + 4 * hd:36 + 4 * hd], ALU.max))
                link(dve.reciprocal(den_of(hd), stat[:, 16:20]))
                link(dve.tensor_tensor(sum_of(hd), sum_of(hd), den_of(hd), ALU.mult))
                dve.tensor_tensor(sum_of(hd), sum_of(hd), den_of(hd), ALU.mult).then_inc(S("hsum_ready"), 1)

            def norm_head(hd):
                dve.wait_ge(S("hrms_ready"), hd + 1)
                link(dve.reciprocal(stat[:, 28:32], rms_of(hd)))
                link(dve.tensor_tensor(stat[:, 28:32], stat[:, 28:32], den_of(hd), ALU.mult))
                for j in range(NT):
                    s = so[:, j, hd * DV:(hd + 1) * DV]
                    m = dve.tensor_scalar(s, s, stat[:, 28 + j:29 + j], None, ALU.mult)
                m.then_inc(S("hg_ready"), 1)
                dve.wait_ge(S("hg_ready"), hd + 1)

            dve.wait_ge(S("em_ready"), 1)
            weigh(0)
            for hd in range(HA):
                if hd + 1 < HA:
                    weigh(hd + 1)
                take_num(hd)
                if hd:
                    norm_head(hd - 1)
            norm_head(HA - 1)
            for k in range(KD):
                dve.wait_ge(S("hgT_hi"), k + 1)
                dve.scalar_tensor_tensor(out=xl[:, k, :], in0=ps[:, k, :], scalar=gains[:, 32 + k:33 + k],
                                         in1=xh[:, k, :].bitcast(F32), op0=ALU.mult, op1=ALU.subtract)\
                    .then_inc(S("hgT_lo"), 1)

            def take_rows(l, t):
                dve.wait_ge(S("h_turned"), NT * l + t + 1)
                dve.tensor_copy(hT[:, t, :, :].rearrange("p (a k) c -> p a (k c)", a=2), ps[:, 2 * t:2 * t + 2, :])\
                    .then_inc(S("hT_ready"), 1)

            def residual(l, w, done):
                for c in range(2):
                    after_chunk(dve, 1, w, 0, c, 0)
                    for t in range(NT):
                        dve.wait_ge(S(done), NT * c + t + 1)
                        hh = h[:, t, c * 512:(c + 1) * 512]
                        m = dve.tensor_tensor(hh, hh, ps[:, NT * c + t, :], ALU.add)
                        if c == 1:
                            m.then_inc(S("h_final"), 1)
                            if t == NT - 1:
                                take_rows(l, 0)
                    if c == 0:
                        after_chunk(dve, 1, w, 0, c, 1)
                for t in range(1, NT):
                    take_rows(l, t)

            residual(0, "a_out", "outA")

            def first_of_max(v, mx, oh):
                link(dve.tensor_reduce(mx, v, AX.X, ALU.max))
                link(dve.tensor_tensor(oh, v, mx.unsqueeze(2).broadcast_to([P, NT, 4]), ALU.is_ge))
                link(dve.tensor_tensor(oh, oh, prio.unsqueeze(1).broadcast_to([P, NT, 4]), ALU.mult))
                link(dve.tensor_reduce(stat[:, 60:64], oh, AX.X, ALU.max))
                link(dve.tensor_tensor(oh, oh, stat[:, 60:64].unsqueeze(2).broadcast_to([P, NT, 4]), ALU.is_ge))

            def moe(l, then):
                dve.wait_ge(S("rms"), l + 1)
                dve.reciprocal(stat[:, 4:8], stat[:, 0:4]).then_inc(S("rstd_ready"), 1)
                dve.wait_ge(S("rstd_ready"), l + 1)
                dve.wait_ge(S("rt_w"), 128)
                for t in range(NT):
                    dve.wait_ge(S("logits"), NT * l + t + 1)
                    m = dve.scalar_tensor_tensor(out=L[:, t, :], in0=ps[:, 2 * t, 0:NG + NE], scalar=stat[:, 4 + t:5 + t],
                                                 in1=rbias[:, l, :], op0=ALU.mult, op1=ALU.add)
                link(m)
                Lg, Le = L[:, :, 0:4], L[:, :, 4:20].rearrange("p t (g e) -> p t g e", g=NG)
                oh1, oh2 = oh12[:, 0], oh12[:, 1]
                first_of_max(Lg, stat[:, 40:44], ohg)
                dve.tensor_tensor(gd, Lg, stat[:, 40:44].unsqueeze(2).broadcast_to([P, NT, 4]), ALU.subtract)\
                    .then_inc(S("gd_ready"), 1)
                p4 = prod[:, 0:64].rearrange("p (t g e) -> p t g e", t=NT, g=NG)
                link(dve.tensor_tensor(p4, Le, ohg.unsqueeze(3).broadcast_to([P, NT, NG, EG]), ALU.mult))
                link(dve.tensor_reduce(esel, prod[:, 0:64].rearrange("p (t g e) -> p t e g", t=NT, g=NG), AX.X, ALU.add))
                first_of_max(esel, stat[:, 44:48], oh1)
                link(dve.scalar_tensor_tensor(out=tmp4, in0=oh1, scalar=-BIG, in1=esel, op0=ALU.mult, op1=ALU.add))
                first_of_max(tmp4, stat[:, 48:52], oh2)
                dve.tensor_tensor(stat[:, 52:56], stat[:, 48:52], stat[:, 44:48], ALU.subtract)\
                    .then_inc(S("gd_ready"), 1)
                for k, oh in enumerate((oh1, oh2)):
                    o4 = oh_e[:, 64 * k:64 * k + 64].rearrange("p (t g e) -> p t g e", t=NT, g=NG)
                    m = dve.tensor_tensor(o4, ohg.unsqueeze(3).broadcast_to([P, NT, NG, EG]),
                                          oh.unsqueeze(2).broadcast_to([P, NT, NG, EG]), ALU.mult)
                link(m)
                dve.tensor_tensor(sel_bf, oh_e[:, 0:64], oh_e[:, 64:128], ALU.add).then_inc(S("sel_ready"), 1)
                dve.wait_ge(S("places"), 2 * l + 1)
                link(dve.tensor_tensor(prod.rearrange("p (k c) -> p k c", k=2), oh_e.rearrange("p (k c) -> p k c", k=2),
                                       ps[:, 1, 0:64].unsqueeze(1).broadcast_to([P, 2, 64]), ALU.mult))
                link(dve.tensor_reduce(stat[:, 8:16], prod.rearrange("p (c e) -> p c e", e=NE), AX.X, ALU.add))
                link(dve.tensor_tensor(reach, stat[:, 8:16].unsqueeze(2).broadcast_to([P, 2 * NT, NB + 1]),
                                       edges.unsqueeze(1).broadcast_to([P, 2 * NT, NB + 1]), ALU.is_ge))
                link(dve.tensor_reduce(stat[:, 16:24], reach, AX.X, ALU.add))
                link(dve.scalar_tensor_tensor(out=stat[:, 24:32], in0=stat[:, 16:24], scalar=-float(TILE),
                                              in1=stat[:, 8:16], op0=ALU.mult, op1=ALU.add))
                link(dve.tensor_tensor(oh_b[:, :, 0:NB], reach[:, :, 0:NB], reach[:, :, 1:NB + 1], ALU.subtract))
                for q, code in enumerate((code_hi, code_lo)):
                    dve.tensor_tensor(oh_bc[q], oh_b[:, :, 0:NB], code.unsqueeze(2).broadcast_to([P, 2 * NT, NB]), ALU.mult)
                link(dve.tensor_tensor(oh_place, place.unsqueeze(1).broadcast_to([P, 2 * NT, TILE]),
                                       stat[:, 24:32].unsqueeze(2).broadcast_to([P, 2 * NT, TILE]), ALU.is_equal))
                for q in range(2):
                    m = dve.tensor_tensor(oh_tile[q].rearrange("p c (e b) -> p c e b", e=NE),
                                          oh_e.rearrange("p (c e) -> p c e", e=NE).unsqueeze(3)
                                          .broadcast_to([P, 2 * NT, NE, NB]),
                                          oh_bc[q].unsqueeze(2).broadcast_to([P, 2 * NT, NE, NB]), ALU.mult)
                m.then_inc(S("oh_ready"), 1)
                dve.wait_ge(S("ge_ready"), 2 * l + 2)
                link(dve.tensor_reduce(stat[:, 64:68], ge, AX.X, ALU.add))
                link(dve.tensor_scalar(stat[:, 68:72], stat[:, 56:60], 1.0, None, ALU.add))
                dve.wait_ge(S("lists"), l + 1)
                link(dve.tensor_copy(cfull, ps[0:TILE, 5, 0:NE * NB]))
                link(dve.tensor_scalar(cneg, cfull, float(SEQ + 1), -float(SEQ), ALU.is_ge, ALU.mult))
                link(dve.scalar_tensor_tensor(out=ctok, in0=cfull, scalar=-1.0, in1=cneg, op0=ALU.add, op1=ALU.add))
                link(dve.tensor_scalar(ctok, ctok, 0.0, None, ALU.max))
                dve.tensor_copy(tok[:, :], ctok).then_inc(S("tok_ready"), 1)
                link(dve.tensor_scalar(cneg, cfull, 1.0, float(NOCODE), ALU.is_lt, ALU.mult))
                link(dve.scalar_tensor_tensor(out=cdst, in0=cfull, scalar=-1.0, in1=cneg, op0=ALU.add, op1=ALU.add))
                dve.tensor_copy(ydst[:, :], cdst).then_inc(S("tok_ready"), 1)
                after_chunk(dve, 1, "a_out" if l == 0 else "b_out", 0, 1, 1)
                if l == 0:
                    dve.wait_ge(S("ws_hi"), 2)
                    small(dve, 1, w_fg[:, :, :].rearrange("p k n -> p (k n)"), KD * HB)
                link(dve.tensor_tensor(stat[:, 64:68], stat[:, 64:68], stat[:, 68:72], ALU.mult))
                link(dve.reciprocal(wts[:, 0, :], stat[:, 64:68]))
                link(dve.tensor_tensor(wts[:, 1, :], wts[:, 0, :], stat[:, 56:60], ALU.mult))

                def further_tiles():
                    dve.wait_ge(S("further_consts"), l + 1)
                    dve.tensor_copy(further, further_i)
                    dve.wait_ge(S("places"), 2 * l + 2)
                    link(dve.tensor_copy(cnt, ps[0:1, 7, 0:NE]))
                    link(dve.tensor_tensor(reached.rearrange("p (e b) -> p e b", b=NB - 1),
                                           cnt.unsqueeze(2).broadcast_to([1, NE, NB - 1]),
                                           starts.rearrange("p (e b) -> p e b", b=NB - 1), ALU.is_gt))
                    link(dve.tensor_tensor_scan(so_far, ones_col[0:1, 0:1].broadcast_to([1, NOV]), reached, 0.0, ALU.mult,
                                                ALU.add))
                    j3 = jth.rearrange("p (j q) -> p j q", j=OVMAX)
                    t3 = taken.rearrange("p (j q) -> p j q", j=OVMAX)
                    link(dve.tensor_tensor(j3, so_far.unsqueeze(1).broadcast_to([1, OVMAX, NOV]),
                                           nth_further.unsqueeze(2).broadcast_to([1, OVMAX, NOV]), ALU.is_equal))
                    link(dve.tensor_tensor(j3, j3, reached.unsqueeze(1).broadcast_to([1, OVMAX, NOV]), ALU.mult))
                    link(dve.memset(ovf, 0.0))
                    link(dve.tensor_copy(ovf[:, 0:1], so_far[:, NOV - 1:NOV]))
                    for src, o in ((list_tiles, 16), (experts, 32)):
                        link(dve.tensor_tensor(t3, j3, src.unsqueeze(1).broadcast_to([1, OVMAX, NOV]), ALU.mult))
                        link(dve.tensor_reduce(ovf[:, o:o + OVMAX], t3, AX.X, ALU.add))
                    dve.tensor_copy(ov[:, :], ovf).then_inc(S("ov_ready"), 1)

                def low_x(n, par):
                    dve.wait_ge(S(f"xg_hi{l}"), n + 1)
                    dve.tensor_tensor(xgr[par][1].rearrange("p (a k) s -> p a (k s)", a=2), ps[:, 2:4, :],
                                      xgr[par][0].bitcast(F32).rearrange("p (a k) s -> p a (k s)", a=2),
                                      ALU.subtract).then_inc(S(f"xg_lo{l}"), 1)

                def hidden(n):
                    dve.wait_ge(S(f"up1_done{l}"), n + 1)
                    dve.wait_ge(S(f"sg_ready{l}"), n + 1)
                    if not isinstance(n, int) or n:
                        dve.wait_ge(S(f"hn_turned{l}"), n)
                    dve.tensor_tensor(hn, sg, ps[:, 1, :], ALU.mult).then_inc(S(f"hn_ready{l}"), 1)

                def low_h(n):
                    dve.wait_ge(S(f"h_hi{l}"), n + 1)
                    dve.tensor_tensor(hr[1], ps[:, 4, :], hr[0].bitcast(F32), ALU.subtract)\
                        .then_inc(S(f"h_lo{l}"), 1)

                p0 = pidx[("gate", l, 0, 0)]
                further_tiles()
                low_x(0, 0)
                split(dve, 1, p0 + 3)
                split(dve, 1, p0 + 4)
                split(dve, 1, p0 + 5)
                hidden(0)
                low_x(1, 1)
                split(dve, 1, p0 + 6)

                def turn(n, i, par, more=True):
                    base = pidx[("gate", l, par, 0)] if par else pidx[("gate", l, 2, 0)] - 12
                    low_h(n - 1)
                    for q in (3, 4, 5):
                        split_turn(dve, 1, l, n, i, base + q, q)
                    hidden(n)
                    split_turn(dve, 1, l, n, i, base + 6, 6)
                    if more:
                        low_x(n + 1, 1 - par)
                    split_turn(dve, 1, l, n, i, base + 7, 7)
                    if more:
                        split_turn(dve, 1, l, n, i, base + 8, 8)

                turn(1, 0, 1)
                with dve.Fori(1, NE // 2 - 1) as i2:
                    turn(2 * i2, i2, 0)
                    turn(2 * i2 + 1, i2, 1)
                turn(NE - 2, NE // 2 - 1, 0)
                turn(NE - 1, NE // 2 - 1, 1, False)
                low_h(NE - 1)
                n_ov = dve.value_load(ov[0:1, 0:1], min_val=0, max_val=OVMAX)
                with dve.If(n_ov > 0), dve.Fori(0, n_ov) as j:
                    dve.wait_ge(S(f"scattered{l}_0"), 16 * (j + NE // 2))
                    dve.wait_ge(S(f"pool_held{l}"), 3 * j + 1)
                    q = dve.value_load(ov[0:1, bass.ds(j + 16, 1)], min_val=0, max_val=NE * NB - 1)
                    dve.tensor_copy(fix[:, 0:1], tok[:, bass.ds(q, 1)])
                    dve.tensor_copy(fix[:, 1:2], ydst[:, bass.ds(q, 1)]).then_inc(S(f"fix_ready{l}"), 1)
                    low_x(j + NE, 0)
                    for o in range(4):
                        split_further(dve, 1, l, j, o)
                    hidden(j + NE)
                    low_h(j + NE)
                    split_further(dve, 1, l, j, 4)
                    split_further(dve, 1, l, j, 5)
                dve.wait_ge(S(f"scattered{l}_1"), NE // 2 * 16)
                dve.wait_ge(S(f"scattered{l}_0"), (n_ov + NE // 2) * 16)
                dve.tensor_copy(stat[:, 93:94], ones_col[:, :]).then_inc(S("tiles_stored"), 1)
                if l == 0:
                    for p in range(SPLIT):
                        split(dve, 1, pidx[("kv", 0, 0, 0)] + p)
                for t in range(NT):
                    dve.wait_ge(S(f"y_back{t}"), 16 * (l + 1))
                    for k in range(2):
                        m = dve.scalar_tensor_tensor(out=h[:, t, :], in0=yy[:, 2 * t + k, :], scalar=wts[:, k, t:t + 1],
                                                     in1=h[:, t, :], op0=ALU.mult, op1=ALU.add)
                        if k == 0:
                            link(m)
                    m.then_inc(S("h_final"), 1)
                    if t:
                        then(t - 1)
                then(NT - 1)

            moe(0, lambda t: norm_tile(1, t, stage_b))

            low_xT(1, 40)
            dve.wait_ge(S("fg_ready"), 1)
            link(dve.scalar_tensor_tensor(out=f_l, in0=f_z, scalar=0.0, in1=f_l, op0=ALU.min, op1=ALU.subtract))
            dve.tensor_tensor_scan(cT, ones_col[0:HB, 0:1].broadcast_to([HB, SEQ]), f_l, 0.0, ALU.mult,
                                   ALU.subtract).then_inc(S("fg_ready"), 1)
            nk = 0
            for g, (w, c, i) in enumerate(B_GROUPS):
                if w == "fg":
                    continue
                wc = ("kv", 0, c) if c < 4 else ("b_in", 0, c - 4)
                if i == 0:
                    after_chunk(dve, 1, *wc, 0)
                if w == "v":
                    dve.wait_ge(S("projB"), g + 1)
                    dve.tensor_copy(vb[:, i, (c - 2) * 512:(c - 1) * 512], ps[:, g % 6, :]).then_inc(S("D_evacB"), 1)
                    if i == 3:
                        after_chunk(dve, 1, *wc, 1)
                        if c == 3:
                            low_xT(2, 8)
                    continue
                dve.wait_ge(S("sq_ready"), nk + 1)
                dve.tensor_reduce(stat[:, 8:16], sq.rearrange("p (a b) -> p a b", a=8), AX.X, ALU.add)\
                    .then_inc(S("hss_ready"), 1)
                dve.wait_ge(S("hrms2_ready"), nk + 1)
                link(dve.reciprocal(stat[:, 24:32], stat[:, 16:24]))
                if nk >= 2:
                    dve.wait_ge(S("nat_turned"), nk - 1)
                dve.wait_ge(S("projB"), g + 1)
                dve.tensor_tensor(nat[:, nk % 2, :].rearrange("p (a b) -> p a b", a=8),
                                  ps[:, g % 6, :].rearrange("p (a b) -> p a b", a=8),
                                  stat[:, 24:32].unsqueeze(2).broadcast_to([P, 8, DH]), ALU.mult)\
                    .then_inc(S("D_evacB"), 1)
                if i == 3:
                    after_chunk(dve, 1, *wc, 1)
                nk += 1
            dve.wait_ge(S("nat_turned"), 16)
            for c in (2, 3):
                after_chunk(dve, 1, "b_in", 0, c, 0)
                if c == 2:
                    after_chunk(dve, 1, "b_in", 0, c, 1)

            steps = [(hd, j) for hd in range(HB) for j in FOX_TILES]

            def max_of(n):
                hd, j = steps[n]
                if n % NT == 0:
                    dve.wait_ge(S(f"negc_in{hd % 2}"), 16 * (hd // 2 + 1))
                    link(dve.tensor_tensor(negd.rearrange("p (a b) -> p a b", a=NT),
                                           negc[:, hd % 2, :].rearrange("p (a b) -> p a b", a=NT),
                                           mask_ts[:, :].unsqueeze(1).broadcast_to([P, NT, P]), ALU.add))
                dve.wait_ge(S("s_ready"), n + 1)
                if n >= 4:
                    dve.wait_ge(S("p_turned"), n - 3)
                a, b = 64 + n % 4, 68 + n % 4
                if j:
                    link(dve.tensor_tensor_reduce(pbuf[:, n % 4, 0:j * P], ps[:, score_bank(n), 0:j * P],
                                                  negc[:, hd % 2, 0:j * P], 1.0, -3e38, ALU.add, ALU.max,
                                                  stat[:, a:a + 1]))
                link(dve.tensor_tensor_reduce(pbuf[:, n % 4, j * P:(j + 1) * P], ps[:, score_bank(n), j * P:(j + 1) * P],
                                              negd[:, j * P:(j + 1) * P], 1.0,
                                              stat[:, a:a + 1] if j else -3e38, ALU.add, ALU.max, stat[:, b:b + 1]))
                dve.tensor_scalar(stat[:, 72 + n % 4:73 + n % 4], stat[:, b:b + 1], -1.0, None, ALU.mult)\
                    .then_inc(S("s_used"), 1)

            def normalise(n):
                hd, j = steps[n]
                dve.wait_ge(S("e_ready"), n + 1)
                link(dve.reciprocal(stat[:, 80 + n % 4:81 + n % 4], stat[:, 76 + n % 4:77 + n % 4]))
                pp = pbuf[:, n % 4, 0:(j + 1) * P]
                dve.tensor_scalar(pp, pp, stat[:, 80 + n % 4:81 + n % 4], None, ALU.mult).then_inc(S("p_ready"), 1)

            def low_o(r):
                dve.wait_ge(S("oT_hi"), r + 1)
                dve.tensor_tensor(xl[:, r, :], negd2, xh[:, r, :].bitcast(F32), ALU.subtract)\
                    .then_inc(S("oT_lo"), 1)

            for n in range(len(steps) + NORM_LAG):
                if n < len(steps):
                    max_of(n)
                if n >= NORM_LAG:
                    normalise(n - NORM_LAG)
                if n >= PAIR_LAG and (n - PAIR_LAG) % 8 == 0 or n == len(steps) + NORM_LAG - 1:
                    r = (n - PAIR_LAG) // 8 if n < len(steps) else 7
                    dve.wait_ge(S("o_ready"), 8 * (r + 1))
                    og = og_t[r // 4][:, r % 4, :]
                    if r:
                        dve.wait_ge(S("oT_hi"), r)
                    dve.tensor_tensor(negd2, ps[:, 4 + r % 2, :], og, ALU.mult).then_inc(S("oT_ready"), 1)
                if n > PAIR_LAG and (n - PAIR_LAG - 1) % 8 == 0 or n == len(steps) + NORM_LAG - 1:
                    low_o((n - PAIR_LAG - 1) // 8 if n < len(steps) else 7)
            after_chunk(dve, 1, "b_in", 0, 3, 1)
            residual(1, "b_out", "outB")

            def final_norm(t):
                dve.wait_ge(S("rms_tile"), NT * 2 + t + 1)
                link(dve.reciprocal(stat[:, 4 + t:5 + t], stat[:, t:t + 1]))
                dve.wait_ge(S("gain_bc"), 48)
                dve.scalar_tensor_tensor(out=fo[:, t, :], in0=h[:, t, :], scalar=stat[:, 4 + t:5 + t], in1=nf,
                                         op0=ALU.mult, op1=ALU.mult).then_inc(S("final_rows"), 1)

            moe(1, final_norm)

        @block.scalar
        def _(act):
            chain = [0]

            def link(ins):
                chain[0] += 1
                ins.then_inc(S("act_step"), 1)
                act.wait_ge(S("act_step"), chain[0])

            act.wait_ge(S("consts"), 1)
            preload = lambda: act.activation(stat[:, 94:95], eps_col[:, :], ACT.Sqrt)
            preload()

            def squares(i, each):
                for t in range(NT):
                    if i == 0:
                        act.wait_ge(S(f"x_loaded{t}"), 16)
                    else:
                        act.wait_ge(S("h_final"), NT * (i - 1) + t + 1)
                    m = act.activation(junk[:, t, :], h[:, t, :], ACT.Square, accum_out=stat[:, 88 + t:89 + t])
                    if each:
                        link(m)
                        act.activation(stat[:, t:t + 1], stat[:, 88 + t:89 + t], ACT.Sqrt, scale=1.0 / D,
                                       bias=eps_col[:, :]).then_inc(S("rms_tile"), 1)
                if not each:
                    link(m)
                    act.activation(stat[:, 0:4], stat[:, 88:92], ACT.Sqrt, scale=1.0 / D, bias=eps_col[:, :])\
                        .then_inc(S("rms"), 1)

            def high_xT(j, col):
                for k in range(KD):
                    act.wait_ge(S("xn_turned"), KD * j + k + 1)
                    act.activation(xh[:, k, :], ps[:, k, :], ACT.Copy, scale=gains[:, col + k:col + k + 1])\
                        .then_inc(S("xT_hi"), 1)

            squares(0, True)
            act.wait_ge(S("gates_w"), 32)
            small(act, 0, w_gates[:, :, :].rearrange("p k n -> p (k n)"), KD * 36)
            act.wait_ge(S("gains_ready"), 1)
            split(act, 0, 0)
            high_xT(0, 0)
            for p in range(1, SPLIT):
                split(act, 0, p)
            act.dma_start(w_fg[:, :, :], kv_w.rearrange("(k p) n -> p k n", p=P)[:, :, 2 * D:2 * D + HB]).then_inc(S("fg_w"), 16)
            for l in range(2):
                act.dma_start(w_rt[:, l, :, 0:NG], moe_w_grp[l].rearrange("(k p) n -> p k n", p=P))\
                    .then_inc(S("rt_w"), 16)
                act.dma_start(w_rt[:, l, :, NG:NG + NE], moe_w_exp[l].rearrange("(k p) n -> p k n", p=P))\
                    .then_inc(S("rt_w"), 16)
                act.dma_start(rbias[:, l, 0:NG], moe_b_grp[l:l + 1, :].broadcast_to([P, NG])).then_inc(S("rt_w"), 16)
                act.dma_start(rbias[:, l, NG:NG + NE], moe_b_exp[l:l + 1, :].broadcast_to([P, NE]))\
                    .then_inc(S("rt_w"), 16)
            act.wait_ge(S("projA"), 1)
            act.activation(g_t, ps[0:36, 0, :], ACT.Tanh, scale=1.0 / CAP, bias=gate15[0:36, :])\
                .then_inc(S("A_evacA"), 1)
            act.wait_ge(S("A_evacA"), 1)
            link(act.activation(g_e, g_t[32:36, :], ACT.Exp, scale=-CAP))
            act.activation(g_lf, g_e, ACT.Ln, bias=ones_col[0:4, :]).then_inc(S("gates_ready"), 1)
            for c in range(3):
                after_chunk(act, 0, "a_in", 0, c, 0)
                after_chunk(act, 0, "a_in", 0, c, 1)
            act.wait_ge(S("umn_ready"), 1)
            umn = arena[:, UMN:UMN + 144].rearrange("p (t c) -> p t c", t=NT)
            act.activation(stat[:, 32:48].rearrange("p (h t) -> p t h", h=HA), umn[:, :, 32:36], ACT.Exp, scale=-1.0)\
                .then_inc(S("em_ready"), 1)
            after_chunk(act, 0, "a_in", 0, 3, 0)
            for hd in range(HA):
                act.wait_ge(S("m_spread_used"), hd + 1)
                for i in range(NT):
                    dd = dec[:, hd, DO[i]:DO[i] + DW[i]]
                    act.activation(dd, dd, ACT.Exp, scale=-1.0, bias=umn[:, i, hd:hd + 1])\
                        .then_inc(S("dec_ready"), 1)
            after_chunk(act, 0, "a_in", 0, 3, 1)
            for g in range(17, 25):
                w, c, i = A_GROUPS[g]
                if i == 0:
                    after_chunk(act, 0, "a_in", 0, c, 0)
                act.wait_ge(S("projA"), g + 1)
                act.activation(so[:, i, (c - 4) * 512:(c - 3) * 512], ps[:, g % 6, :], ACT.Sigmoid)\
                    .then_inc(S("A_evacA"), 1)
                if i == 3:
                    after_chunk(act, 0, "a_in", 0, c, 1)
            def head_rms(hd):
                act.wait_ge(S("hsum_ready"), hd + 1)
                act.activation(stat[:, 24:28] if hd % 2 else stat[:, 68:72],
                               stat[:, 84:88] if hd % 2 else stat[:, 72:76], ACT.Sqrt, scale=1.0 / DV,
                               bias=eps_col[:, :]).then_inc(S("hrms_ready"), 1)

            for hd in range(HA):
                for j in range(NT):
                    act.wait_ge(S("num_ready"), NT * hd + j + 1)
                    if hd >= 2 and j == 0:
                        act.wait_ge(S("hrms_ready"), hd - 1)
                    c = (84 if hd % 2 else 72) + j
                    act.activation(sqa[:, j, :], ps[:, 4 + j, 0:DV], ACT.Square, accum_out=stat[:, c:c + 1])\
                        .then_inc(S("num_squared"), 1)
                    if hd and j == 1:
                        head_rms(hd - 1)
            head_rms(HA - 1)
            for k in range(KD):
                act.wait_ge(S("hg_turned"), k + 1)
                act.activation(xh[:, k, :], ps[:, k, :], ACT.Copy, scale=gains[:, 32 + k:33 + k])\
                    .then_inc(S("hgT_hi"), 1)
            for c in range(2):
                after_chunk(act, 0, "a_out", 0, c, 0)
                after_chunk(act, 0, "a_out", 0, c, 1)

            def moe(l):
                i = 2 * l + 1
                squares(i, False)
                act.wait_ge(S("rstd_ready"), l + 1)
                for t in range(NT):
                    act.activation(stage[:, t, :], h[:, t, :], ACT.Copy, scale=stat[:, 4 + t:5 + t])\
                        .then_inc(S("ffn_scaled"), 1)
                for t in range(NT):
                    act.wait_ge(S("ffn_rows"), NT * l + t + 1)
                    act.dma_start(xd[l][t * P:(t + 1) * P, :], stage[:, t, :]).then_inc(S("rows_stored"), 16)
                act.wait_ge(S("gd_ready"), 2 * l + 1)
                act.activation(ge, gd, ACT.Exp).then_inc(S("ge_ready"), 1)
                act.wait_ge(S("gd_ready"), 2 * l + 2)
                act.activation(stat[:, 56:60], stat[:, 52:56], ACT.Exp).then_inc(S("ge_ready"), 1)

                if l == 0:
                    act.wait_ge(S("fg_w"), 16)
                    small(act, 0, w_fg[:, :, :].rearrange("p k n -> p (k n)"), KD * HB)

                def high_x(n, par):
                    act.wait_ge(S(f"xg_turned{l}"), n + 1)
                    act.activation(xgr[par][0].rearrange("p (a k) s -> p a (k s)", a=2), ps[:, 2:4, :], ACT.Copy)\
                        .then_inc(S(f"xg_hi{l}"), 1)

                def gate(n):
                    act.wait_ge(S(f"gate1_done{l}"), n + 1)
                    if not isinstance(n, int) or n:
                        act.wait_ge(S(f"hn_ready{l}"), n)
                    act.activation(sg, ps[:, 0, :], ACT.Silu).then_inc(S(f"sg_ready{l}"), 1)

                def high_h(n):
                    act.wait_ge(S(f"hn_turned{l}"), n + 1)
                    act.activation(hr[0], ps[:, 4, :], ACT.Copy).then_inc(S(f"h_hi{l}"), 1)

                def take_y(n, a, par, scattered=None):
                    act.wait_ge(S(f"down{a}_done{l}"), n + 1)
                    if scattered is not None:
                        act.wait_ge(S(f"scattered{l}_{par}"), scattered)
                    act.activation(yb[:, par, a * 512:(a + 1) * 512], ps[:, 5 + a, :], ACT.Copy)\
                        .then_inc(S(f"y{a}_ready{l}"), 1)

                p0 = pidx[("gate", l, 0, 0)]
                high_x(0, 0)
                split(act, 0, p0 + 3)
                gate(0)
                split(act, 0, p0 + 4)
                split(act, 0, p0 + 5)
                high_x(1, 1)
                split(act, 0, p0 + 6)

                def turn(n, i, par, scattered, more=True):
                    base = pidx[("gate", l, par, 0)] if par else pidx[("gate", l, 2, 0)] - 12
                    high_h(n - 1)
                    split_turn(act, 0, l, n, i, base + 3, 3)
                    split_turn(act, 0, l, n, i, base + 4, 4)
                    gate(n)
                    split_turn(act, 0, l, n, i, base + 5, 5)
                    split_turn(act, 0, l, n, i, base + 6, 6)
                    if more:
                        high_x(n + 1, 1 - par)
                    split_turn(act, 0, l, n, i, base + 7, 7)
                    take_y(n - 1, 0, 1 - par, scattered)
                    if more:
                        split_turn(act, 0, l, n, i, base + 8, 8)
                    take_y(n - 1, 1, 1 - par, scattered)

                turn(1, 0, 1, None)
                turn(2, 1, 0, None)
                turn(3, 1, 1, 16)
                with act.Fori(2, NE // 2 - 1) as i2:
                    turn(2 * i2, i2, 0, 16 * i2 - 16)
                    turn(2 * i2 + 1, i2, 1, 16 * i2)
                turn(NE - 2, NE // 2 - 1, 0, 16 * (NE // 2 - 2))
                turn(NE - 1, NE // 2 - 1, 1, 16 * (NE // 2 - 1), False)
                high_h(NE - 1)
                take_y(NE - 1, 0, 1, 16 * (NE // 2 - 1))
                take_y(NE - 1, 1, 1, 16 * (NE // 2 - 1))
                act.wait_ge(S("ov_ready"), l + 1)
                n_ov = act.value_load(ov[0:1, 0:1], min_val=0, max_val=OVMAX)
                with act.If(n_ov > 0), act.Fori(0, n_ov) as j:
                    high_x(j + NE, 0)
                    for o in range(4):
                        split_further(act, 0, l, j, o)
                    gate(j + NE)
                    high_h(j + NE)
                    split_further(act, 0, l, j, 4)
                    split_further(act, 0, l, j, 5)
                    take_y(j + NE, 0, 0)
                    take_y(j + NE, 1, 0)
                preload()
                if l == 0:
                    for p in range(SPLIT):
                        split(act, 0, pidx[("kv", 0, 0, 0)] + p)

            moe(0)

            squares(2, True)
            high_xT(1, 40)
            act.wait_ge(S("projB"), 1)
            act.activation(f_z, ps[0:HB, 0, :], ACT.Identity, bias=gains[0:HB, 51:52]).then_inc(S("A_evacB"), 1)
            act.wait_ge(S("A_evacB"), 1)
            link(act.activation(f_a, f_z, ACT.Abs))
            link(act.activation(f_e, f_a, ACT.Exp, scale=-1.0))
            act.activation(f_l, f_e, ACT.Ln, bias=ones_col[0:HB, :]).then_inc(S("fg_ready"), 1)

            def take_heads(n):
                act.wait_ge(S("nat_turned"), n + 1)
                q = n >= 8
                c, i = (n % 8) // 4, n % 4
                dd = (qTb if q else kTb)[:, 4 * c:4 * c + 4, i * P:(i + 1) * P]
                act.activation(dd, ps[:, 6 + n % 2, :].rearrange("p (r t) -> p r t", r=4), ACT.Copy,
                               scale=qg_col if q else gains[:, 48:49]).then_inc(S("headsT_ready"), 1)

            qg_col = stat[:, 92:93]
            link(act.activation(qg_col, gains[:, 49:50], ACT.Copy, scale=DH ** -0.5))
            nk = 0
            for g, (w, c, i) in enumerate(B_GROUPS):
                if w == "fg":
                    continue
                wc = ("kv", 0, c) if c < 4 else ("b_in", 0, c - 4)
                if i == 0:
                    after_chunk(act, 0, *wc, 0)
                if w == "v":
                    if i == 3:
                        after_chunk(act, 0, *wc, 1)
                        if c == 2:
                            take_heads(6)
                            take_heads(7)
                        if c == 3:
                            high_xT(2, 8)
                    continue
                act.wait_ge(S("projB"), g + 1)
                if nk:
                    act.wait_ge(S("hss_ready"), nk)
                act.activation(sq, ps[:, g % 6, :], ACT.Square).then_inc(S("sq_ready"), 1)
                act.wait_ge(S("hss_ready"), nk + 1)
                act.activation(stat[:, 16:24], stat[:, 8:16], ACT.Sqrt, scale=1.0 / DH, bias=eps_col[:, :])\
                    .then_inc(S("hrms2_ready"), 1)
                nk += 1
                if nk > 2 and nk not in (9, 10):
                    take_heads(nk - 3)
                if i == 3:
                    after_chunk(act, 0, *wc, 1)
            take_heads(14)
            take_heads(15)
            for c in range(2):
                after_chunk(act, 0, "b_in", 0, 2 + c, 0)
                for q in range(4):
                    act.wait_ge(S("ogB"), 4 * c + q + 1)
                    act.activation(og_t[c][:, q, :], ps[:, q, :], ACT.Sigmoid).then_inc(S("og_ready"), 1)
                if c == 0:
                    after_chunk(act, 0, "b_in", 0, 2, 1)

            steps = [(hd, j) for hd in range(HB) for j in FOX_TILES]

            act.wait_ge(S("fg_ready"), 1)
            act.wait_ge(S("D_evacB"), EVAC["B"].count("D"))
            for n in range(len(steps) + TURN_LAG):
                if n < len(steps):
                    hd, j = steps[n]
                    act.wait_ge(S("s_used"), n + 1)
                    pp = pbuf[:, n % 4, 0:(j + 1) * P]
                    act.activation(pp, pp, ACT.Exp, bias=stat[:, 72 + n % 4:73 + n % 4],
                                   accum_out=stat[:, 76 + n % 4:77 + n % 4]).then_inc(S("e_ready"), 1)
                m = n - TURN_LAG
                if m >= 0:
                    hd, j = steps[m]
                    act.wait_ge(S("p_turned"), m + 1)
                    if m >= 4:
                        act.wait_ge(S("o_ready"), m - 3)
                    act.activation(ptb[:, m % 4, 0:(j + 1) * P], ps[:, pT_bank(m), 0:(j + 1) * P], ACT.Copy)\
                        .then_inc(S("pT_ready"), 1)
                if n >= PAIR_LAG and (n - PAIR_LAG) % 8 == 0 or n == len(steps) + TURN_LAG - 1:
                    r = (n - PAIR_LAG) // 8 if n < len(steps) else 7
                    act.wait_ge(S("oT_ready"), r + 1)
                    act.activation(xh[:, r, :], negd2, ACT.Copy).then_inc(S("oT_hi"), 1)
            preload()
            after_chunk(act, 0, "b_in", 0, 3, 1)
            for c in range(2):
                after_chunk(act, 0, "b_out", 0, c, 0)
                after_chunk(act, 0, "b_out", 0, c, 1)
            moe(1)
            squares(4, True)


ROWS_DMAS = 11
ARENA = 17568
WSN = 384
UMN = 17424
NORM_LAG, TURN_LAG, ATTEND_LAG, PAIR_LAG = 1, 3, 5, 13
FOX_TILES = (0, 2, 1, 3)
EVAC = {"A": ["A"] + ["D"] * 16 + ["A"] * 8, "B": ["A"] + ["D"] * 24}


_INS = ['x', 'norm_mix', 'norm_ffn', 'a_w_in', 'a_b_gate', 'a_head_gain', 'a_w_out', 'kv_norm', 'kv_w', 'kv_b_f',
        'kv_k_gain', 'b_w_in', 'b_q_gain', 'b_w_out', 'moe_w_grp', 'moe_b_grp', 'moe_w_exp', 'moe_b_exp',
        'moe_w_gate', 'moe_w_up', 'moe_w_down', 'norm_final']
_OUTS = [((1, SEQ, D), 'float32')]


def kernel(**inputs):
    import numpy as _np
    import concourse.bacc as _bacc
    from concourse import mybir as _mybir
    from concourse.bass_utils import run_bass_kernel_spmd as _run

    nc = _bacc.Bacc("TRN2", target_bir_lowering=False, num_devices=1)
    arrays, args = {}, []
    for name in _INS:
        a = _np.ascontiguousarray(inputs[name])
        arrays[f"in_{name}_dram"] = a
        args.append(nc.dram_tensor(f"in_{name}_dram", a.shape, _mybir.dt.from_np(a.dtype), kind="ExternalInput").ap())
    for i, (shape, dtype) in enumerate(_OUTS):
        dt = _mybir.dt.from_np(_np.dtype(dtype))
        args.append(nc.dram_tensor(f"out_{i}_dram", shape, dt, kind="ExternalOutput").ap())
    trunk(nc, *args)
    r = _run(nc, [arrays], core_ids=[0])
    return r.results[0]["out_0_dram"]
```
